# Optimizing a Trainium2 kernel written in Bass

```python
import jax, jax.numpy as jnp
from jax import lax
import numpy as np

D_MODEL = 1024
BATCH = 1
SEQ = 512
DEPTH = 2

CHUNK = 64
Q_BLOCK = 128

D_MIX = D_MODEL
MLA_HEADS = 8
QK_NOPE = 64
QK_ROPE = 32
V_DIM = 64
Q_LORA = 256
KV_LORA = 128
ROPE_THETA = 10000.0
SGU_GROUPS = 4
SGU_GROUP_DIM = 64
SGU_WIDTH = SGU_GROUPS * SGU_GROUP_DIM
SGU_BLOCK = 128
LRU_HEADS = 4
LRU_HEAD_DIM = 64
LRU_WIDTH = LRU_HEADS * LRU_HEAD_DIM
CONV_W = 4
LRU_C = 8.0
D_IN = Q_LORA + KV_LORA + QK_ROPE + 2 * SGU_WIDTH + 2 * LRU_WIDTH
IN_SPLITS = (Q_LORA,
             Q_LORA + KV_LORA,
             Q_LORA + KV_LORA + QK_ROPE,
             Q_LORA + KV_LORA + QK_ROPE + SGU_WIDTH,
             Q_LORA + KV_LORA + QK_ROPE + 2 * SGU_WIDTH,
             Q_LORA + KV_LORA + QK_ROPE + 2 * SGU_WIDTH + LRU_WIDTH)
D_FF = 2816
N_EXPERTS = 8
TOP_K = 2
D_FF_EXPERT = 1408
N_DENSE = (DEPTH + 1) // 2
N_MOE = DEPTH // 2
NEG_INF = -1e30

kernel_name = "hybrid_mla_sgu_rglru_moe_trunk"

def rms_norm(x, g, eps=1e-6):
    xf = x.astype(jnp.float32)
    y = xf * lax.rsqrt(jnp.mean(xf * xf, axis=-1, keepdims=True) + eps)
    return (y * g.astype(jnp.float32)).astype(x.dtype)

def layer_norm(x, g, b, eps=1e-5):
    xf = x.astype(jnp.float32)
    mu = jnp.mean(xf, axis=-1, keepdims=True)
    var = jnp.mean(jnp.square(xf - mu), axis=-1, keepdims=True)
    y = (xf - mu) * lax.rsqrt(var + eps) * g.astype(jnp.float32) + b.astype(jnp.float32)
    return y.astype(x.dtype)

def rope_tables(seq):
    pos = jnp.arange(seq, dtype=jnp.float32)
    inv = ROPE_THETA ** (-jnp.arange(0, QK_ROPE, 2, dtype=jnp.float32) / QK_ROPE)
    ang = pos[:, None] * inv[None, :]
    return jnp.cos(ang), jnp.sin(ang)

def apply_rope(x, cos, sin):
    half = x.shape[-1] // 2
    x1 = x[..., :half].astype(jnp.float32)
    x2 = x[..., half:].astype(jnp.float32)
    return jnp.concatenate([x1 * cos - x2 * sin, x2 * cos + x1 * sin], axis=-1).astype(x.dtype)

def chunk_causal_attention(q, k, v):
    B, S, H, Dq = q.shape
    n_qb = S // Q_BLOCK
    scale = Dq ** -0.5
    qb = q.reshape(B, n_qb, Q_BLOCK, H, Dq).transpose(1, 0, 3, 2, 4)
    kt = k.transpose(0, 2, 1, 3)
    vt = v.transpose(0, 2, 1, 3)
    key_chunk = jnp.arange(S) // CHUNK

    def one_block(args):
        q_blk, blk = args
        s = jnp.einsum('bhqd,bhkd->bhqk', q_blk, kt, preferred_element_type=jnp.float32) * scale
        q_chunk = (blk * Q_BLOCK + jnp.arange(Q_BLOCK)) // CHUNK
        mask = key_chunk[None, :] <= q_chunk[:, None]
        p = jax.nn.softmax(jnp.where(mask, s, NEG_INF), axis=-1).astype(vt.dtype)
        return jnp.einsum('bhqk,bhkd->bhqd', p, vt)

    o = lax.map(one_block, (qb, jnp.arange(n_qb)))
    return o.transpose(1, 0, 3, 2, 4).reshape(B, S, H, vt.shape[-1])

def mla_mixer(z_q, z_kv, z_kr, q_norm_g, w_uq, kv_norm_g, w_ukv, cos, sin):
    B, S, _ = z_q.shape
    q = (rms_norm(z_q, q_norm_g) @ w_uq).reshape(B, S, MLA_HEADS, QK_NOPE + QK_ROPE)
    q_rope = apply_rope(q[..., QK_NOPE:], cos[:, None, :], sin[:, None, :])
    q = jnp.concatenate([q[..., :QK_NOPE], q_rope], axis=-1)
    kv = (rms_norm(z_kv, kv_norm_g) @ w_ukv).reshape(B, S, MLA_HEADS, QK_NOPE + V_DIM)
    k_rope = apply_rope(z_kr, cos, sin)
    k = jnp.concatenate([kv[..., :QK_NOPE],
                         jnp.broadcast_to(k_rope[:, :, None, :], (B, S, MLA_HEADS, QK_ROPE))], axis=-1)
    v = kv[..., QK_NOPE:]
    o = chunk_causal_attention(q, k, v)
    return o.reshape(B, S, MLA_HEADS * V_DIM)

def sgu_mixer(z_u, z_v, ln_g, ln_b, w_s, b_s):
    B, S, _ = z_u.shape
    u = jax.nn.gelu(z_u)
    v = layer_norm(jax.nn.gelu(z_v), ln_g, ln_b)
    vb = v.reshape(B, S // SGU_BLOCK, SGU_BLOCK, SGU_GROUPS, SGU_GROUP_DIM)
    w = w_s * jnp.tril(jnp.ones((SGU_BLOCK, SGU_BLOCK), dtype=w_s.dtype))[None]
    mixed = jnp.einsum('gts,bnsgc->bntgc', w, vb) + b_s.T[None, None, :, :, None]
    return u * mixed.reshape(B, S, SGU_WIDTH)

def rglru_mixer(z_x, z_y, conv_w, conv_b, wa, ba, wx, bx, lam):
    B, S, W = z_x.shape
    xp = jnp.pad(z_x, ((0, 0), (CONV_W - 1, 0), (0, 0)))
    xc = conv_b + xp[:, 0:S, :] * conv_w[0]
    for tap in range(1, CONV_W):
        xc = xc + xp[:, tap:tap + S, :] * conv_w[tap]
    xh = xc.reshape(B, S, LRU_HEADS, LRU_HEAD_DIM)
    r = jax.nn.sigmoid(jnp.einsum('bshi,hij->bshj', xh, wa).reshape(B, S, W) + ba)
    i = jax.nn.sigmoid(jnp.einsum('bshi,hij->bshj', xh, wx).reshape(B, S, W) + bx)
    log_a = -LRU_C * r.astype(jnp.float32) * jax.nn.softplus(-lam.astype(jnp.float32))
    a = jnp.exp(log_a)
    b = jnp.sqrt(-jnp.expm1(2.0 * log_a)) * (i * xc).astype(jnp.float32)

    def combine(left, right):
        a_l, b_l = left
        a_r, b_r = right
        return a_l * a_r, a_r * b_l + b_r

    _, h = lax.associative_scan(combine, (a, b), axis=1)
    return h.astype(z_x.dtype) * jax.nn.gelu(z_y)

def swiglu(h, wg, wu, wd):
    return (jax.nn.silu(h @ wg) * (h @ wu)) @ wd

def moe_swiglu(h, router, wg, wu, wd):
    B, S, D = h.shape
    t = h.reshape(B * S, D)
    logits = (t @ router).astype(jnp.float32)
    top_v, top_i = lax.top_k(logits, TOP_K)
    gates = jax.nn.softmax(top_v, axis=-1)
    comb = jnp.sum(jax.nn.one_hot(top_i, N_EXPERTS, dtype=jnp.float32) * gates[..., None], axis=1)
    comb = comb.astype(t.dtype)
    out = jnp.zeros_like(t)
    for e in range(N_EXPERTS):
        out = out + comb[:, e:e + 1] * swiglu(t, wg[e], wu[e], wd[e])
    return out.reshape(B, S, D)

def setup_inputs(seed: int = 0) -> dict:
    key = jax.random.key(seed)
    ks = iter(jax.random.split(key, 48))
    f32 = jnp.float32

    def nrm(shape, fan_in, mult=1.0):
        return jax.random.normal(next(ks), shape, f32) * (mult * fan_in ** -0.5)

    def gain(shape):
        return 1.0 + 0.02 * jax.random.normal(next(ks), shape, f32)

    def small(shape, s=0.02):
        return s * jax.random.normal(next(ks), shape, f32)

    L = DEPTH
    u = jax.random.uniform(next(ks), (L, LRU_WIDTH), f32, minval=0.9, maxval=0.999)
    p = u ** (1.0 / LRU_C)
    lam = jnp.log(p) - jnp.log1p(-p)
    return {
        "x": jax.random.normal(next(ks), (BATCH, SEQ, D_MODEL), f32),
        "c": jax.random.normal(next(ks), (BATCH, D_MODEL), f32),
        "w_mod": nrm((L, D_MODEL, 6 * D_MODEL), D_MODEL, 0.5),
        "b_mod": small((L, 6 * D_MODEL)),
        "pre_mix_g": gain((L, D_MODEL)),
        "post_mix_g": gain((L, D_MODEL)),
        "w_in": nrm((L, D_MODEL, D_IN), D_MODEL),
        "q_norm_g": gain((L, Q_LORA)),
        "w_uq": nrm((L, Q_LORA, MLA_HEADS * (QK_NOPE + QK_ROPE)), Q_LORA),
        "kv_norm_g": gain((L, KV_LORA)),
        "w_ukv": nrm((L, KV_LORA, MLA_HEADS * (QK_NOPE + V_DIM)), KV_LORA),
        "sgu_ln_g": gain((L, SGU_WIDTH)),
        "sgu_ln_b": small((L, SGU_WIDTH)),
        "sgu_w": nrm((L, SGU_GROUPS, SGU_BLOCK, SGU_BLOCK), SGU_BLOCK),
        "sgu_b": gain((L, SGU_GROUPS, SGU_BLOCK)),
        "conv_w": nrm((L, CONV_W, LRU_WIDTH), CONV_W),
        "conv_b": small((L, LRU_WIDTH)),
        "lru_wa": nrm((L, LRU_HEADS, LRU_HEAD_DIM, LRU_HEAD_DIM), LRU_HEAD_DIM),
        "lru_ba": small((L, LRU_WIDTH)),
        "lru_wx": nrm((L, LRU_HEADS, LRU_HEAD_DIM, LRU_HEAD_DIM), LRU_HEAD_DIM),
        "lru_bx": small((L, LRU_WIDTH)),
        "lru_lambda": lam,
        "w_o": nrm((L, D_MIX, D_MODEL), D_MIX),
        "pre_ffn_g": gain((L, D_MODEL)),
        "post_ffn_g": gain((L, D_MODEL)),
        "ffn_w_gate": nrm((N_DENSE, D_MODEL, D_FF), D_MODEL),
        "ffn_w_up": nrm((N_DENSE, D_MODEL, D_FF), D_MODEL),
        "ffn_w_down": nrm((N_DENSE, D_FF, D_MODEL), D_FF),
        "moe_router": nrm((N_MOE, D_MODEL, N_EXPERTS), D_MODEL),
        "moe_w_gate": nrm((N_MOE, N_EXPERTS, D_MODEL, D_FF_EXPERT), D_MODEL),
        "moe_w_up": nrm((N_MOE, N_EXPERTS, D_MODEL, D_FF_EXPERT), D_MODEL),
        "moe_w_down": nrm((N_MOE, N_EXPERTS, D_FF_EXPERT, D_MODEL), D_FF_EXPERT),
    }

def reference(x, c, w_mod, b_mod, pre_mix_g, post_mix_g, w_in, q_norm_g, w_uq, kv_norm_g, w_ukv,
              sgu_ln_g, sgu_ln_b, sgu_w, sgu_b, conv_w, conv_b, lru_wa, lru_ba, lru_wx, lru_bx,
              lru_lambda, w_o, pre_ffn_g, post_ffn_g, ffn_w_gate, ffn_w_up, ffn_w_down,
              moe_router, moe_w_gate, moe_w_up, moe_w_down):
    S = x.shape[1]
    cos, sin = rope_tables(S)
    cond = jax.nn.silu(c)
    for l in range(DEPTH):
        mod = cond @ w_mod[l] + b_mod[l]
        sh_m, sc_m, g_m, sh_f, sc_f, g_f = [m[:, None, :] for m in jnp.split(mod, 6, axis=-1)]

        h = rms_norm(x, pre_mix_g[l]) * (1.0 + sc_m) + sh_m
        z = h @ w_in[l]
        z_q, z_kv, z_kr, z_u, z_v, z_x, z_y = jnp.split(z, IN_SPLITS, axis=-1)
        y_mla = mla_mixer(z_q, z_kv, z_kr, q_norm_g[l], w_uq[l], kv_norm_g[l], w_ukv[l], cos, sin)
        y_sgu = sgu_mixer(z_u, z_v, sgu_ln_g[l], sgu_ln_b[l], sgu_w[l], sgu_b[l])
        y_lru = rglru_mixer(z_x, z_y, conv_w[l], conv_b[l], lru_wa[l], lru_ba[l],
                            lru_wx[l], lru_bx[l], lru_lambda[l])
        y = jnp.concatenate([y_mla, y_sgu, y_lru], axis=-1) @ w_o[l]
        x = x + g_m * rms_norm(y, post_mix_g[l])

        h = rms_norm(x, pre_ffn_g[l]) * (1.0 + sc_f) + sh_f
        if l % 2 == 0:
            f = swiglu(h, ffn_w_gate[l // 2], ffn_w_up[l // 2], ffn_w_down[l // 2])
        else:
            f = moe_swiglu(h, moe_router[l // 2], moe_w_gate[l // 2], moe_w_up[l // 2], moe_w_down[l // 2])
        x = x + g_f * rms_norm(f, post_ffn_g[l])
    return x


_drawn_inputs = setup_inputs


def setup_inputs(seed=0):
    import zlib

    import numpy as np

    out = dict(_drawn_inputs(seed))
    spreads = {}
    factors = {'pre_mix_g': 2.7,
     'q_norm_g': 6.973,
     'kv_norm_g': 4.006,
     'sgu_ln_g': 4.446,
     'sgu_ln_b': 15.633,
     'sgu_b': 4.478,
     'lru_ba': 45.424,
     'lru_bx': 32.912,
     'post_ffn_g': 3.253}
    for name, (base, spread) in spreads.items():
        noise = np.random.default_rng([zlib.crc32(name.encode()), seed]).standard_normal(out[name].shape)
        drawn = base * np.exp(spread * noise) if base else spread * noise
        out[name] = __import__('jax').numpy.asarray(drawn.astype(out[name].dtype))
    for name, factor in factors.items():
        out[name] = (out[name] * factor).astype(out[name].dtype)
    return out
```

```python
from contextlib import ExitStack

import numpy as np

import concourse.bass as bass
from concourse import mybir

F32 = mybir.dt.float32
F32R = mybir.dt.float32r
I32 = mybir.dt.int32
U32 = mybir.dt.uint32
ALU = mybir.AluOpType
ACT = mybir.ActivationFunctionType
AX = mybir.AxisListType

P = 128
L = 2
S = 512
T = S // P
D = 1024
KD = D // P
HEADS, NOPE, ROPE, VD = 8, 64, 32, 64
QL, KVL = 256, 128
HALF = ROPE // 2
QKR = QL + KVL + ROPE
SGU, LRU = 256, 256
NEG = -1e30
SCALE = (NOPE + ROPE) ** -0.5
FF, FFE, E = 2816, 1408, 8
NB = FFE // P
UNIT = 2048
RAWS, SPLS, MRAWS = 4, 3, 6
MAXT = 16
MODC = 6 * D // 512
GROUPS = [list(range(0, 6)), list(range(6, 12)), list(range(12, 18)), list(range(18, 22))]
EW = [(0, 512), (512, 512), (1024, 384)]
EU = 4 * len(EW) + (NB + 1) // 2


def plan():
    units = []

    def mod(m):
        for kh in range(2):
            units.append(("mod", m // MODC, m % MODC, kh))

    m = 0
    for m in range(4):
        mod(m)
    m = 4
    for l in range(L):
        for part in range(3):
            for kh in range(2):
                units.append(("win", l, part, kh))
        if l == 0:
            for _ in range(6):
                mod(m)
                m += 1
        for n in range(2):
            for kh in (1, 0):
                units.append(("wo", l, n, kh))
        if l == 0:
            for g, blocks in enumerate(GROUPS):
                for c in range(blocks[0] // 2, blocks[-1] // 2 + 1):
                    units.append(("gate", l, c, 0))
                    units.append(("up", l, c, 0))
                    mod(m)
                    m += 1
                step = 3 if len(blocks) == 6 else 4
                for n in range(2):
                    for f in range(blocks[0], blocks[-1] + 1, step):
                        units.append(("down", n, f, step))
                if g < 3:
                    mod(m)
                    m += 1
    assert m == L * MODC
    return units


UNITS = plan()
WEIGHTS = [r for r, u in enumerate(UNITS) if u[0] != "mod"]
MODS = [r for r, u in enumerate(UNITS) if u[0] == "mod"]
SB = len(WEIGHTS)
W_IN = [WEIGHTS.index(UNITS.index(("win", l, 0, 0))) for l in range(L)]
W_O = [WEIGHTS.index(UNITS.index(("wo", l, 0, 1))) for l in range(L)]
W_FF = WEIGHTS.index(UNITS.index(("gate", 0, 0, 0)))


def build(nc, a, out):
    with ExitStack() as ctx:
        base = 16512
        place = [base]

        def at(name, offset, shape, dt=F32):
            return nc.alloc_sbuf_tensor_at(name, shape, dt, offset=offset)

        def region(size):
            o = place[0]
            place[0] += size
            return o

        X_, RAW_, HT_, SPL_ = region(16384), region(32768), region(32768), region(49152)
        W_ = region(57856)
        x = at("x", X_, [P, T, D])
        raw = at("raw", RAW_, [P, RAWS, UNIT])
        spl = at("spl", SPL_, [P, SPLS, 2, UNIT], F32R)
        hT = at("hT", HT_, [P, 2, KD, S], F32R)
        yT = at("yT", HT_, [P, 2, KD, S], F32R)
        zq = at("zq", W_, [P, T, QKR])
        qT = at("qT", W_, [P, 3, S])
        wuq = at("wuq", W_ + 6656, [P, 2, HEADS, P])
        wukv = at("wukv", W_ + 6656 + 8192, [P, HEADS, NOPE + VD])
        xn = at("xn", W_ + 18944, [P, T, D])
        zuv = at("zuv", W_ + 18944, [P, T, 2 * SGU])
        zxy = at("zxy", W_ + 27136, [P, 4, S])
        pr = at("pr", W_ + 18944, [P, T, S])
        pT = at("pT", W_ + 27136, [P, T, S])
        T1 = W_ + 35328
        lt = at("lt", T1, [P, 4, 2, S])
        vb = at("vb", T1, [P, T, S])
        qb = at("qb", T1 + 8192, [P, 2, S])
        kb = at("kb", T1 + 12288, [P, 2, S])
        full = at("full", T1 + 8192, [P, 2, S])
        lnrow = at("lnrow", T1 + 16384, [P, 2, SGU])
        sguw = at("sguw", T1 + 18432, [P, 4, P])
        bd = at("bd", T1 + 20480, [P, 2, 2, P])
        tmpm = at("tmpm", T1, [P, 2, D])
        act = at("act", W_, [P, 2, 6, S], F32R)
        yf = at("yf", W_ + 24576, [P, T, D])
        sgf = at("sgf", W_ + 40960, [P, 2, S])
        actf = at("actf", W_ + 45056, [P, 2, S])
        tmpf = at("tmpf", W_ + 49152, [P, 2, D])
        mraw = at("mraw", RAW_, [P, MRAWS, UNIT])
        hTf = at("hTf", HT_, [P, KD, S])
        xgT = at("xgT", HT_ + 16384, [P, 2, KD, P], F32R)
        yg = at("yg", HT_, [P, T, 2, D])
        xg = at("xg", W_, [P, D])
        acte = at("acte", W_ + 4096, [P, FFE])
        sge = at("sge", W_ + 9728, [P, 512])
        ye = at("ye", W_ + 11776, [P, D])
        aT = at("aT", W_ + 35328, [P, 2, NB, P], F32R)
        xfull = at("xfull", W_ + 46592, [P, KD, P])
        ym = at("ym", W_ + 18944, [P, T, D])
        small = [W_ + 15872]

        def little(name, shape, dt=F32):
            n = int(np.prod(shape[1:])) * 4
            o = small[0]
            small[0] += (n + 31) // 32 * 32
            return at(name, o, shape, dt)

        lg = little("lg", [P, T, E])
        mx8 = little("mx8", [P, T, 8])
        ix8 = little("ix8", [P, T, 8], U32)
        ixf = little("ixf", [P, T, 8])
        oh = little("oh", [P, 2, T, E])
        msk = little("msk", [P, T, E])
        gpos = little("gpos", [P, T, E])
        prod = little("prod", [P, 2, T, E])
        slf = little("slf", [P, 2, T])
        sli = little("sli", [P, 2, T], I32)
        gt = little("gt", [P, 2, T])
        ge = little("ge", [P, 2, T])
        tl = little("tl", [P, 3, E])
        cmp_ = little("cmp", [P, MAXT, E])
        etf = little("etf", [P, 1 + MAXT])
        eti = little("eti", [P, 1 + MAXT], I32)
        assert small[0] <= W_ + 18944

        def keep(name, shape, dt=F32):
            return at(name, region((int(np.prod(shape[1:])) * 4 + 31) // 32 * 32), shape, dt)

        gp = keep("gp", [P, 3, D])
        acc = keep("acc", [P, 2, 512])
        ident = keep("ident", [P, P])
        ones = keep("ones", [P, P])
        upper = keep("upper", [P, P])
        cs = keep("cs", [P, S])
        trig = keep("trig", [P, 2, T, HALF])
        krd = keep("krd", [P, T, 2, ROPE])
        colp = keep("colp", [P, 2, 96])
        prow = at("prow", W_ + 49152, [P, 2, P])
        bmod = colp[:, 0, :].rearrange("p (l k) -> p l k", l=L)
        gpre = colp[:, 1, 0:32].rearrange("p (w l k) -> p w l k", w=2, l=L)
        qg = colp[:, 1, 32:36].rearrange("p (l k) -> p l k", l=L)
        kvg = colp[:, 1, 36:38]
        lcol = colp[:, 1, 38:54].rearrange("p (w l k) -> p w l k", w=4, l=L)
        cw = colp[:, 1, 54:70].rearrange("p (l w k) -> p l w k", l=L, w=4)
        sgub = colp[:, 1, 70:78].rearrange("p (l g) -> p l g", l=L)
        modc = keep("modc", [P, 4, KD])
        modn = keep("modn", [P, 4, KD])
        sp = keep("sp", [P, 4, L, 2])
        nsp = keep("nsp", [P, L, 2])
        hb = keep("hb", [P, 2, L, 2])
        cond = keep("cond", [P, 2, KD])
        eps = keep("eps", [P, 2])
        ss = keep("ss", [P, T])
        rms = keep("rms", [P, T])
        rinv = keep("rinv", [P, T])
        st8 = keep("st8", [P, 3, 8])
        bn = keep("bn", [P, T, 6])
        mv = keep("mv", [P, T, 2])
        sd = keep("sd", [P, 2, T])
        am = keep("am", [P, 2, 4, T])
        router = keep("router", [P, KD, E])
        iot = keep("iot", [P, MAXT])
        assert place[0] <= 229344, place[0]

        ps = ctx.enter_context(nc.psum_tensor("ps", [P, 8, 512], F32))
        scratch = nc.dram_tensor("scratch", (MAXT * P, D), F32).ap()

        def sem(name):
            return ctx.enter_context(nc.semaphore(name))

        raw_full = [sem(f"raw_full{i}") for i in range(RAWS)]
        mraw_full = [sem(f"mraw_full{i}") for i in range(MRAWS)]
        mod_read, hi_ready, lo_ready, w_used, mod_ps, mod_out = map(sem, (
            "mod_read", "hi_ready", "lo_ready", "w_used", "mod_ps", "mod_out"))
        x_dma, c_dma, par_dma, lpar_dma, post_dma, zero_dma, out_dma = map(sem, (
            "x_dma", "c_dma", "par_dma", "lpar_dma", "post_dma", "zero_dma", "out_dma"))
        const_ready, cond_ready, sp_a, sp_b, sp_c, zeros_ready, zeros2_ready = map(sem, (
            "const_ready", "cond_ready", "sp_a", "sp_b", "sp_c", "zeros_ready", "zeros2_ready"))
        act_chain, dve_chain = sem("act_chain"), sem("dve_chain")
        rms_ready, xn_ready, xT_ps, hT_hi, hT_ready, x_upd, upd_tmp, pss = map(sem, (
            "rms_ready", "xn_ready", "xT_ps", "hT_hi", "hT_ready", "x_upd", "upd_tmp", "pss"))
        za_ps, zb_ps, zc_ps, zq_cp, zuv_ready, zx_cp, zy_ready = map(sem, (
            "za_ps", "zb_ps", "zc_ps", "zq_cp", "zuv_ready", "zx_cp", "zy_ready"))
        sw_ps, sw_cp, sw_ready, bn_done, sd_ready, vn_ready, mix_ps, ysg_ready, ysT_ps = map(sem, (
            "sw_ps", "sw_cp", "sw_ready", "bn_done", "sd_ready", "vn_ready", "mix_ps", "ysg_ready", "ysT_ps"))
        yT_hi, yT_ready = sem("yT_hi"), sem("yT_ready")
        xc_ready, gate_ps, gate_t, la_ready, ea_ready, lq_ready, lsq_ready, ylru = map(sem, (
            "xc_ready", "gate_ps", "gate_t", "la_ready", "ea_ready", "lq_ready", "lsq_ready", "ylru"))
        bd_ready, col_ps, col_ready = map(sem, ("bd_ready", "col_ps", "col_ready"))
        qs_ready, zqn_ready, qkT_ps, att_in, v_ps, v_ready = map(sem, (
            "qs_ready", "zqn_ready", "qkT_ps", "att_in", "v_ps", "v_ready"))
        q_ps, k_ps, q_ev, k_ev, s_ps, nm_ready, exp_ready, pn_ready, pt_ps, pt_ev, o_ps = map(sem, (
            "q_ps", "k_ps", "q_ev", "k_ev", "s_ps", "nm_ready", "exp_ready", "pn_ready", "pt_ps", "pt_ev", "o_ps"))
        wo_ps, ye_free = sem("wo_ps"), sem("ye_free")
        gu_ps, silu_ready, act_mul, act_hi, act_ready, dn_ps, dn_ev = map(sem, (
            "gu_ps", "silu_ready", "act_mul", "act_hi", "act_ready", "dn_ps", "dn_ev"))
        lg_ps, msk_ready, pos_ps, gexp_in, gexp, tab_ready, scat_dma = map(sem, (
            "lg_ps", "msk_ready", "pos_ps", "gexp_in", "gexp", "tab_ready", "scat_dma"))
        xg_dma, xg_ps, xg_full, xg_hi, xg_ready = map(sem, ("xg_dma", "xg_ps", "xg_full", "xg_hi", "xg_ready"))
        e_ps, e_silu, e_mul, aT_ps, aT_hi, aT_ready, ye_ps, ye_ev, ye_dma, yg_dma, ym_ready = map(sem, (
            "e_ps", "e_silu", "e_mul", "aT_ps", "aT_hi", "aT_ready", "ye_ps", "ye_ev", "ye_dma", "yg_dma",
            "ym_ready"))

        wmod = a["w_mod"].rearrange("l (p k) n -> l p k n", k=KD)

        def src_of(u):
            kind, l, c, kh = u
            if kind == "mod":
                return wmod[l, :, 4 * kh:4 * kh + 4, 512 * c:512 * c + 512], 4, 512
            if kind == "win":
                c0, w = ((0, QKR), (QKR, 512), (QKR + 512, 512))[c]
                return a["w_in"][l, 512 * kh:512 * kh + 512, c0:c0 + w].rearrange("(k p) n -> p k n", p=P), 4, w
            if kind == "wo":
                return a["w_o"][l, 512 * kh:512 * kh + 512, 512 * c:512 * c + 512].rearrange(
                    "(k p) n -> p k n", p=P), 4, 512
            if kind in ("gate", "up"):
                return a[f"ffn_w_{kind}"][0, :, 256 * c:256 * c + 256].rearrange("(k p) n -> p k n", p=P), 8, 256
            n, f, step = l, c, kh
            return a["ffn_w_down"][0, P * f:P * (f + step), 512 * n:512 * n + 512].rearrange(
                "(k p) n -> p k n", p=P), step, 512

        def unit_size(j):
            return 4 * EW[j // 4][1] if j < 4 * len(EW) else min(2, NB - 2 * (j - 4 * len(EW))) * D

        def size_of(u):
            _, k, w = src_of(u)
            return k * w

        block = ctx.enter_context(nc.Block())

        @block.sync
        def _(eng):
            mods = weights = 0
            seen = []
            for r, u in enumerate(UNITS):
                if r >= RAWS:
                    kind, count = seen[r - RAWS]
                    eng.wait_ge(mod_read if kind == "mod" else lo_ready, count)
                src, k, w = src_of(u)
                eng.dma_start(raw[:, r % RAWS, 0:k * w].rearrange("p (k n) -> p k n", k=k), src).then_inc(
                    raw_full[r % RAWS], 16)
                if u[0] == "mod":
                    mods += 1
                    seen.append(("mod", mods))
                else:
                    weights += 1
                    seen.append(("w", weights))
                if r == 0:
                    eng.dma_start(x[:], a["x"][0].rearrange("(t p) d -> p t d", p=P)).then_inc(x_dma, 16)
            eng.wait_ge(lo_ready, SB)
            eng.wait_ge(lg_ps, 1)
            eng.wait_ge(tab_ready, 1)
            n = eng.value_load(eti[0:1, 0:1], min_val=8, max_val=MAXT - 1)

            def unit(i, e, j):
                eng.wait_ge(lo_ready, i * EU + (SB + j - MRAWS + 1))
                dst = mraw[:, j % MRAWS, :]
                if j < 4 * len(EW):
                    c0, w = EW[j // 4]
                    name = "moe_w_gate" if j % 4 < 2 else "moe_w_up"
                    kh = j % 2
                    src = a[name][0][bass.ds(e, 1), 512 * kh:512 * kh + 512, c0:c0 + w].rearrange(
                        "a (k p) n -> p (a k) n", p=P)
                    dst = dst[:, 0:4 * w].rearrange("p (k n) -> p k n", k=4)
                else:
                    f = 2 * (j - 4 * len(EW))
                    k = min(2, NB - f)
                    src = a["moe_w_down"][0][bass.ds(e, 1), P * f:P * (f + k), :].rearrange(
                        "a (k p) n -> p (a k) n", p=P)
                    dst = dst[:, 0:k * D].rearrange("p (k n) -> p k n", k=k)
                eng.dma_start(dst, src).then_inc(mraw_full[j % MRAWS], 16)

            with eng.Fori(0, n) as i:
                e = eng.value_load(eti[0:1, bass.ds(i + 1, 1)], min_val=0, max_val=E - 1)
                for j in range(EU):
                    unit(i, e, j)
            e = eng.value_load(eti[0:1, bass.ds(n + 1, 1)], min_val=0, max_val=E - 1)
            for j in range(2):
                unit(n, e, j)
            for t in range(T):
                eng.wait_ge(x_upd, 3 * T + t + 1)
                eng.dma_start(out[0, P * t:P * t + P, :], x[:, t, :]).then_inc(out_dma, 16)
            eng.wait_ge(out_dma, 16 * T)
            eng.wait_ge(mraw_full[1], 16)

        @block.gpsimd
        def _(eng):
            g = nc.gpsimd
            g.dma_start(cond[:, 0, :], a["c"][0].rearrange("(p k) -> p k", k=KD)).then_inc(c_dma, 16)
            g.dma_start(gp[:, 0, :], a["post_mix_g"][0:1, :].to_broadcast([P, D])).then_inc(post_dma, 16)
            g.dma_start(gp[:, 1, :], a["post_ffn_g"][0:1, :].to_broadcast([P, D])).then_inc(post_dma, 16)
            g.dma_start(gp[:, 2, :], a["post_ffn_g"][1:2, :].to_broadcast([P, D])).then_inc(post_dma, 16)
            g.memset(prow[:], 0.0).then_inc(zeros_ready, 1)
            eng.wait_ge(zeros_ready, 1)
            rows = [a["b_mod"].rearrange("l (k p) -> (l k) p", p=P)]
            rows += [a[n].rearrange("l (k p) -> (l k) p", p=P) for n in (
                "pre_mix_g", "pre_ffn_g", "q_norm_g", "kv_norm_g", "conv_b", "lru_ba", "lru_bx", "lru_lambda")]
            rows += [a["conv_w"].rearrange("l w (j p) -> (l w j) p", p=P), a["sgu_b"].rearrange("l g p -> (l g) p")]
            at_row = 0
            for n, src in enumerate(rows):
                k = src.shape[0]
                dst = prow[0:k, 0, :] if n == 0 else prow[at_row:at_row + k, 1, :]
                at_row += k if n else 0
                g.dma_start(dst, src).then_inc(par_dma, 16)
            assert at_row == 78
            for dst, src in (
                    (cs[:], a["cs_table"]), (trig[:], a["trig_table"]),
                    (router[:], a["moe_router"][0].rearrange("(k p) e -> p k e", p=P))):
                g.dma_start(dst, src).then_inc(par_dma, 16)

            g.memset(ident[:], 0.0).then_inc(zeros_ready, 1)
            g.memset(upper[:], 1.0).then_inc(zeros_ready, 1)
            g.memset(ones[:], 1.0)
            g.memset(eps[:, 0:1], 1e-6)
            g.memset(eps[:, 1:2], 1e-5)
            g.iota(iot[:], [[1, MAXT]], base=0, channel_multiplier=0, allow_small_or_imprecise_dtypes=True)
            eng.wait_ge(zeros_ready, 3)
            g.affine_select(out=ident[:], in_=ident[:], compare_op=ALU.not_equal, fill=1.0, base=0,
                            pattern=[[-1, P]], channel_multiplier=1)
            g.affine_select(out=upper[:], in_=upper[:], compare_op=ALU.is_gt, fill=0.0, base=0,
                            pattern=[[1, P]], channel_multiplier=-1).then_inc(const_ready, 1)

            def layer_params(l):
                if l:
                    eng.wait_ge(x_upd, 2 * T * l)
                loads = [
                    (lnrow[:, 0, :], a["sgu_ln_g"][l:l + 1, :].to_broadcast([P, SGU])),
                    (lnrow[:, 1, :], a["sgu_ln_b"][l:l + 1, :].to_broadcast([P, SGU])),
                    (sguw[:], a["sgu_w"][l].rearrange("g t s -> t g s")),
                    (wukv[:], a["w_ukv"][l].rearrange("p (h n) -> p h n", h=HEADS)),
                ]
                for k in range(2):
                    w = a["w_uq"][l, P * k:P * k + P, :].rearrange("p (h n) -> p h n", h=HEADS)
                    loads += [
                        (wuq[:, k, :, 0:NOPE + ROPE], w),
                        (wuq[:, k, :, NOPE + ROPE:NOPE + ROPE + HALF], w[:, :, NOPE + HALF:NOPE + ROPE]),
                        (wuq[:, k, :, NOPE + ROPE + HALF:P], w[:, :, NOPE:NOPE + HALF]),
                    ]
                for dst, src in loads:
                    g.dma_start(dst, src).then_inc(lpar_dma, 16)
                g.memset(bd[:], 0.0).then_inc(zeros2_ready, 1)
                eng.wait_ge(zeros2_ready, l + 1)
                for which, name in enumerate(("lru_wa", "lru_wx")):
                    for h in range(4):
                        o = 64 * (h % 2)
                        g.dma_start(bd[o:o + 64, which, h // 2, o:o + 64], a[name][l, h]).then_inc(bd_ready, 16)

            def sgu_mask(l):
                eng.wait_ge(sw_cp, l + 1)
                g.affine_select(out=sguw[:], in_=sguw[:], compare_op=ALU.is_ge, fill=0.0, base=0,
                                pattern=[[0, 4], [1, P]], channel_multiplier=-1).then_inc(sw_ready, 1)

            def add_update(s, tmp):
                for t in range(T):
                    eng.wait_ge(upd_tmp, T * s + t + 1)
                    g.tensor_tensor(x[:, t, :], x[:, t, :], tmp[:, t % 2, :], ALU.add).then_inc(x_upd, 1)

            layer_params(0)
            sgu_mask(0)
            add_update(0, tmpm)
            g.dma_start(gp[:, 0, :], a["post_mix_g"][1:2, :].to_broadcast([P, D])).then_inc(post_dma, 16)
            add_update(1, tmpf)
            layer_params(1)
            sgu_mask(1)
            g.memset(gp[:, 1, :], 0.0).then_inc(zeros2_ready, 1)
            eng.wait_ge(zeros2_ready, L + 1)
            for i in range(MAXT):
                g.dma_start(scratch[P * i:P * i + P, :], gp[:, 1, :]).then_inc(zero_dma, 16)
            add_update(2, tmpm)

            eng.wait_ge(tab_ready, 1)
            eng.wait_ge(xn_ready, 4 * T)
            eng.wait_ge(zero_dma, 16 * MAXT)
            for t in range(T):
                for k in range(2):
                    g.indirect_dma_start(out=scratch, out_offset=bass.IndirectOffsetOnAxis(
                        ap=sli[:, k, t:t + 1], axis=0), in_=xn[:, t, :], in_offset=None).then_inc(scat_dma, 16)
            eng.wait_ge(scat_dma, 16 * 2 * T)
            n = eng.value_load(eti[0:1, 0:1], min_val=8, max_val=MAXT - 1)
            eng.sem_inc(ye_free, 1)
            g.dma_start(xg[:], scratch[0:P, :]).then_inc(xg_dma, 16)
            with eng.Fori(0, n) as i:
                eng.wait_ge(xg_ps, i + 1)
                g.dma_start(xg[:], scratch[bass.ds((i + 1) * P, P), :]).then_inc(xg_dma, 16)
                eng.wait_ge(ye_ev, i + 1)
                g.dma_start(scratch[bass.ds(i * P, P), :], ye[:]).then_inc(ye_dma, 16)
                eng.wait_ge(xg_ready, i + 2)
                eng.wait_ge(lo_ready, i * EU + (SB + EU + 2))
                eng.wait_ge(ye_dma, i * 16 + 16)
                eng.sem_inc(ye_free, 1)
            for t in range(T):
                for k in range(2):
                    g.indirect_dma_start(out=yg[:, t, k, :], out_offset=None, in_=scratch,
                                         in_offset=bass.IndirectOffsetOnAxis(ap=sli[:, k, t:t + 1], axis=0)
                                         ).then_inc(yg_dma, 16)
                eng.wait_ge(yg_dma, 32 * (t + 1))
            add_update(3, tmpf)

        @block.tensor
        def _(eng):
            mm = nc.tensor.matmul

            def mm3(o, lhs, rhs, start, stop):
                (lh, ll), (rh, rl) = lhs, rhs
                mm(o, lh, rh, start=start, stop=False)
                mm(o, lh, rl, start=False, stop=False)
                return mm(o, ll, rh, start=False, stop=stop)

            def unit_of(s, k, w):
                v = spl[:, s % SPLS, :, 0:k * w].rearrange("p h (k n) -> p h k n", k=k)
                return lambda kk, c0, n: (v[:, 0, kk, c0:c0 + n], v[:, 1, kk, c0:c0 + n])

            def hi_lo(t, k, c0, n):
                return t[:, 0, k, c0:c0 + n], t[:, 1, k, c0:c0 + n]

            def tr(o, i):
                return nc.tensor.transpose(o, i, ident[:])

            def mod(m, bank):
                c = m % MODC
                eng.wait_ge(mod_read, 2 * (m + 1))
                if m:
                    eng.wait_ge(mod_out, m)
                v = acc[:, m % 2, :]
                if c // 2 in (2, 5):
                    mm(ps[:, bank, :], ones[:], v, start=True, stop=True, skip_group_check=True)
                    for q in range(4):
                        b = bmod[:, m // MODC, 4 * c + q:4 * c + q + 1].to_broadcast([P, P])
                        last = mm(ps[:, bank, P * q:P * q + P], b, ident[:], start=False, stop=True,
                                  skip_group_check=True)
                else:
                    for q in range(4):
                        last = mm(ps[:, bank, q:q + 1], v[:, P * q:P * q + P], ones[:, 0:1], start=True, stop=True)
                last.then_inc(mod_ps, 1)

            def prenorm(s):
                for k in range(KD):
                    for t in range(T):
                        if k == 0:
                            eng.wait_ge(xn_ready, T * s + t + 1)
                        last = tr(ps[:, k, P * t:P * t + P], xn[:, t, P * k:P * k + P])
                    last.then_inc(xT_ps, 1)

            def in_proj(l):
                for part, (w, bank0, done) in enumerate(((QKR, 0, za_ps), (512, 4, zb_ps), (512, 0, zc_ps))):
                    for kh in range(2):
                        s = W_IN[l] + 2 * part + kh
                        u = unit_of(s, 4, w)
                        eng.wait_ge(lo_ready, s + 1)
                        for t in range(4):
                            if part == 2 and kh == 0:
                                eng.wait_ge(zq_cp, T * l + t + 1)
                            for kk in range(4):
                                k = 4 * kh + kk
                                if part == 0 and kh == 0 and t == 0 and kk == 0:
                                    eng.wait_ge(hT_ready, KD * (2 * l + 1))
                                o = ps[:, bank0 + t, 0:w]
                                if part < 2:
                                    last = mm3(o, hi_lo(hT, k, P * t, P), u(kk, 0, w), k == 0, k == 7)
                                else:
                                    last = mm3(o, u(kk, P * t, P), hi_lo(hT, k, 0, S), k == 0, k == 7)
                            if kh and t < 3:
                                last.then_inc(done, 1)
                        last.then_inc(w_used, 1)

            def sgu(l):
                eng.wait_ge(lpar_dma, 16 * 10 * (l + 1))
                eng.wait_ge(zuv_ready, T * (l + 1))
                for g in range(4):
                    last = tr(ps[:, 4, P * g:P * g + P], sguw[:, g, :])
                last.then_inc(sw_ps, 1)

            def lru_gates(l):
                eng.wait_ge(bd_ready, 16 * 8 * (l + 1))
                eng.wait_ge(zx_cp, 2 * (l + 1))
                eng.wait_ge(zy_ready, 2 * (l + 1))
                eng.wait_ge(xc_ready, l + 1)
                for which in range(2):
                    for j in range(2):
                        last = mm(ps[:, 2 * which + j, :], bd[:, which, j, :], lt[:, 0, j, :], start=True, stop=True)
                last.then_inc(gate_ps, 1)

            def sgu_mix(l):
                eng.wait_ge(vn_ready, l + 1)
                eng.wait_ge(sw_ready, l + 1)
                for g in range(4):
                    o = ps[:, 5 + g // 2, 256 * (g % 2):256 * (g % 2) + 256].rearrange("p (t c) -> p t c", t=T)
                    last = mm(o, sguw[:, g, :], zuv[:, :, SGU + 64 * g:SGU + 64 * g + 64], start=True, stop=True)
                last.then_inc(mix_ps, 1)
                eng.wait_ge(ysg_ready, l + 1)
                for j in range(2):
                    for t in range(T):
                        last = tr(ps[:, (4, 7)[j], P * t:P * t + P], zuv[:, t, P * j:P * j + P])
                    last.then_inc(ysT_ps, 1)

            def latents(l):
                eng.wait_ge(zqn_ready, l + 1)
                eng.wait_ge(gate_t, l + 1)
                eng.wait_ge(yT_ready, 8 * l + 2)
                for j in range(3):
                    for t in range(T):
                        tr(ps[:, 5 + j, P * t:P * t + P], zq[:, t, P * j:P * j + P])
                for t in range(T):
                    last = tr(ps[0:64, 3, P * t:P * t + P], krd[:, t].rearrange("p a b -> p (a b)"))
                last.then_inc(qkT_ps, 1)
                eng.wait_ge(att_in, l + 1)
                for t in range(T):
                    last = mm(ps[:, 4 + t, :].rearrange("p (h c) -> p h c", h=HEADS), qT[:, 2, P * t:P * t + P],
                              wukv[:, :, NOPE:NOPE + VD], start=True, stop=True)
                last.then_inc(v_ps, 1)

            def queries(l, h):
                n = HEADS * l + h
                eng.wait_ge(q_ev, n) if n else None
                for k in range(2):
                    last = mm(ps[:, 0, :], wuq[:, k, h, :], qT[:, k, :], start=(k == 0), stop=(k == 1))
                last.then_inc(q_ps, 1)
                eng.wait_ge(k_ev, n) if n else None
                mm(ps[0:NOPE, 1, :], wukv[:, h, 0:NOPE], qT[:, 2, :], start=True, stop=True).then_inc(k_ps, 1)

            def scores(l, h):
                n = HEADS * l + h
                eng.wait_ge(q_ev, n + 1)
                eng.wait_ge(k_ev, n + 1)
                for i in range(T):
                    if h == 0:
                        eng.wait_ge(v_ready, l + 1)
                    else:
                        eng.wait_ge(pt_ev, T * (n - 1) + i + 1)
                    w = P * (i + 1)
                    mm(ps[:, 4 + i, 0:w], qb[:, h % 2, P * i:w], kb[:, h % 2, 0:w], start=True,
                       stop=True).then_inc(s_ps, 1)

            def turn(l, h):
                n = HEADS * l + h
                for i in range(T):
                    eng.wait_ge(pn_ready, T * n + i + 1)
                    for j in range(i + 1):
                        last = tr(ps[:, 4 + i, P * j:P * j + P], pr[:, i, P * j:P * j + P])
                    last.then_inc(pt_ps, 1)

            def values(l, h):
                n = HEADS * l + h
                eng.wait_ge(pt_ev, T * (n + 1))
                if h % 2 == 0:
                    eng.wait_ge(yT_ready, 8 * l + 4 + h // 2)
                o = 64 * (h % 2)
                for j in range(T):
                    last = mm(ps[o:o + 64, 2, P * j:S], vb[:, j, VD * h:VD * h + VD], pT[:, j, P * j:S],
                              start=(j == 0), stop=True, skip_group_check=True)
                last.then_inc(o_ps, 1)

            def out_proj(l):
                for n in range(2):
                    for i, kh in enumerate((1, 0)):
                        s = W_O[l] + 2 * n + i
                        u = unit_of(s, 4, 512)
                        if n == 0 and i == 0:
                            eng.wait_ge(yT_ready, 8 * (l + 1))
                            eng.wait_ge(pt_ev, T * HEADS * (l + 1))
                            eng.wait_ge(mod_out, 10 if l == 0 else L * MODC)
                        eng.wait_ge(lo_ready, s + 1)
                        for t in range(T):
                            for kk in range(4):
                                last = mm3(ps[:, 2 * t + n, :], hi_lo(yT, 4 * kh + kk, P * t, P), u(kk, 0, 512),
                                           i == 0 and kk == 0, i == 1 and kk == 3)
                            if t < 3 and i == 1:
                                last.then_inc(wo_ps, 1)
                        last.then_inc(w_used, 1)

            def dense():
                s, m, downs = W_FF, 10, 0
                eng.wait_ge(hT_ready, KD * 2)
                for g, blocks in enumerate(GROUPS):
                    for c in range(blocks[0] // 2, blocks[-1] // 2 + 1):
                        units = [unit_of(s + i, KD, 256) for i in range(2)]
                        for b in range(2):
                            f = 2 * c + b
                            if f >= 2:
                                eng.wait_ge(act_mul, f - 1)
                            for i in range(2):
                                if b == 0:
                                    eng.wait_ge(lo_ready, s + i + 1)
                                for k in range(KD):
                                    last = mm3(ps[:, 2 * b + i, :], units[i](k, P * b, P), hi_lo(hT, k, 0, S),
                                               k == 0, k == KD - 1)
                                if b == 1:
                                    last.then_inc(w_used, 1)
                                elif i == 1:
                                    last.then_inc(gu_ps, 1)
                        s += 2
                        eng.wait_ge(dn_ev, 8 * g) if g else None
                        mod(m, 4)
                        m += 1
                    eng.wait_ge(mod_out, m)
                    eng.wait_ge(act_ready, blocks[-1] + 1)
                    step = 3 if len(blocks) == 6 else 4
                    for n in range(2):
                        for f0 in range(blocks[0], blocks[-1] + 1, step):
                            u = unit_of(s, step, 512)
                            eng.wait_ge(lo_ready, s + 1)
                            for t in range(T):
                                if downs and f0 == blocks[0]:
                                    eng.wait_ge(dn_ev, 4 * (downs - 1) + t + 1)
                                for i in range(step):
                                    f = f0 + i
                                    last = mm3(ps[:, 4 + t, :], hi_lo(act, f - blocks[0], P * t, P), u(i, 0, 512),
                                               f == blocks[0], f == blocks[-1])
                                if t < 3 and f0 + step > blocks[-1]:
                                    last.then_inc(dn_ps, 1)
                            last.then_inc(w_used, 1)
                            s += 1
                        downs += 1
                    if g < 3:
                        eng.wait_ge(dn_ev, 4 * downs)
                        mod(m, 4)
                        m += 1

            def route():
                eng.wait_ge(par_dma, 16 * 14)
                eng.wait_ge(hT_ready, KD * 4)
                for t in range(T):
                    for k in range(KD):
                        last = mm(ps[:, 0, E * t:E * t + E], hTf[:, k, P * t:P * t + P], router[:, k, :],
                                  start=(k == 0), stop=(k == KD - 1))
                last.then_inc(lg_ps, 1)
                eng.wait_ge(msk_ready, 1)
                for t in range(T):
                    for i in range(t + 1):
                        mm(ps[:, 1, E * t:E * t + E], upper[:] if i == t else ones[:], msk[:, i, :],
                           start=(i == 0), stop=(i == t))
                for t in range(T):
                    last = mm(ps[:, 2, 0:E], ones[:], msk[:, t, :], start=(t == 0), stop=(t == T - 1))
                last.then_inc(pos_ps, 1)

            def turn_rows(count):
                eng.wait_ge(xg_dma, count * 16)
                for k in range(KD):
                    last = tr(ps[:, 2 + k // 4, P * (k % 4):P * (k % 4) + P], xg[:, P * k:P * k + P])
                last.then_inc(xg_ps, 1)

            def experts():
                eng.wait_ge(tab_ready, 1)
                n = eng.value_load(eti[0:1, 0:1], min_val=8, max_val=MAXT - 1)
                turn_rows(1)
                with eng.Fori(0, n) as i:
                    def unit(j, k, w):
                        eng.wait_ge(lo_ready, i * EU + (SB + j + 1))
                        return unit_of(SB + j, k, w)

                    def turn_act(c):
                        eng.wait_ge(e_mul, i * 3 + (c + 1))
                        if c == 2:
                            eng.wait_ge(aT_ready, i * 3 + 1)
                        for q in range(EW[c][1] // P):
                            last = tr(ps[:, 6 + c % 2, P * q:P * q + P],
                                      acte[:, EW[c][0] + P * q:EW[c][0] + P * q + P])
                        last.then_inc(aT_ps, 1)

                    eng.wait_ge(xg_ready, i + 1)
                    for c, (c0, w) in enumerate(EW):
                        if c == 2:
                            eng.wait_ge(e_mul, i * 3 + 1)
                        for part in range(2):
                            for kh in range(2):
                                u = unit(4 * c + 2 * part + kh, 4, w)
                                for kk in range(4):
                                    k = 4 * kh + kk
                                    last = mm3(ps[:, 2 * (c % 2) + part, 0:w], hi_lo(xgT, k, 0, P), u(kk, 0, w),
                                               k == 0, k == KD - 1)
                                last.then_inc(w_used, 1)
                        if c:
                            turn_act(c - 1)
                    turn_rows(i + 2)
                    turn_act(2)
                    for j in range(4 * len(EW), EU):
                        f0 = 2 * (j - 4 * len(EW))
                        step = min(2, NB - f0)
                        u = unit(j, step, D)
                        eng.wait_ge(aT_ready, i * 3 + (min(f0 + step - 1, NB - 1) // 4 + 1))
                        for b in range(step):
                            for h in range(2):
                                last = mm3(ps[:, 4 + h, :], hi_lo(aT, f0 + b, 0, P), u(b, 512 * h, 512),
                                           f0 + b == 0, f0 + b == NB - 1)
                        last.then_inc(w_used, 1)

            eng.wait_ge(const_ready, 1)
            eng.wait_ge(par_dma, 16 * 14)
            for i in range(2):
                last = tr(ps[0:P, 0, P * i:P * i + P], prow[:, i, :])
            last.then_inc(col_ps, 1)
            eng.wait_ge(col_ready, 1)
            for m in range(4):
                mod(m, 3)
            for l in range(L):
                eng.wait_ge(mod_out, 4 if l == 0 else L * MODC)
                prenorm(2 * l)
                in_proj(l)
                sgu(l)
                lru_gates(l)
                sgu_mix(l)
                latents(l)
                queries(l, 0)
                scores(l, 0)
                queries(l, 1)
                for h in range(HEADS):
                    turn(l, h)
                    if h + 1 < HEADS:
                        scores(l, h + 1)
                    values(l, h)
                    if h + 2 < HEADS:
                        queries(l, h + 2)
                    if l == 0 and h < 6:
                        mod(4 + h, 3)
                out_proj(l)
                eng.wait_ge(upd_tmp, T * (2 * l + 1))
                prenorm(2 * l + 1)
                if l == 0:
                    dense()
                else:
                    route()
                    experts()

        @block.scalar
        def _(eng):
            A = nc.scalar.activation
            chain = [0]

            def link(ins):
                chain[0] += 1
                ins.then_inc(act_chain, 1)
                eng.wait_ge(act_chain, chain[0])

            def hi(s):
                r = WEIGHTS[s]
                n = size_of(UNITS[r])
                eng.wait_ge(raw_full[r % RAWS], 16 * (r // RAWS + 1))
                if s >= SPLS:
                    eng.wait_ge(w_used, s - SPLS + 1)
                A(spl[:, s % SPLS, 0, 0:n], raw[:, r % RAWS, 0:n], ACT.Copy).then_inc(hi_ready, 1)

            def root(out_, in_, scale, e):
                return A(out_, in_, ACT.Sqrt, scale=scale, bias=eps[:, e:e + 1])

            def prenorm(s):
                if s:
                    eng.wait_ge(x_upd, T * s)
                else:
                    eng.wait_ge(x_dma, 16)
                for t in range(T):
                    last = A(xn[:, t, :], x[:, t, :], ACT.Square, accum_out=ss[:, t:t + 1])
                link(last)
                root(rms[:], ss[:], 1.0 / D, 0).then_inc(rms_ready, 1)
                if s < 3:
                    for q in range(KD):
                        eng.wait_ge(xT_ps, KD * s + q + 1)
                        if q == 0:
                            eng.wait_ge(mod_out, MODC * (s // 2) + (4 if s % 2 == 0 else 10))
                        c = modn if s >= 2 else modc
                        b = 2 * (s % 2)
                        A(hT[:, 0, q, :], ps[:, q, :], ACT.Identity, scale=c[:, b + 1, q:q + 1],
                          bias=c[:, b, q:q + 1]).then_inc(hT_hi, 1)

            def tile_hi(k, bank):
                A(yT[:, 0, k, :], ps[:, bank, :], ACT.Copy).then_inc(yT_hi, 1)

            def mixer(l):
                for s in range(W_IN[l], W_IN[l] + 6):
                    if l and s - W_IN[l] < 2:
                        continue
                    hi(s)
                for t in range(T):
                    eng.wait_ge(*((zb_ps, 3 * l + t + 1) if t < 3 else (w_used, W_IN[l] + 4)))
                    A(zuv[:, t, :], ps[:, 4 + t, :], ACT.Gelu_apprx_tanh).then_inc(zuv_ready, 1)
                for j in (2, 3):
                    eng.wait_ge(*((zc_ps, 3 * l + j + 1) if j < 3 else (w_used, W_IN[l] + 6)))
                    A(zxy[:, j, :], ps[:, j, :], ACT.Gelu_apprx_tanh).then_inc(zy_ready, 1)
                eng.wait_ge(gate_ps, l + 1)
                for which in range(2):
                    for j in range(2):
                        last = A(lt[:, 1 + which, j, :], ps[:, 2 * which + j, :], ACT.Tanh, scale=0.5,
                                 bias=hb[:, which, l, j:j + 1])
                last.then_inc(gate_t, 1)
                eng.wait_ge(bn_done, l + 1)
                A(sd[:, 0, :], mv[:, :, 1], ACT.Sqrt, bias=eps[:, 1:2]).then_inc(sd_ready, 1)
                eng.wait_ge(zq_cp, T * (l + 1))
                junk = krd[:].rearrange("p t a b -> p (t a b)")
                for t in range(T):
                    link(A(junk[:, 0:QL], zq[:, t, 0:QL], ACT.Square, accum_out=st8[:, 0, t:t + 1]))
                    link(A(junk[:, 0:KVL], zq[:, t, QL:QL + KVL], ACT.Square, accum_out=st8[:, 0, 4 + t:5 + t]))
                root(st8[:, 1, 0:4], st8[:, 0, 0:4], 1.0 / QL, 0)
                root(st8[:, 1, 4:8], st8[:, 0, 4:8], 1.0 / KVL, 0).then_inc(qs_ready, 1)
                eng.wait_ge(la_ready, l + 1)
                lf = lt[:].rearrange("p a j s -> p a (j s)")
                A(lf[:, 3], lf[:, 1], ACT.Exp)
                A(lf[:, 1], lf[:, 1], ACT.Tanh).then_inc(ea_ready, 1)
                for j in range(2):
                    eng.wait_ge(ysT_ps, 2 * l + j + 1)
                    tile_hi(4 + j, (4, 7)[j])
                eng.wait_ge(lq_ready, l + 1)
                q = zxy[:, 0:2, :]
                A(q, q, ACT.Sqrt, scale=-0.25).then_inc(lsq_ready, 1)
                eng.wait_ge(ylru, l + 1)
                for j in range(2):
                    A(yT[:, 0, 6 + j, :], lt[:, 0, j, :], ACT.Copy).then_inc(yT_hi, 1)
                eng.wait_ge(yT_ready, 8 * l + 4)
                eng.wait_ge(qkT_ps, l + 1)
                for j in range(2):
                    A(qT[:, j, :], ps[:, 5 + j, :], ACT.Copy, scale=qg[:, l, j:j + 1])
                A(qT[:, 2, :], ps[:, 7, :], ACT.Copy, scale=kvg[:, l:l + 1])
                for b in range(2):
                    last = A(kb[64:128, b, :], ps[0:64, 3, :], ACT.Copy)
                last.then_inc(att_in, 1)
                eng.wait_ge(v_ps, l + 1)
                A(vb[:], ps[:, 4:8, :], ACT.Copy).then_inc(v_ready, 1)

                def keys(h):
                    n = HEADS * l + h
                    eng.wait_ge(k_ps, n + 1)
                    if h >= 2:
                        eng.wait_ge(s_ps, T * (n - 1))
                    A(kb[0:NOPE, h % 2, :], ps[0:NOPE, 1, :], ACT.Copy).then_inc(k_ev, 1)

                keys(0)
                for h in range(HEADS):
                    n = HEADS * l + h
                    for i in range(T):
                        eng.wait_ge(nm_ready, T * n + i + 1)
                        if h:
                            eng.wait_ge(pt_ps, T * (n - 1) + i + 1)
                        w = P * (i + 1)
                        A(pr[:, i, 0:w], ps[:, 4 + i, 0:w], ACT.Exp, scale=SCALE, bias=am[:, 1, h % 4, i:i + 1],
                          accum_out=st8[:, 2, 4 * (h % 2) + i:4 * (h % 2) + i + 1]).then_inc(exp_ready, 1)
                    if h + 1 < HEADS:
                        keys(h + 1)
                    if h and h % 2 == 0:
                        eng.wait_ge(o_ps, n)
                        tile_hi(h // 2 - 1, 2)
                    if h:
                        eng.wait_ge(o_ps, n)
                    for i in range(T):
                        eng.wait_ge(pt_ps, T * n + i + 1)
                        w = P * (i + 1)
                        A(pT[:, 0:i + 1, P * i:w], ps[:, 4 + i, 0:w].rearrange("p (j q) -> p j q", j=i + 1),
                          ACT.Copy).then_inc(pt_ev, 1)
                    if h >= HEADS - 3:
                        hi(W_O[l] + h - (HEADS - 3))
                eng.wait_ge(o_ps, HEADS * (l + 1))
                tile_hi(3, 2)
                hi(W_O[l] + 3)
                if l == 0:
                    for i in range(2):
                        hi(W_FF + i)
                for t in range(T):
                    eng.wait_ge(*((wo_ps, 6 * l + 4 + t) if t < 3 else (w_used, W_O[l] + 4)))
                    link(A(tmpm[:, t % 2, :].rearrange("p (n c) -> p n c", n=2), ps[:, 2 * t:2 * t + 2, :],
                           ACT.Square, accum_out=ss[:, t:t + 1]))
                root(rms[:], ss[:], 1.0 / D, 0).then_inc(pss, 1)

            def post(s, y):
                for t in range(T):
                    link(A(tmpf[:, t % 2, :], y[:, t, :], ACT.Square, accum_out=ss[:, t:t + 1]))
                root(rms[:], ss[:], 1.0 / D, 0).then_inc(pss, 1)

            def dense():
                s, f = W_FF, 0

                def evict(w_end):
                    eng.wait_ge(*w_end)
                    if f >= 2:
                        eng.wait_ge(act_mul, f - 1)
                    A(sgf[:, f % 2, :], ps[:, 2 * (f % 2), :], ACT.Silu).then_inc(silu_ready, 1)
                    eng.wait_ge(act_mul, f + 1)
                    A(act[:, 0, f % 6, :], actf[:, f % 2, :], ACT.Copy).then_inc(act_hi, 1)

                for g, blocks in enumerate(GROUPS):
                    for c in range(blocks[0] // 2, blocks[-1] // 2 + 1):
                        hi(s + 2)
                        evict((gu_ps, c + 1))
                        f += 1
                        hi(s + 3)
                        evict((w_used, s + 2))
                        f += 1
                        s += 2
                    n = 4 if len(blocks) == 6 else 2
                    for i in range(n):
                        if s + 2 < SB:
                            hi(s + 2)
                        s += 1
                eng.wait_ge(dn_ev, 32)
                post(1, yf)

            def experts():
                eng.wait_ge(gexp_in, 1)
                A(ge[:, 0, :], ge[:, 0, :], ACT.Exp).then_inc(gexp, 1)
                eng.wait_ge(tab_ready, 1)
                n = eng.value_load(eti[0:1, 0:1], min_val=8, max_val=MAXT - 1)

                def part(i, j):
                    eng.wait_ge(mraw_full[j % MRAWS], i * (16 * EU // MRAWS) + 16 * (j // MRAWS + 1))
                    eng.wait_ge(w_used, i * EU + (SB + j - SPLS + 1))
                    w = unit_size(j % EU)
                    A(spl[:, (SB + j) % SPLS, 0, 0:w], mraw[:, j % MRAWS, 0:w], ACT.Copy).then_inc(hi_ready, 1)

                def rows(count):
                    eng.wait_ge(xg_full, count)
                    A(xgT[:, 0], xfull[:], ACT.Copy).then_inc(xg_hi, 1)

                part(0, 0)
                part(0, 1)
                rows(1)
                with eng.Fori(0, n) as i:
                    def silu(c):
                        eng.wait_ge(w_used, i * EU + (SB + 4 * c + 2))
                        w = EW[c][1]
                        eng.wait_ge(e_mul, i * 3 + c) if c else None
                        A(sge[:, 0:w], ps[:, 2 * (c % 2), 0:w], ACT.Silu).then_inc(e_silu, 1)

                    def turned(c):
                        eng.wait_ge(aT_ps, i * 3 + (c + 1))
                        w = EW[c][1]
                        A(aT[:, 0, 4 * c:4 * c + w // P, :].rearrange("p f q -> p (f q)"), ps[:, 6 + c % 2, 0:w],
                          ACT.Copy).then_inc(aT_hi, 1)

                    for j in range(2, 6):
                        part(i, j)
                        if j == 4:
                            silu(0)
                    for j in range(6, 10):
                        part(i, j)
                        if j == 8:
                            silu(1)
                    turned_at = {11: 0}
                    for j in range(10, 14):
                        part(i, j)
                        if j in turned_at:
                            turned(0)
                        if j == 12:
                            silu(2)
                    turned(1)
                    rows(i + 2)
                    turned(2)
                    for j in range(14, 20):
                        part(i, j)
                    eng.wait_ge(w_used, i * EU + (SB + EU))
                    eng.wait_ge(ye_free, i + 1)
                    A(ye[:].rearrange("p (h c) -> p h c", h=2), ps[:, 4:6, :], ACT.Copy).then_inc(ye_ev, 1)
                eng.wait_ge(ym_ready, T)
                post(3, ym)

            eng.wait_ge(c_dma, 16)
            A(cond[:, 1, :], cond[:, 0, :], ACT.Silu).then_inc(cond_ready, 1)
            eng.wait_ge(const_ready, 1)
            eng.wait_ge(col_ps, 1)
            A(colp[:], ps[:, 0, 0:2 * P].rearrange("p (a b) -> p a b", a=2)[:, :, 0:96], ACT.Copy).then_inc(col_ready, 1)
            eng.wait_ge(col_ready, 1)
            link(A(sp[:, 0], lcol[:, 3], ACT.Abs))
            A(sp[:, 0], sp[:, 0], ACT.Exp, scale=-1.0).then_inc(sp_a, 1)
            eng.wait_ge(sp_b, 1)
            A(sp[:, 2], sp[:, 1], ACT.Ln).then_inc(sp_c, 1)
            for l in range(L):
                prenorm(2 * l)
                mixer(l)
                prenorm(2 * l + 1)
                if l == 0:
                    dense()
                else:
                    experts()

        @block.vector
        def _(eng):
            V = nc.vector
            chain = [0]

            def link(ins):
                chain[0] += 1
                ins.then_inc(dve_chain, 1)
                eng.wait_ge(dve_chain, chain[0])

            def after(ins, s, v):
                ins.then_inc(s, 1)
                eng.wait_ge(s, v)

            def lo(s):
                r = WEIGHTS[s]
                n = size_of(UNITS[r])
                eng.wait_ge(hi_ready, s + 1)
                V.tensor_tensor(spl[:, s % SPLS, 1, 0:n], raw[:, r % RAWS, 0:n],
                                spl[:, s % SPLS, 0, 0:n].bitcast(F32), ALU.subtract).then_inc(lo_ready, 1)

            def mod_sum(m):
                v = acc[:, m % 2, :]
                if m >= 2:
                    eng.wait_ge(mod_ps, m - 1)
                for kh in range(2):
                    r = MODS[2 * m + kh]
                    eng.wait_ge(raw_full[r % RAWS], 16 * (r // RAWS + 1))
                    for kk in range(4):
                        w = raw[:, r % RAWS, 512 * kk:512 * kk + 512]
                        c = cond[:, 1, 4 * kh + kk:4 * kh + kk + 1]
                        if kh + kk == 0:
                            ins = V.tensor_scalar(v, w, c, None, ALU.mult)
                        else:
                            ins = V.scalar_tensor_tensor(out=v, in0=w, scalar=c, in1=v, op0=ALU.mult, op1=ALU.add)
                        if kk < 3:
                            link(ins)
                        else:
                            after(ins, mod_read, 2 * m + kh + 1)

            def mod_evict(m):
                l, c = divmod(m, MODC)
                bank = 3 if m < 10 else 4
                kind, half = divmod(c, 2)
                eng.wait_ge(mod_ps, m + 1)
                if kind in (2, 5):
                    slot = 0 if kind == 2 else 1 + l
                    eng.wait_ge(post_dma, 64 if l and kind == 2 else 48)
                    g = gp[:, slot, 512 * half:512 * half + 512]
                    V.tensor_tensor(g, ps[:, bank, :], g, ALU.mult).then_inc(mod_out, 1)
                else:
                    k = slice(4 * half, 4 * half + 4)
                    dst = (modn if l else modc)[:, {0: 0, 1: 1, 3: 2, 4: 3}[kind], k]
                    ins = V.tensor_tensor(dst, ps[:, bank, 0:4], bmod[:, l, 4 * c:4 * c + 4], ALU.add)
                    if kind in (1, 4):
                        link(ins)
                        ins = V.scalar_tensor_tensor(out=dst, in0=dst, scalar=1.0, in1=gpre[:, kind // 4, l, k],
                                                     op0=ALU.add, op1=ALU.mult)
                    after(ins, mod_out, m + 1)

            def prenorm(s):
                eng.wait_ge(rms_ready, s + 1)
                link(V.reciprocal(rinv[:], rms[:]))
                for t in range(T):
                    V.tensor_scalar(xn[:, t, :], x[:, t, :], rinv[:, t:t + 1], None, ALU.mult).then_inc(xn_ready, 1)
                c = modn if s >= 2 else modc
                b = 2 * (s % 2)
                for q in range(KD):
                    eng.wait_ge(*((xT_ps, KD * s + q + 1) if s == 3 else (hT_hi, KD * s + q + 1)))
                    o = hTf[:, q, :] if s == 3 else full[:, q % 2, :]
                    ins = V.tensor_scalar(o, ps[:, q, :], c[:, b + 1, q:q + 1], c[:, b, q:q + 1], ALU.mult, ALU.add)
                    if s == 3:
                        ins.then_inc(hT_ready, 1)
                        continue
                    link(ins)
                    V.tensor_tensor(hT[:, 1, q, :], o, hT[:, 0, q, :].bitcast(F32), ALU.subtract).then_inc(hT_ready, 1)

            def tile_lo(l, i, k, src):
                eng.wait_ge(yT_hi, 8 * l + i + 1)
                V.tensor_tensor(yT[:, 1, k, :], src, yT[:, 0, k, :].bitcast(F32), ALU.subtract).then_inc(yT_ready, 1)

            def mixer(l):
                w0 = W_IN[l]
                for s in range(w0 + (2 if l else 0), w0 + 4):
                    lo(s)
                for t in range(T):
                    eng.wait_ge(*((za_ps, 3 * l + t + 1) if t < 3 else (w_used, w0 + 2)))
                    V.tensor_copy(zq[:, t, :], ps[:, t, 0:QKR]).then_inc(zq_cp, 1)
                lo(w0 + 4)
                lo(w0 + 5)
                for t in range(T):
                    eng.wait_ge(zuv_ready, T * l + t + 1)
                    link(V.bn_stats(bn[:, t, :], zuv[:, t, SGU:2 * SGU]))
                    ins = V.bn_aggr(mv[:, t, :], bn[:, t, :])
                after(ins, bn_done, l + 1)
                for j in range(2):
                    eng.wait_ge(zc_ps, 3 * l + j + 1)
                    V.tensor_copy(zxy[:, j, :], ps[:, j, :]).then_inc(zx_cp, 1)
                eng.wait_ge(zx_cp, 2 * (l + 1))
                for j in range(2):
                    link(V.tensor_scalar(lt[:, 0, j, :], zxy[:, j, :], cw[:, l, 3, j:j + 1], lcol[:, 0, l, j:j + 1],
                                         ALU.mult, ALU.add))
                for tap in range(3):
                    sh = 3 - tap
                    for j in range(2):
                        ins = V.scalar_tensor_tensor(out=lt[:, 0, j, sh:], in0=zxy[:, j, 0:S - sh],
                                                     scalar=cw[:, l, tap, j:j + 1], in1=lt[:, 0, j, sh:],
                                                     op0=ALU.mult, op1=ALU.add)
                        if tap == 2 and j == 1:
                            after(ins, xc_ready, l + 1)
                        else:
                            link(ins)
                eng.wait_ge(sw_ps, l + 1)
                V.tensor_copy(sguw[:], ps[:, 4, :].rearrange("p (g t) -> p g t", g=4)).then_inc(sw_cp, 1)
                eng.wait_ge(sd_ready, l + 1)
                link(V.reciprocal(sd[:, 1, :], sd[:, 0, :]))
                v = zuv[:, :, SGU:2 * SGU]
                for t in range(T):
                    link(V.tensor_scalar(v[:, t, :], v[:, t, :], mv[:, t, 0:1], sd[:, 1, t:t + 1],
                                         ALU.subtract, ALU.mult))
                for i, op in enumerate((ALU.mult, ALU.add)):
                    ins = V.tensor_tensor(v, v, lnrow[:, i:i + 1, :].to_broadcast([P, T, SGU]), op)
                    if i == 0:
                        link(ins)
                    else:
                        after(ins, vn_ready, l + 1)
                eng.wait_ge(gate_t, l + 1)
                for j in range(2):
                    ins = V.tensor_scalar(lt[:, 1, j, :], lt[:, 1, j, :], 1.0, nsp[:, l, j:j + 1], ALU.add, ALU.mult)
                after(ins, la_ready, l + 1)
                link(V.scalar_tensor_tensor(out=lt[:, 2], in0=lt[:, 2], scalar=1.0, in1=lt[:, 0],
                                            op0=ALU.add, op1=ALU.mult))
                eng.wait_ge(mix_ps, l + 1)
                for g in range(4):
                    u = zuv[:, :, 64 * g:64 * g + 64]
                    o = ps[:, 5 + g // 2, 256 * (g % 2):256 * (g % 2) + 256].rearrange("p (t c) -> p t c", t=T)
                    ins = V.scalar_tensor_tensor(out=u, in0=o, scalar=sgub[:, l, g:g + 1], in1=u,
                                                 op0=ALU.add, op1=ALU.mult)
                after(ins, ysg_ready, l + 1)
                eng.wait_ge(qs_ready, l + 1)
                link(V.reciprocal(st8[:, 0, :], st8[:, 1, :]))
                for t in range(T):
                    V.tensor_scalar(zq[:, t, 0:QL], zq[:, t, 0:QL], st8[:, 0, t:t + 1], None, ALU.mult)
                    V.tensor_scalar(zq[:, t, QL:QL + KVL], zq[:, t, QL:QL + KVL], st8[:, 0, 4 + t:5 + t], None,
                                    ALU.mult)
                x1, x2 = zq[:, :, QL + KVL:QL + KVL + HALF], zq[:, :, QL + KVL + HALF:QKR]
                cos, sin = trig[:, 0], trig[:, 1]
                ra, rb = krd[:, :, 0, 0:HALF], krd[:, :, 0, HALF:ROPE]
                rc, rd = krd[:, :, 1, 0:HALF], krd[:, :, 1, HALF:ROPE]
                V.tensor_tensor(ra, x1, cos, ALU.mult)
                V.tensor_tensor(rc, x2, sin, ALU.mult)
                V.tensor_tensor(rb, x2, cos, ALU.mult)
                link(V.tensor_tensor(rd, x1, sin, ALU.mult))
                V.tensor_tensor(ra, ra, rc, ALU.subtract)
                link(V.tensor_tensor(rb, rb, rd, ALU.add))
                after(V.tensor_copy(krd[:, :, 1, :], krd[:, :, 0, :]), zqn_ready, l + 1)
                eng.wait_ge(ea_ready, l + 1)
                q = zxy[:, 0:2, :]
                link(V.tensor_tensor(q, lt[:, 3], lt[:, 3], ALU.mult))
                after(V.scalar_tensor_tensor(out=q, in0=q, scalar=1.0, in1=lt[:, 1], op0=ALU.add, op1=ALU.mult),
                      lq_ready, l + 1)
                for j in range(2):
                    tile_lo(l, j, 4 + j, ps[:, (4, 7)[j], :])
                eng.wait_ge(lsq_ready, l + 1)
                link(V.tensor_tensor(lt[:, 2], lt[:, 2], q, ALU.mult))
                for j in range(2):
                    ins = V.tensor_tensor_scan(lt[:, 0, j, :], lt[:, 3, j, :], lt[:, 2, j, :], 0.0, ALU.mult, ALU.add)
                link(ins)
                after(V.tensor_tensor(lt[:, 0], lt[:, 0], zxy[:, 2:4, :], ALU.mult), ylru, l + 1)
                for j in range(2):
                    tile_lo(l, 2 + j, 6 + j, lt[:, 0, j, :])

                def queries(h):
                    n = HEADS * l + h
                    eng.wait_ge(q_ps, n + 1)
                    if h >= 2:
                        eng.wait_ge(s_ps, T * (n - 1))
                    V.tensor_tensor(qb[:, h % 2, :], ps[:, 0, :], cs[:], ALU.mult).then_inc(q_ev, 1)

                queries(0)
                for h in range(HEADS):
                    n = HEADS * l + h
                    for i in range(T):
                        eng.wait_ge(s_ps, T * n + i + 1)
                        link(V.memset(ps[0:64, 4 + i, P * i + 64:P * i + P], NEG))
                        link(V.reduce_max(am[:, 0, h % 4, i:i + 1], ps[:, 4 + i, 0:P * (i + 1)], AX.X))
                        V.tensor_scalar(am[:, 1, h % 4, i:i + 1], am[:, 0, h % 4, i:i + 1], -SCALE, None,
                                        ALU.mult).then_inc(nm_ready, 1)
                    for i in range(T):
                        eng.wait_ge(exp_ready, T * n + i + 1)
                        r = am[:, 0, h % 4, i:i + 1]
                        link(V.reciprocal(r, st8[:, 2, 4 * (h % 2) + i:4 * (h % 2) + i + 1]))
                        p = pr[:, i, 0:P * (i + 1)]
                        V.tensor_scalar(p, p, r, None, ALU.mult).then_inc(pn_ready, 1)
                    if h + 1 < HEADS:
                        queries(h + 1)
                    if h and h % 2 == 0:
                        eng.wait_ge(o_ps, n)
                        tile_lo(l, 3 + h // 2, h // 2 - 1, ps[:, 2, :])
                    if l == 0 and h <= 6:
                        if h:
                            mod_evict(3 + h)
                        if h < 6:
                            mod_sum(4 + h)
                    if h >= HEADS - 3:
                        lo(W_O[l] + h - (HEADS - 3))
                tile_lo(l, 7, 3, ps[:, 2, :])
                lo(W_O[l] + 3)
                if l == 0:
                    for i in range(2):
                        lo(W_FF + i)

            def post(s, y, slot, tmp):
                eng.wait_ge(pss, s + 1)
                link(V.reciprocal(rinv[:], rms[:]))
                for t in range(T):
                    if t >= 2:
                        eng.wait_ge(x_upd, T * s + t - 1)
                    V.scalar_tensor_tensor(out=tmp[:, t % 2, :].rearrange("p (n c) -> p n c", n=2), in0=y(t),
                                           scalar=rinv[:, t:t + 1],
                                           in1=gp[:, slot, :].rearrange("p (n c) -> p n c", n=2),
                                           op0=ALU.mult, op1=ALU.mult).then_inc(upd_tmp, 1)

            def dense():
                s, f, m, downs = W_FF, 0, 10, 0

                def evict(w_end):
                    eng.wait_ge(*w_end)
                    eng.wait_ge(silu_ready, f + 1)
                    after(V.tensor_tensor(actf[:, f % 2, :], sgf[:, f % 2, :], ps[:, 2 * (f % 2) + 1, :], ALU.mult),
                          act_mul, f + 1)
                    eng.wait_ge(act_hi, f + 1)
                    V.tensor_tensor(act[:, 1, f % 6, :], actf[:, f % 2, :], act[:, 0, f % 6, :].bitcast(F32),
                                    ALU.subtract).then_inc(act_ready, 1)

                def down_evict(g, n, w_last):
                    for t in range(T):
                        eng.wait_ge(*((dn_ps, 6 * g + 3 * n + t + 1) if t < 3 else (w_used, w_last)))
                        o = yf[:, t, 512 * n:512 * n + 512]
                        if g:
                            V.tensor_tensor(o, ps[:, 4 + t, :], o, ALU.add).then_inc(dn_ev, 1)
                        else:
                            V.tensor_copy(o, ps[:, 4 + t, :]).then_inc(dn_ev, 1)

                for g, blocks in enumerate(GROUPS):
                    for c in range(blocks[0] // 2, blocks[-1] // 2 + 1):
                        lo(s + 2)
                        if m > 10:
                            mod_evict(m - 1)
                        evict((gu_ps, c + 1))
                        f += 1
                        lo(s + 3)
                        evict((w_used, s + 2))
                        f += 1
                        mod_sum(m)
                        m += 1
                        s += 2
                    n = 4 if len(blocks) == 6 else 2
                    for i in range(n):
                        lo(s + 2)
                        s += 1
                        if i == 0:
                            mod_evict(m - 1)
                            if g < 3:
                                mod_sum(m)
                        if i == n // 2 - 1:
                            down_evict(g, 0, s if n == 2 else s)
                    down_evict(g, 1, s)
                    if g < 3:
                        m += 1
                post(1, lambda t: yf[:, t, :].rearrange("p (n c) -> p n c", n=2), 1, tmpf)

            def route():
                eng.wait_ge(lg_ps, 1)
                link(V.tensor_copy(lg[:], ps[:, 0, 0:T * E].rearrange("p (t e) -> p t e", t=T)))
                for t in range(T):
                    link(V.max(mx8[:, t, :], lg[:, t, :]))
                    link(V.max_index(ix8[:, t, :], mx8[:, t, :], lg[:, t, :]))
                link(V.tensor_copy(ixf[:], ix8[:]))
                ex = iot[:, 0:E].unsqueeze(1).to_broadcast([P, T, E])
                for k in range(2):
                    link(V.tensor_tensor(oh[:, k], ex, ixf[:, :, k:k + 1].to_broadcast([P, T, E]), ALU.is_equal))
                after(V.tensor_tensor(msk[:], oh[:, 0], oh[:, 1], ALU.add), msk_ready, 1)
                V.tensor_tensor(ge[:, 0, :], mx8[:, :, 1], mx8[:, :, 0], ALU.subtract).then_inc(gexp_in, 1)
                eng.wait_ge(gexp, 1)
                link(V.tensor_scalar(ge[:, 1, :], ge[:, 0, :], 1.0, None, ALU.add))
                link(V.reciprocal(gt[:, 0, :], ge[:, 1, :]))
                link(V.tensor_tensor(gt[:, 1, :], gt[:, 0, :], ge[:, 0, :], ALU.mult))
                eng.wait_ge(pos_ps, 1)
                link(V.tensor_copy(tl[:, 1, :], ps[:, 2, 0:E]))
                link(V.tensor_scalar(tl[:, 0, :], tl[:, 1, :], 0.0, None, ALU.is_gt))
                for r in range(1, T):
                    link(V.scalar_tensor_tensor(out=tl[:, 0, :], in0=tl[:, 1, :], scalar=float(P * r), in1=tl[:, 0, :],
                                                op0=ALU.is_gt, op1=ALU.add))
                link(V.tensor_tensor_scan(tl[:, 1, :], ones[:, 0:E], tl[:, 0, :], 0.0, ALU.mult, ALU.add))
                link(V.tensor_tensor(tl[:, 2, :], tl[:, 1, :], tl[:, 0, :], ALU.subtract))
                link(V.scalar_tensor_tensor(out=gpos[:], in0=tl[:, 2:3, :].to_broadcast([P, T, E]), scalar=float(P),
                                            in1=ps[:, 1, 0:T * E].rearrange("p (t e) -> p t e", t=T),
                                            op0=ALU.mult, op1=ALU.add))
                for k in range(2):
                    link(V.tensor_tensor(prod[:, k], oh[:, k], gpos[:], ALU.mult))
                    link(V.reduce_sum(slf[:, k, :], prod[:, k], AX.X))
                link(V.tensor_copy(sli[:], slf[:]))
                link(V.tensor_tensor(cmp_[:], tl[:, 1:2, :].to_broadcast([P, MAXT, E]),
                                     iot[:].unsqueeze(2).to_broadcast([P, MAXT, E]), ALU.is_le))
                link(V.reduce_sum(etf[:, 1:], cmp_[:], AX.X))
                link(V.tensor_scalar(etf[:, 1:], etf[:, 1:], float(E - 1), None, ALU.min))
                link(V.tensor_copy(etf[:, 0:1], tl[:, 1, E - 1:E]))
                V.tensor_copy(eti[:], etf[:]).then_inc(tab_ready, 1)

            def experts():
                eng.wait_ge(tab_ready, 1)
                n = eng.value_load(eti[0:1, 0:1], min_val=8, max_val=MAXT - 1)

                def part(i, j):
                    eng.wait_ge(hi_ready, i * EU + (SB + j + 1))
                    w = unit_size(j % EU)
                    o = spl[:, (SB + j) % SPLS]
                    V.tensor_tensor(o[:, 1, 0:w], mraw[:, j % MRAWS, 0:w], o[:, 0, 0:w].bitcast(F32),
                                    ALU.subtract).then_inc(lo_ready, 1)

                def rows(count):
                    eng.wait_ge(xg_ps, count)
                    for k in range(KD):
                        ins = V.tensor_scalar(xfull[:, k, :], ps[:, 2 + k // 4, P * (k % 4):P * (k % 4) + P],
                                              modn[:, 3, k:k + 1], modn[:, 2, k:k + 1], ALU.mult, ALU.add)
                    ins.then_inc(xg_full, 1)
                    eng.wait_ge(xg_hi, count)
                    V.tensor_tensor(xgT[:, 1], xfull[:], xgT[:, 0].bitcast(F32), ALU.subtract).then_inc(xg_ready, 1)

                part(0, 0)
                part(0, 1)
                rows(1)
                with eng.Fori(0, n) as i:
                    def multiply(c):
                        eng.wait_ge(e_silu, i * 3 + (c + 1))
                        eng.wait_ge(w_used, i * EU + (SB + 4 * c + 4))
                        c0, w = EW[c]
                        V.tensor_tensor(acte[:, c0:c0 + w], sge[:, 0:w], ps[:, 2 * (c % 2) + 1, 0:w],
                                        ALU.mult).then_inc(e_mul, 1)

                    def turned(c):
                        eng.wait_ge(aT_hi, i * 3 + (c + 1))
                        w = EW[c][1]
                        f = slice(4 * c, 4 * c + w // P)
                        V.tensor_tensor(aT[:, 1, f, :], ps[:, 6 + c % 2, 0:w].rearrange("p (f q) -> p f q", q=P),
                                        aT[:, 0, f, :].bitcast(F32), ALU.subtract).then_inc(aT_ready, 1)

                    for j in range(2, 6):
                        part(i, j)
                    multiply(0)
                    for j in range(6, 10):
                        part(i, j)
                    multiply(1)
                    part(i, 10)
                    part(i, 11)
                    turned(0)
                    part(i, 12)
                    part(i, 13)
                    multiply(2)
                    turned(1)
                    rows(i + 2)
                    turned(2)
                    for j in range(14, 20):
                        part(i, j)
                for t in range(T):
                    eng.wait_ge(yg_dma, 32 * (t + 1))
                    link(V.tensor_scalar(ym[:, t, :], yg[:, t, 0, :], gt[:, 0, t:t + 1], None, ALU.mult))
                    V.scalar_tensor_tensor(out=ym[:, t, :], in0=yg[:, t, 1, :], scalar=gt[:, 1, t:t + 1],
                                           in1=ym[:, t, :], op0=ALU.mult, op1=ALU.add).then_inc(ym_ready, 1)
                post(3, lambda t: ym[:, t, :].rearrange("p (n c) -> p n c", n=2), 2, tmpf)

            eng.wait_ge(sp_a, 1)
            after(V.tensor_scalar(sp[:, 1], sp[:, 0], 1.0, None, ALU.add), sp_b, 1)
            eng.wait_ge(sp_c, 1)
            link(V.tensor_scalar(sp[:, 1], sp[:, 1], 1.0, None, ALU.subtract))
            link(V.tensor_scalar(sp[:, 3], sp[:, 1], 0.0, None, ALU.is_equal))
            link(V.tensor_tensor(sp[:, 1], sp[:, 1], sp[:, 3], ALU.add))
            link(V.reciprocal(sp[:, 1], sp[:, 1]))
            link(V.tensor_tensor(sp[:, 2], sp[:, 2], sp[:, 1], ALU.mult))
            link(V.tensor_tensor(sp[:, 2], sp[:, 2], sp[:, 3], ALU.add))
            link(V.tensor_tensor(sp[:, 2], sp[:, 2], sp[:, 0], ALU.mult))
            link(V.tensor_scalar(sp[:, 3], lcol[:, 3], -1.0, 0.0, ALU.mult, ALU.max))
            link(V.tensor_tensor(sp[:, 2], sp[:, 2], sp[:, 3], ALU.add))
            link(V.tensor_scalar(nsp[:], sp[:, 2], -4.0, None, ALU.mult))
            link(V.tensor_scalar(hb[:], lcol[:, 1:3], 0.5, None, ALU.mult))
            eng.wait_ge(cond_ready, 1)
            for m in range(4):
                mod_sum(m)
                if m:
                    mod_evict(m - 1)
            mod_evict(3)
            for l in range(L):
                prenorm(2 * l)
                mixer(l)
                post(2 * l, lambda t: ps[:, 2 * t:2 * t + 2, :], 0, tmpm)
                prenorm(2 * l + 1)
                if l == 0:
                    dense()
                else:
                    route()
                    experts()


def tables():
    pos = np.arange(S, dtype=np.float32)
    inv = np.float32(10000.0) ** (-np.arange(0, ROPE, 2, dtype=np.float32) / np.float32(ROPE))
    ang = (pos[:, None] * inv[None, :]).astype(np.float32)
    cos, sin = np.cos(ang), np.sin(ang)
    cs = np.concatenate([np.ones((NOPE, S), np.float32), cos.T, cos.T, -sin.T, sin.T]).astype(np.float32)
    trig = np.stack([cos, sin]).reshape(2, T, P, HALF).transpose(2, 0, 1, 3)
    return {"cs_table": np.ascontiguousarray(cs), "trig_table": np.ascontiguousarray(trig.astype(np.float32))}


def kernel(**inputs):
    from concourse import bacc
    from concourse.bass_utils import run_bass_kernel_spmd

    nc = bacc.Bacc("TRN2", target_bir_lowering=False, num_devices=1)
    arrays = {name: np.ascontiguousarray(v) for name, v in inputs.items()} | tables()
    args = {name: nc.dram_tensor(f"in_{name}", v.shape, mybir.dt.from_np(v.dtype), kind="ExternalInput").ap()
            for name, v in arrays.items()}
    out = nc.dram_tensor("out", (1, S, D), F32, kind="ExternalOutput").ap()
    build(nc, args, out)
    r = run_bass_kernel_spmd(nc, [{f"in_{name}": v for name, v in arrays.items()}], core_ids=[0])
    return r.results[0]["out"]
```

```python
from contextlib import ExitStack

import numpy as np

import concourse.bass as bass
from concourse import mybir

F32 = mybir.dt.float32
F32R = mybir.dt.float32r
I32 = mybir.dt.int32
U32 = mybir.dt.uint32
ALU = mybir.AluOpType
ACT = mybir.ActivationFunctionType
AX = mybir.AxisListType

P = 128
L = 2
S = 512
T = S // P
D = 1024
KD = D // P
HEADS, NOPE, ROPE, VD = 8, 64, 32, 64
QL, KVL = 256, 128
HALF = ROPE // 2
QKR = QL + KVL + ROPE
SGU, LRU = 256, 256
NEG = -1e30
SCALE = (NOPE + ROPE) ** -0.5
FF, FFE, E = 2816, 1408, 8
NB = FFE // P
UNIT = 2048
RAWS, SPLS, MRAWS = 4, 3, 6
MAXT = 16
MODC = 6 * D // 512
GROUPS = [list(range(0, 6)), list(range(6, 12)), list(range(12, 18)), list(range(18, 22))]
EW = [(0, 512), (512, 512), (1024, 384)]
SCORE_AT = ((5, 384), (6, 0), (5, 0), (4, 0))
SCORE_ORDER = (1, 0, 2, 3)
TURN_BANK = (3, 7)
EU = 4 * len(EW) + (NB + 1) // 2


def plan():
    units = []

    def mod(m):
        for kh in range(2):
            units.append(("mod", m // MODC, m % MODC, kh))

    m = 0
    for m in range(4):
        mod(m)
    m = 4
    for l in range(L):
        for part in range(3):
            for kh in range(2):
                units.append(("win", l, part, kh))
                if l == 0 and part * 2 + kh < 3:
                    mod(m)
                    m += 1
        if l == 0:
            for _ in range(3):
                mod(m)
                m += 1
        for n in range(2):
            for kh in (1, 0):
                units.append(("wo", l, n, kh))
        if l == 0:
            for g, blocks in enumerate(GROUPS):
                for c in range(blocks[0] // 2, blocks[-1] // 2 + 1):
                    units.append(("gate", l, c, 0))
                    units.append(("up", l, c, 0))
                    mod(m)
                    m += 1
                step = 3 if len(blocks) == 6 else 4
                for n in range(2):
                    for f in range(blocks[0], blocks[-1] + 1, step):
                        units.append(("down", n, f, step))
                if g < 3:
                    mod(m)
                    m += 1
    assert m == L * MODC
    return units


UNITS = plan()
WEIGHTS = [r for r, u in enumerate(UNITS) if u[0] != "mod"]
MODS = [r for r, u in enumerate(UNITS) if u[0] == "mod"]
SB = len(WEIGHTS)
W_IN = [WEIGHTS.index(UNITS.index(("win", l, 0, 0))) for l in range(L)]
W_O = [WEIGHTS.index(UNITS.index(("wo", l, 0, 1))) for l in range(L)]
W_FF = WEIGHTS.index(UNITS.index(("gate", 0, 0, 0)))


def build(nc, a, out):
    with ExitStack() as ctx:
        base = 16512
        place = [base]

        def at(name, offset, shape, dt=F32):
            return nc.alloc_sbuf_tensor_at(name, shape, dt, offset=offset)

        def region(size):
            o = place[0]
            place[0] += size
            return o

        X_, RAW_, HT_, SPL_ = region(16384), region(32768), region(32768), region(49152)
        W_ = region(57856)
        x = at("x", X_, [P, T, D])
        raw = at("raw", RAW_, [P, RAWS, UNIT])
        spl = at("spl", SPL_, [P, SPLS, 2, UNIT], F32R)
        hT = at("hT", HT_, [P, 2, KD, S], F32R)
        yT = at("yT", HT_, [P, 2, KD, S], F32R)
        zq = at("zq", W_, [P, T, QKR])
        qT = at("qT", W_, [P, 3, S])
        wuq = at("wuq", W_ + 6656, [P, 2, HEADS, P])
        wukv = at("wukv", W_ + 6656 + 8192, [P, HEADS, NOPE + VD])
        xn = at("xn", W_ + 18944, [P, T, D])
        xnf = at("xnf", HT_, [P, T, D])
        zuv = at("zuv", W_ + 18944, [P, T, 2 * SGU])
        zxy = at("zxy", W_ + 27136, [P, 4, S])
        pr = at("pr", W_ + 18944, [P, T, S])
        pT = at("pT", W_ + 27136, [P, T, S])
        T1 = W_ + 35328
        lt = at("lt", T1, [P, 4, 2, S])
        vb = at("vb", T1, [P, T, S])
        qb = at("qb", T1 + 8192, [P, 2, S])
        kb = at("kb", T1 + 12288, [P, 2, S])
        full = at("full", T1 + 8192, [P, 2, S])
        lnrow = at("lnrow", T1 + 16384, [P, 2, SGU])
        sguw = at("sguw", T1 + 18432, [P, 4, P])
        bd = at("bd", T1 + 20480, [P, 2, 2, P])
        tmpm = at("tmpm", T1, [P, 2, D])
        act = at("act", W_, [P, 2, 6, S], F32R)
        yf = at("yf", W_ + 24576, [P, T, D])
        sgf = at("sgf", W_ + 40960, [P, 2, S])
        actf = at("actf", W_ + 45056, [P, 2, S])
        tmpf = at("tmpf", W_ + 49152, [P, 2, D])
        mraw = at("mraw", RAW_, [P, MRAWS, UNIT])
        hTf = at("hTf", HT_, [P, KD, S])
        xgT = at("xgT", HT_ + 16384, [P, 2, KD, P], F32R)
        yg = at("yg", HT_, [P, T, 2, D])
        xg = at("xg", W_, [P, D])
        acte = at("acte", W_ + 4096, [P, FFE])
        sge = at("sge", W_ + 9728, [P, 512])
        ye = at("ye", W_ + 11776, [P, D])
        aT = at("aT", W_ + 35328, [P, 2, NB, P], F32R)
        xfull = at("xfull", W_ + 46592, [P, KD, P])
        ym = at("ym", W_ + 18944, [P, T, D])
        small = [W_ + 15872]

        def little(name, shape, dt=F32):
            n = int(np.prod(shape[1:])) * 4
            o = small[0]
            small[0] += (n + 31) // 32 * 32
            return at(name, o, shape, dt)

        lg = little("lg", [P, T, E])
        mx8 = little("mx8", [P, T, 8])
        ix8 = little("ix8", [P, T, 8], U32)
        ixf = little("ixf", [P, T, 8])
        oh = little("oh", [P, 2, T, E])
        msk = little("msk", [P, T, E])
        gpos = little("gpos", [P, T, E])
        prod = little("prod", [P, 2, T, E])
        slf = little("slf", [P, 2, T])
        sli = little("sli", [P, 2, T], I32)
        gt = little("gt", [P, 2, T])
        ge = little("ge", [P, 2, T])
        tl = little("tl", [P, 3, E])
        cmp_ = little("cmp", [P, MAXT, E])
        etf = little("etf", [P, 1 + MAXT])
        eti = little("eti", [P, 1 + MAXT], I32)
        assert small[0] <= W_ + 18944

        def keep(name, shape, dt=F32):
            return at(name, region((int(np.prod(shape[1:])) * 4 + 31) // 32 * 32), shape, dt)

        gp = keep("gp", [P, 3, D])
        acc = keep("acc", [P, 2, 512])
        ident = keep("ident", [P, P])
        ones = keep("ones", [P, P])
        upper = keep("upper", [P, P])
        cs = keep("cs", [P, S])
        trig = keep("trig", [P, 2, T, HALF])
        krd = keep("krd", [P, T, 2, ROPE])
        colp = keep("colp", [P, 2, 96])
        prow = at("prow", W_ + 49152, [P, 2, P])
        bmod = colp[:, 0, :].rearrange("p (l k) -> p l k", l=L)
        gpre = colp[:, 1, 0:32].rearrange("p (w l k) -> p w l k", w=2, l=L)
        qg = colp[:, 1, 32:36].rearrange("p (l k) -> p l k", l=L)
        kvg = colp[:, 1, 36:38]
        lcol = colp[:, 1, 38:54].rearrange("p (w l k) -> p w l k", w=4, l=L)
        cw = colp[:, 1, 54:70].rearrange("p (l w k) -> p l w k", l=L, w=4)
        sgub = colp[:, 1, 70:78].rearrange("p (l g) -> p l g", l=L)
        modc = keep("modc", [P, 4, KD])
        modn = keep("modn", [P, 4, KD])
        sp = keep("sp", [P, 4, L, 2])
        nsp = keep("nsp", [P, L, 2])
        hb = keep("hb", [P, 2, L, 2])
        cond = keep("cond", [P, 2, KD])
        eps = keep("eps", [P, 2])
        ss = keep("ss", [P, T])
        rms = keep("rms", [P, T])
        rinv = keep("rinv", [P, T])
        st8 = keep("st8", [P, 3, 8])
        bn = keep("bn", [P, T, 6])
        mv = keep("mv", [P, T, 2])
        sd = keep("sd", [P, 2, T])
        am = keep("am", [P, 2, 4, T])
        router = keep("router", [P, KD, E])
        iot = keep("iot", [P, MAXT])
        assert place[0] <= 229344, place[0]

        ps = ctx.enter_context(nc.psum_tensor("ps", [P, 8, 512], F32))
        scratch = nc.dram_tensor("scratch", (MAXT * P, D), F32).ap()

        def sem(name):
            return ctx.enter_context(nc.semaphore(name))

        raw_full = [sem(f"raw_full{i}") for i in range(RAWS)]
        mraw_full = [sem(f"mraw_full{i}") for i in range(MRAWS)]
        mod_read, hi_ready, lo_ready, w_used, mod_ps, mod_out = map(sem, (
            "mod_read", "hi_ready", "lo_ready", "w_used", "mod_ps", "mod_out"))
        x_dma, c_dma, par_dma, lpar_dma, post_dma, zero_dma, out_dma = map(sem, (
            "x_dma", "c_dma", "par_dma", "lpar_dma", "post_dma", "zero_dma", "out_dma"))
        const_ready, cond_ready, sp_a, sp_b, sp_c, zeros_ready, zeros2_ready = map(sem, (
            "const_ready", "cond_ready", "sp_a", "sp_b", "sp_c", "zeros_ready", "zeros2_ready"))
        act_chain, dve_chain = sem("act_chain"), sem("dve_chain")
        rms_ready, xn_ready, xT_ps, hT_hi, hT_ready, x_upd, pss = map(sem, (
            "rms_ready", "xn_ready", "xT_ps", "hT_hi", "hT_ready", "x_upd", "pss"))
        za_ps, zb_ps, zc_ps, zq_cp, zuv_ready, zx_cp, zy_ready = map(sem, (
            "za_ps", "zb_ps", "zc_ps", "zq_cp", "zuv_ready", "zx_cp", "zy_ready"))
        sw_ps, sw_cp, sw_ready, bn_done, sd_ready, vn_ready, mix_ps, ysg_ready, ysT_ps = map(sem, (
            "sw_ps", "sw_cp", "sw_ready", "bn_done", "sd_ready", "vn_ready", "mix_ps", "ysg_ready", "ysT_ps"))
        yT_hi, yT_ready = sem("yT_hi"), sem("yT_ready")
        xc_ready, gate_ps, gate_t, la_ready, ea_ready, lq_ready, lsq_ready, ylru = map(sem, (
            "xc_ready", "gate_ps", "gate_t", "la_ready", "ea_ready", "lq_ready", "lsq_ready", "ylru"))
        bd_ready, col_ps, col_ready, kr_ready, q_in, v2_ready = map(sem, (
            "bd_ready", "col_ps", "col_ready", "kr_ready", "q_in", "v2_ready"))
        qs_ready, zqn_ready, qkT_ps, att_in, v_ps, v_ready = map(sem, (
            "qs_ready", "zqn_ready", "qkT_ps", "att_in", "v_ps", "v_ready"))
        q_ps, k_ps, q_ev, k_ev, s_ps, nm_ready, exp_ready, pn_ready, pt_ps, pt_ev, o_ps = map(sem, (
            "q_ps", "k_ps", "q_ev", "k_ev", "s_ps", "nm_ready", "exp_ready", "pn_ready", "pt_ps", "pt_ev", "o_ps"))
        wo_ps, ye_free = sem("wo_ps"), sem("ye_free")
        gu_ps, silu_ready, act_mul, act_hi, act_ready, dn_ps, dn_ev = map(sem, (
            "gu_ps", "silu_ready", "act_mul", "act_hi", "act_ready", "dn_ps", "dn_ev"))
        lg_ps, msk_ready, pos_ps, gexp_in, gexp, tab_ready, scat_dma = map(sem, (
            "lg_ps", "msk_ready", "pos_ps", "gexp_in", "gexp", "tab_ready", "scat_dma"))
        xg_dma, xg_ps, xg_full, xg_hi, xg_ready = map(sem, ("xg_dma", "xg_ps", "xg_full", "xg_hi", "xg_ready"))
        e_ps, e_silu, e_mul, aT_ps, aT_hi, aT_ready, ye_ps, ye_ev, ye_dma, yg_dma, ym_ready = map(sem, (
            "e_ps", "e_silu", "e_mul", "aT_ps", "aT_hi", "aT_ready", "ye_ps", "ye_ev", "ye_dma", "yg_dma",
            "ym_ready"))

        wmod = a["w_mod"].rearrange("l (p k) n -> l p k n", k=KD)

        def src_of(u):
            kind, l, c, kh = u
            if kind == "mod":
                return wmod[l, :, 4 * kh:4 * kh + 4, 512 * c:512 * c + 512], 4, 512
            if kind == "win":
                c0, w = ((QKR + 512, 512), (QKR, 512), (0, QKR))[c]
                return a["w_in"][l, 512 * kh:512 * kh + 512, c0:c0 + w].rearrange("(k p) n -> p k n", p=P), 4, w
            if kind == "wo":
                return a["w_o"][l, 512 * kh:512 * kh + 512, 512 * c:512 * c + 512].rearrange(
                    "(k p) n -> p k n", p=P), 4, 512
            if kind in ("gate", "up"):
                return a[f"ffn_w_{kind}"][0, :, 256 * c:256 * c + 256].rearrange("(k p) n -> p k n", p=P), 8, 256
            n, f, step = l, c, kh
            return a["ffn_w_down"][0, P * f:P * (f + step), 512 * n:512 * n + 512].rearrange(
                "(k p) n -> p k n", p=P), step, 512

        def score(i):
            bank, c0 = SCORE_AT[i]
            return ps[:, bank, c0:c0 + P * (i + 1)]

        def xn_of(s):
            return xnf if s == 2 else xn

        def unit_size(j):
            return 4 * EW[j // 4][1] if j < 4 * len(EW) else min(2, NB - 2 * (j - 4 * len(EW))) * D

        def size_of(u):
            _, k, w = src_of(u)
            return k * w

        block = ctx.enter_context(nc.Block())

        @block.sync
        def _(eng):
            mods = weights = 0
            seen = []
            for r, u in enumerate(UNITS):
                if r >= RAWS:
                    kind, count = seen[r - RAWS]
                    eng.wait_ge(mod_read if kind == "mod" else lo_ready, count)
                src, k, w = src_of(u)
                eng.dma_start(raw[:, r % RAWS, 0:k * w].rearrange("p (k n) -> p k n", k=k), src).then_inc(
                    raw_full[r % RAWS], 16)
                if u[0] == "mod":
                    mods += 1
                    seen.append(("mod", mods))
                else:
                    weights += 1
                    seen.append(("w", weights))
                if r == 0:
                    eng.dma_start(x[:], a["x"][0].rearrange("(t p) d -> p t d", p=P)).then_inc(x_dma, 16)
            eng.wait_ge(lo_ready, SB)
            eng.wait_ge(lg_ps, 1)
            eng.wait_ge(tab_ready, 1)
            n = eng.value_load(eti[0:1, 0:1], min_val=8, max_val=MAXT - 1)

            def unit(i, e, j):
                eng.wait_ge(lo_ready, i * EU + (SB + j - MRAWS + 1))
                dst = mraw[:, j % MRAWS, :]
                if j < 4 * len(EW):
                    c0, w = EW[j // 4]
                    name = "moe_w_gate" if j % 4 < 2 else "moe_w_up"
                    kh = j % 2
                    src = a[name][0][bass.ds(e, 1), 512 * kh:512 * kh + 512, c0:c0 + w].rearrange(
                        "a (k p) n -> p (a k) n", p=P)
                    dst = dst[:, 0:4 * w].rearrange("p (k n) -> p k n", k=4)
                else:
                    f = 2 * (j - 4 * len(EW))
                    k = min(2, NB - f)
                    src = a["moe_w_down"][0][bass.ds(e, 1), P * f:P * (f + k), :].rearrange(
                        "a (k p) n -> p (a k) n", p=P)
                    dst = dst[:, 0:k * D].rearrange("p (k n) -> p k n", k=k)
                eng.dma_start(dst, src).then_inc(mraw_full[j % MRAWS], 16)

            with eng.Fori(0, n) as i:
                e = eng.value_load(eti[0:1, bass.ds(i + 1, 1)], min_val=0, max_val=E - 1)
                for j in range(EU):
                    unit(i, e, j)
            e = eng.value_load(eti[0:1, bass.ds(n + 1, 1)], min_val=0, max_val=E - 1)
            for j in range(2):
                unit(n, e, j)
            for t in range(T):
                eng.wait_ge(x_upd, 3 * T + t + 1)
                eng.dma_start(out[0, P * t:P * t + P, :], x[:, t, :]).then_inc(out_dma, 16)
            eng.wait_ge(out_dma, 16 * T)
            eng.wait_ge(mraw_full[1], 16)

        @block.gpsimd
        def _(eng):
            g = nc.gpsimd
            g.dma_start(cond[:, 0, :], a["c"][0].rearrange("(p k) -> p k", k=KD)).then_inc(c_dma, 16)
            g.dma_start(gp[:, 0, :], a["post_mix_g"][0:1, :].to_broadcast([P, D])).then_inc(post_dma, 16)
            g.dma_start(gp[:, 1, :], a["post_ffn_g"][0:1, :].to_broadcast([P, D])).then_inc(post_dma, 16)
            g.dma_start(gp[:, 2, :], a["post_ffn_g"][1:2, :].to_broadcast([P, D])).then_inc(post_dma, 16)
            g.memset(prow[:], 0.0).then_inc(zeros_ready, 1)
            eng.wait_ge(zeros_ready, 1)
            rows = [a["b_mod"].rearrange("l (k p) -> (l k) p", p=P)]
            rows += [a[n].rearrange("l (k p) -> (l k) p", p=P) for n in (
                "pre_mix_g", "pre_ffn_g", "q_norm_g", "kv_norm_g", "conv_b", "lru_ba", "lru_bx", "lru_lambda")]
            rows += [a["conv_w"].rearrange("l w (j p) -> (l w j) p", p=P), a["sgu_b"].rearrange("l g p -> (l g) p")]
            at_row = 0
            for n, src in enumerate(rows):
                k = src.shape[0]
                dst = prow[0:k, 0, :] if n == 0 else prow[at_row:at_row + k, 1, :]
                at_row += k if n else 0
                g.dma_start(dst, src).then_inc(par_dma, 16)
            assert at_row == 78
            for dst, src in (
                    (cs[:], a["cs_table"]), (trig[:], a["trig_table"]),
                    (router[:], a["moe_router"][0].rearrange("(k p) e -> p k e", p=P))):
                g.dma_start(dst, src).then_inc(par_dma, 16)

            g.memset(ident[:], 0.0).then_inc(zeros_ready, 1)
            g.memset(upper[:], 1.0).then_inc(zeros_ready, 1)
            g.memset(ones[:], 1.0)
            g.memset(eps[:, 0:1], 1e-6)
            g.memset(eps[:, 1:2], 1e-5)
            g.iota(iot[:], [[1, MAXT]], base=0, channel_multiplier=0, allow_small_or_imprecise_dtypes=True)
            eng.wait_ge(zeros_ready, 3)
            g.affine_select(out=ident[:], in_=ident[:], compare_op=ALU.not_equal, fill=1.0, base=0,
                            pattern=[[-1, P]], channel_multiplier=1)
            g.affine_select(out=upper[:], in_=upper[:], compare_op=ALU.is_gt, fill=0.0, base=0,
                            pattern=[[1, P]], channel_multiplier=-1).then_inc(const_ready, 1)

            def layer_params(l):
                if l:
                    eng.wait_ge(x_upd, 2 * T * l)
                loads = [
                    (lnrow[:, 0, :], a["sgu_ln_g"][l:l + 1, :].to_broadcast([P, SGU])),
                    (lnrow[:, 1, :], a["sgu_ln_b"][l:l + 1, :].to_broadcast([P, SGU])),
                    (sguw[:], a["sgu_w"][l].rearrange("g t s -> t g s")),
                    (wukv[:], a["w_ukv"][l].rearrange("p (h n) -> p h n", h=HEADS)),
                ]
                for k in range(2):
                    w = a["w_uq"][l, P * k:P * k + P, :].rearrange("p (h n) -> p h n", h=HEADS)
                    loads += [
                        (wuq[:, k, :, 0:NOPE + ROPE], w),
                        (wuq[:, k, :, NOPE + ROPE:NOPE + ROPE + HALF], w[:, :, NOPE + HALF:NOPE + ROPE]),
                        (wuq[:, k, :, NOPE + ROPE + HALF:P], w[:, :, NOPE:NOPE + HALF]),
                    ]
                for dst, src in loads:
                    g.dma_start(dst, src).then_inc(lpar_dma, 16)
                g.memset(bd[:], 0.0).then_inc(zeros2_ready, 1)
                eng.wait_ge(zeros2_ready, l + 1)
                for which, name in enumerate(("lru_wa", "lru_wx")):
                    for h in range(4):
                        o = 64 * (h % 2)
                        g.dma_start(bd[o:o + 64, which, h // 2, o:o + 64], a[name][l, h]).then_inc(bd_ready, 16)

            def sgu_mask(l):
                eng.wait_ge(sw_cp, l + 1)
                g.affine_select(out=sguw[:], in_=sguw[:], compare_op=ALU.is_ge, fill=0.0, base=0,
                                pattern=[[0, 4], [1, P]], channel_multiplier=-1).then_inc(sw_ready, 1)

            layer_params(0)
            sgu_mask(0)
            eng.wait_ge(x_upd, T)
            g.dma_start(gp[:, 0, :], a["post_mix_g"][1:2, :].to_broadcast([P, D])).then_inc(post_dma, 16)
            layer_params(1)
            sgu_mask(1)
            g.memset(gp[:, 1, :], 0.0).then_inc(zeros2_ready, 1)
            eng.wait_ge(zeros2_ready, L + 1)
            for i in range(MAXT):
                g.dma_start(scratch[P * i:P * i + P, :], gp[:, 1, :]).then_inc(zero_dma, 16)
            eng.wait_ge(tab_ready, 1)
            eng.wait_ge(xn_ready, 4 * T)
            eng.wait_ge(zero_dma, 16 * MAXT)
            for t in range(T):
                for k in range(2):
                    g.indirect_dma_start(out=scratch, out_offset=bass.IndirectOffsetOnAxis(
                        ap=sli[:, k, t:t + 1], axis=0), in_=xn[:, t, :], in_offset=None).then_inc(scat_dma, 16)
            eng.wait_ge(scat_dma, 16 * 2 * T)
            n = eng.value_load(eti[0:1, 0:1], min_val=8, max_val=MAXT - 1)
            eng.sem_inc(ye_free, 1)
            g.dma_start(xg[:], scratch[0:P, :]).then_inc(xg_dma, 16)
            with eng.Fori(0, n) as i:
                eng.wait_ge(xg_ps, i + 1)
                g.dma_start(xg[:], scratch[bass.ds((i + 1) * P, P), :]).then_inc(xg_dma, 16)
                eng.wait_ge(ye_ev, i + 1)
                g.dma_start(scratch[bass.ds(i * P, P), :], ye[:]).then_inc(ye_dma, 16)
                eng.wait_ge(xg_ready, i + 2)
                eng.wait_ge(lo_ready, i * EU + (SB + EU + 2))
                eng.wait_ge(ye_dma, i * 16 + 16)
                eng.sem_inc(ye_free, 1)
            for t in range(T):
                for k in range(2):
                    g.indirect_dma_start(out=yg[:, t, k, :], out_offset=None, in_=scratch,
                                         in_offset=bass.IndirectOffsetOnAxis(ap=sli[:, k, t:t + 1], axis=0)
                                         ).then_inc(yg_dma, 16)
                eng.wait_ge(yg_dma, 32 * (t + 1))
        @block.tensor
        def _(eng):
            mm = nc.tensor.matmul

            def mm3(o, lhs, rhs, start, stop):
                (lh, ll), (rh, rl) = lhs, rhs
                mm(o, lh, rh, start=start, stop=False)
                mm(o, lh, rl, start=False, stop=False)
                return mm(o, ll, rh, start=False, stop=stop)

            def unit_of(s, k, w):
                v = spl[:, s % SPLS, :, 0:k * w].rearrange("p h (k n) -> p h k n", k=k)
                return lambda kk, c0, n: (v[:, 0, kk, c0:c0 + n], v[:, 1, kk, c0:c0 + n])

            def hi_lo(t, k, c0, n):
                return t[:, 0, k, c0:c0 + n], t[:, 1, k, c0:c0 + n]

            def tr(o, i):
                return nc.tensor.transpose(o, i, ident[:])

            def mod(m, bank):
                c = m % MODC
                eng.wait_ge(mod_read, 2 * (m + 1))
                if m:
                    eng.wait_ge(mod_out, m)
                v = acc[:, m % 2, :]
                if c // 2 in (2, 5):
                    mm(ps[:, bank, :], ones[:], v, start=True, stop=True, skip_group_check=True)
                    for q in range(4):
                        b = bmod[:, m // MODC, 4 * c + q:4 * c + q + 1].to_broadcast([P, P])
                        last = mm(ps[:, bank, P * q:P * q + P], b, ident[:], start=False, stop=True,
                                  skip_group_check=True)
                else:
                    for q in range(4):
                        last = mm(ps[:, bank, q:q + 1], v[:, P * q:P * q + P], ones[:, 0:1], start=True, stop=True)
                last.then_inc(mod_ps, 1)

            def prenorm(s):
                if s:
                    eng.wait_ge(x_upd, T * s)
                for t in range(T):
                    eng.wait_ge(xn_ready, T * s + t + 1)
                    for k in range(KD):
                        last = tr(ps[:, k, P * t:P * t + P], xn_of(s)[:, t, P * k:P * k + P])
                        if t == T - 1:
                            last.then_inc(xT_ps, 1)

            def in_proj(l, part, kh):
                w, bank0, done = ((512, 0, zc_ps), (512, 4, zb_ps), (QKR, 0, za_ps))[part]
                s = W_IN[l] + 2 * part + kh
                u = unit_of(s, 4, w)
                eng.wait_ge(lo_ready, s + 1)
                if part == 0 and kh == 0:
                    eng.wait_ge(hT_ready, KD * 2 * l + 4)
                if part == 2 and kh == 0:
                    eng.wait_ge(gate_t, l + 1)
                for t in range(T):
                    if part == 1 and kh == 0 and t == 2:
                        eng.wait_ge(sw_cp, l + 1)
                    if part == 1 and kh == 0 and t == 3 and l == 0:
                        eng.wait_ge(mod_out, 6)
                    for kk in range(4):
                        k = 4 * kh + kk
                        if part == 0 and kh == 1 and t == 0:
                            eng.wait_ge(hT_ready, KD * 2 * l + k + 1)
                        o = ps[:, bank0 + t, 0:w]
                        if part:
                            last = mm3(o, hi_lo(hT, k, P * t, P), u(kk, 0, w), k == 0, k == 7)
                        else:
                            last = mm3(o, u(kk, P * t, P), hi_lo(hT, k, 0, S), k == 0, k == 7)
                    if kh and t < 3:
                        last.then_inc(done, 1)
                last.then_inc(w_used, 1)

            def projections(l):
                for kh in range(2):
                    in_proj(l, 0, kh)
                    if l == 0:
                        eng.wait_ge(hT_ready, KD)
                        mod(4 + kh, 7)
                eng.wait_ge(lpar_dma, 16 * 10 * (l + 1))
                for g in range(4):
                    last = tr(ps[:, 6, P * g:P * g + P], sguw[:, g, :])
                last.then_inc(sw_ps, 1)
                in_proj(l, 1, 0)
                eng.wait_ge(bd_ready, 16 * 8 * (l + 1))
                eng.wait_ge(zy_ready, 2 * (l + 1))
                eng.wait_ge(xc_ready, l + 1)
                for which in range(2):
                    for j in range(2):
                        last = mm(ps[:, 2 * which + j, :], bd[:, which, j, :], lt[:, 0, j, :], start=True, stop=True)
                last.then_inc(gate_ps, 1)
                in_proj(l, 1, 1)
                in_proj(l, 2, 0)
                eng.wait_ge(zuv_ready, T * (l + 1))
                if l == 0:
                    mod(6, 7)
                eng.wait_ge(vn_ready, l + 1)
                eng.wait_ge(sw_ready, l + 1)
                for g in range(4):
                    o = ps[:, 5 + g // 2, 256 * (g % 2):256 * (g % 2) + 256].rearrange("p (t c) -> p t c", t=T)
                    last = mm(o, sguw[:, g, :], zuv[:, :, SGU + 64 * g:SGU + 64 * g + 64], start=True, stop=True)
                last.then_inc(mix_ps, 1)
                in_proj(l, 2, 1)
                eng.wait_ge(ysg_ready, l + 1)
                eng.wait_ge(zq_cp, T * l + 3)
                for j in range(2):
                    for t in range(T):
                        last = tr(ps[:, 1 + j, P * t:P * t + P], zuv[:, t, P * j:P * j + P])
                    last.then_inc(ysT_ps, 1)

            def latents(l):
                eng.wait_ge(zq_cp, T * (l + 1))
                for t in range(T):
                    eng.wait_ge(zqn_ready, T * l + t + 1)
                    for j in range(3):
                        tr(ps[:, (5, 6, 0)[j], P * t:P * t + P], zq[:, t, P * j:P * j + P])
                eng.wait_ge(kr_ready, l + 1)
                for t in range(T):
                    last = tr(ps[0:64, 3, P * t:P * t + P], krd[:, t].rearrange("p a b -> p (a b)"))
                last.then_inc(qkT_ps, 1)
                eng.wait_ge(att_in, l + 1)
                eng.wait_ge(q_in, l + 1)
                if l == 0:
                    eng.wait_ge(mod_out, 7)
                for t in range(T):
                    last = mm(ps[:, 4 + t, :].rearrange("p (h c) -> p h c", h=HEADS), qT[:, 2, P * t:P * t + P],
                              wukv[:, :, NOPE:NOPE + VD], start=True, stop=True)
                last.then_inc(v_ps, 1)

            def queries(l, h):
                n = HEADS * l + h
                if n:
                    eng.wait_ge(q_ev, n)
                if l == 0 and h in (5, 7):
                    eng.wait_ge(mod_out, 5 + h // 2 + 1)
                for k in range(2):
                    last = mm(ps[:, 0, :], wuq[:, k, h, :], qT[:, k, :], start=(k == 0), stop=(k == 1))
                last.then_inc(q_ps, 1)

            def keys(l, h):
                n = HEADS * l + h
                if n:
                    eng.wait_ge(k_ev, n)
                if h == 0:
                    eng.wait_ge(yT_ready, 8 * l + 1)
                mm(ps[0:NOPE, 1, :], wukv[:, h, 0:NOPE], qT[:, 2, :], start=True, stop=True).then_inc(k_ps, 1)

            def scores(l, h):
                n = HEADS * l + h
                eng.wait_ge(q_ev, n + 1)
                eng.wait_ge(k_ev, n + 1)
                if h == 0:
                    eng.wait_ge(v_ready, l + 1)
                    eng.wait_ge(v2_ready, l + 1)
                else:
                    eng.wait_ge(exp_ready, T * n)
                for i in SCORE_ORDER:
                    mm(score(i), qb[:, h % 2, P * i:P * (i + 1)], kb[:, h % 2, 0:P * (i + 1)], start=True,
                       stop=True).then_inc(s_ps, 1)

            def turn(l, h, i):
                n = HEADS * l + h
                eng.wait_ge(pn_ready, T * n + i + 1)
                if T * n + i >= 2:
                    eng.wait_ge(pt_ev, T * n + i - 1)
                for j in range(i + 1):
                    last = tr(ps[:, TURN_BANK[i % 2], P * j:P * j + P], pr[:, i, P * j:P * j + P])
                last.then_inc(pt_ps, 1)

            def values(l, h):
                n = HEADS * l + h
                eng.wait_ge(pt_ev, T * (n + 1))
                if h % 2 == 0:
                    eng.wait_ge(yT_ready, 8 * l + 4 + h // 2)
                o = 64 * (h % 2)
                for j in range(T):
                    last = mm(ps[o:o + 64, 2, P * j:S], vb[:, j, VD * h:VD * h + VD], pT[:, j, P * j:S],
                              start=(j == 0), stop=True, skip_group_check=True)
                last.then_inc(o_ps, 1)

            def attention(l):
                for h in range(2):
                    queries(l, h)
                    keys(l, h)
                scores(l, 0)
                for h in range(HEADS):
                    if h + 1 < HEADS:
                        scores(l, h + 1)
                    turn(l, h, 0)
                    turn(l, h, 1)
                    if h + 2 < HEADS:
                        queries(l, h + 2)
                    turn(l, h, 2)
                    turn(l, h, 3)
                    if h + 2 < HEADS:
                        keys(l, h + 2)
                    values(l, h)
                    if l == 0 and h in (2, 4, 6):
                        eng.wait_ge(q_ev, min(h + 3, HEADS))
                        mod(6 + h // 2, 0)

            def out_proj(l):
                for n in range(2):
                    for i, kh in enumerate((1, 0)):
                        s = W_O[l] + 2 * n + i
                        u = unit_of(s, 4, 512)
                        if n == 0 and i == 0:
                            eng.wait_ge(yT_ready, 8 * (l + 1))
                            eng.wait_ge(pt_ev, T * HEADS * (l + 1))
                            if l == 0:
                                eng.wait_ge(mod_out, 10)
                        eng.wait_ge(lo_ready, s + 1)
                        for t in range(T):
                            for kk in range(4):
                                last = mm3(ps[:, 2 * t + n, :], hi_lo(yT, 4 * kh + kk, P * t, P), u(kk, 0, 512),
                                           i == 0 and kk == 0, i == 1 and kk == 3)
                            if t < 3 and i == 1:
                                last.then_inc(wo_ps, 1)
                        last.then_inc(w_used, 1)

            def dense():
                s, m, downs = W_FF, 10, 0
                for g, blocks in enumerate(GROUPS):
                    for c in range(blocks[0] // 2, blocks[-1] // 2 + 1):
                        units = [unit_of(s + i, KD, 256) for i in range(2)]
                        for b in range(2):
                            f = 2 * c + b
                            if f >= 2:
                                eng.wait_ge(act_mul, f - 1)
                            if b == 0 and 2 * c == blocks[0] and g:
                                eng.wait_ge(mod_out, m)
                            for i in range(2):
                                if b == 0:
                                    eng.wait_ge(lo_ready, s + i + 1)
                                for k in range(KD):
                                    if f == 0 and i == 0:
                                        eng.wait_ge(hT_ready, KD + k + 1)
                                    last = mm3(ps[:, 2 * b + i, :], units[i](k, P * b, P), hi_lo(hT, k, 0, S),
                                               k == 0, k == KD - 1)
                                if b == 1:
                                    last.then_inc(w_used, 1)
                                elif i == 1:
                                    last.then_inc(gu_ps, 1)
                            if b == 0 and 2 * c > blocks[0]:
                                if g:
                                    eng.wait_ge(dn_ev, 8 * g)
                                mod(m, 4)
                                m += 1
                        s += 2
                    eng.wait_ge(mod_out, m)
                    step = 3 if len(blocks) == 6 else 4
                    if g == 3:
                        break
                    for n in range(2):
                        for f0 in range(blocks[0], blocks[-1] + 1, step):
                            u = unit_of(s, step, 512)
                            eng.wait_ge(lo_ready, s + 1)
                            for t in range(T):
                                if downs and f0 == blocks[0]:
                                    eng.wait_ge(dn_ev, 4 * (downs - 1) + t + 1)
                                for i in range(step):
                                    f = f0 + i
                                    if t == 0 and n == 0:
                                        eng.wait_ge(act_ready, f + 1)
                                    last = mm3(ps[:, 4 + t, :], hi_lo(act, f - blocks[0], P * t, P), u(i, 0, 512),
                                               f == blocks[0], f == blocks[-1])
                                if t < 3 and f0 + step > blocks[-1]:
                                    last.then_inc(dn_ps, 1)
                            last.then_inc(w_used, 1)
                            s += 1
                            if f0 == blocks[0]:
                                if n == 0:
                                    eng.wait_ge(act_mul, blocks[-1])
                                mod(m, 0)
                                m += 1
                        downs += 1
                eng.wait_ge(act_mul, FF // P)
                eng.wait_ge(dn_ev, 4 * downs)
                for t in range(T):
                    for n in range(2):
                        u = unit_of(s + n, step, 512)
                        if t == 0:
                            eng.wait_ge(lo_ready, s + n + 1)
                        for i in range(step):
                            if t == 0 and n == 0:
                                eng.wait_ge(act_ready, blocks[i] + 1)
                            last = mm3(ps[:, 2 * t + n, :], hi_lo(act, i, P * t, P), u(i, 0, 512),
                                       i == 0, i == step - 1)
                        if t == 3:
                            last.then_inc(w_used, 1)
                        elif n == 1:
                            last.then_inc(dn_ps, 1)
                eng.wait_ge(dn_ev, 4 * downs + 1)
                mod(m, 0)

            def route():
                eng.wait_ge(par_dma, 16 * 14)
                eng.wait_ge(hT_ready, KD * 4)
                for t in range(T):
                    for k in range(KD):
                        last = mm(ps[:, 0, E * t:E * t + E], hTf[:, k, P * t:P * t + P], router[:, k, :],
                                  start=(k == 0), stop=(k == KD - 1))
                last.then_inc(lg_ps, 1)
                eng.wait_ge(msk_ready, 1)
                for t in range(T):
                    for i in range(t + 1):
                        mm(ps[:, 1, E * t:E * t + E], upper[:] if i == t else ones[:], msk[:, i, :],
                           start=(i == 0), stop=(i == t))
                for t in range(T):
                    last = mm(ps[:, 2, 0:E], ones[:], msk[:, t, :], start=(t == 0), stop=(t == T - 1))
                last.then_inc(pos_ps, 1)

            def turn_rows(count):
                eng.wait_ge(xg_dma, count * 16)
                for k in range(KD):
                    last = tr(ps[:, 2 + k // 4, P * (k % 4):P * (k % 4) + P], xg[:, P * k:P * k + P])
                last.then_inc(xg_ps, 1)

            def experts():
                eng.wait_ge(tab_ready, 1)
                n = eng.value_load(eti[0:1, 0:1], min_val=8, max_val=MAXT - 1)
                turn_rows(1)
                with eng.Fori(0, n) as i:
                    def unit(j, k, w):
                        eng.wait_ge(lo_ready, i * EU + (SB + j + 1))
                        return unit_of(SB + j, k, w)

                    def turn_act(c):
                        eng.wait_ge(e_mul, i * 3 + (c + 1))
                        if c == 2:
                            eng.wait_ge(aT_ready, i * 3 + 1)
                        for q in range(EW[c][1] // P):
                            last = tr(ps[:, 6 + c % 2, P * q:P * q + P],
                                      acte[:, EW[c][0] + P * q:EW[c][0] + P * q + P])
                        last.then_inc(aT_ps, 1)

                    eng.wait_ge(xg_ready, i + 1)
                    for c, (c0, w) in enumerate(EW):
                        if c == 2:
                            eng.wait_ge(e_mul, i * 3 + 1)
                        for part in range(2):
                            for kh in range(2):
                                u = unit(4 * c + 2 * part + kh, 4, w)
                                for kk in range(4):
                                    k = 4 * kh + kk
                                    last = mm3(ps[:, 2 * (c % 2) + part, 0:w], hi_lo(xgT, k, 0, P), u(kk, 0, w),
                                               k == 0, k == KD - 1)
                                last.then_inc(w_used, 1)
                        if c:
                            turn_act(c - 1)
                    turn_rows(i + 2)
                    turn_act(2)
                    for j in range(4 * len(EW), EU):
                        f0 = 2 * (j - 4 * len(EW))
                        step = min(2, NB - f0)
                        u = unit(j, step, D)
                        eng.wait_ge(aT_ready, i * 3 + (min(f0 + step - 1, NB - 1) // 4 + 1))
                        for b in range(step):
                            for h in range(2):
                                last = mm3(ps[:, 4 + h, :], hi_lo(aT, f0 + b, 0, P), u(b, 512 * h, 512),
                                           f0 + b == 0, f0 + b == NB - 1)
                        last.then_inc(w_used, 1)

            eng.wait_ge(const_ready, 1)
            eng.wait_ge(par_dma, 16 * 14)
            for i in range(2):
                last = tr(ps[0:P, 0, P * i:P * i + P], prow[:, i, :])
            last.then_inc(col_ps, 1)
            eng.wait_ge(col_ready, 1)
            for m in range(4):
                mod(m, 3)
            for l in range(L):
                eng.wait_ge(mod_out, 4 if l == 0 else L * MODC)
                prenorm(2 * l)
                projections(l)
                latents(l)
                attention(l)
                out_proj(l)
                prenorm(2 * l + 1)
                if l == 0:
                    dense()
                else:
                    route()
                    experts()

        @block.scalar
        def _(eng):
            A = nc.scalar.activation
            chain = [0]

            def link(ins):
                chain[0] += 1
                ins.then_inc(act_chain, 1)
                eng.wait_ge(act_chain, chain[0])

            def hi(s):
                r = WEIGHTS[s]
                n = size_of(UNITS[r])
                eng.wait_ge(raw_full[r % RAWS], 16 * (r // RAWS + 1))
                if s >= SPLS:
                    eng.wait_ge(w_used, s - SPLS + 1)
                A(spl[:, s % SPLS, 0, 0:n], raw[:, r % RAWS, 0:n], ACT.Copy).then_inc(hi_ready, 1)

            def root(out_, in_, scale, e):
                return A(out_, in_, ACT.Sqrt, scale=scale, bias=eps[:, e:e + 1])

            def post_stat(s, t, y, junk):
                link(A(junk, y, ACT.Square, accum_out=ss[:, t:t + 1]))
                root(rms[:, t:t + 1], ss[:, t:t + 1], 1.0 / D, 0).then_inc(pss, 1)

            def pre_stat(s, t):
                if s:
                    eng.wait_ge(x_upd, T * (s - 1) + t + 1)
                elif t == 0:
                    eng.wait_ge(x_dma, 16)
                link(A(xn_of(s)[:, t, :], x[:, t, :], ACT.Square, accum_out=ss[:, t:t + 1]))
                root(rms[:, t:t + 1], ss[:, t:t + 1], 1.0 / D, 0).then_inc(rms_ready, 1)

            def update(s, tile):
                for t in range(T):
                    tile(t)
                    if t:
                        pre_stat(s + 1, t - 1)
                pre_stat(s + 1, T - 1)

            def prenorm(s):
                c = modn if s >= 2 else modc
                b = 2 * (s % 2)
                for q in range(KD):
                    eng.wait_ge(xT_ps, KD * (s + 1) if s == 2 else KD * s + q + 1)
                    if q == 0:
                        eng.wait_ge(mod_out, MODC * (s // 2) + (4 if s % 2 == 0 else 10))
                    A(hT[:, 0, q, :], ps[:, q, :], ACT.Identity, scale=c[:, b + 1, q:q + 1],
                      bias=c[:, b, q:q + 1]).then_inc(hT_hi, 1)

            def tile_hi(k, bank):
                A(yT[:, 0, k, :], ps[:, bank, :], ACT.Copy).then_inc(yT_hi, 1)

            def mixer(l):
                w0 = W_IN[l]
                for s in range(w0 + 2, w0 + 5):
                    hi(s)
                for j in (2, 3):
                    eng.wait_ge(*((zc_ps, 3 * l + j + 1) if j < 3 else (w_used, w0 + 2)))
                    A(zxy[:, j, :], ps[:, j, :], ACT.Gelu_apprx_tanh).then_inc(zy_ready, 1)
                hi(w0 + 5)
                eng.wait_ge(gate_ps, l + 1)
                for which in range(2):
                    for j in range(2):
                        last = A(lt[:, 1 + which, j, :], ps[:, 2 * which + j, :], ACT.Tanh, scale=0.5,
                                 bias=hb[:, which, l, j:j + 1])
                last.then_inc(gate_t, 1)
                eng.wait_ge(la_ready, l + 1)
                lf = lt[:].rearrange("p a j s -> p a (j s)")
                A(lf[:, 3], lf[:, 1], ACT.Exp)
                A(lf[:, 1], lf[:, 1], ACT.Tanh).then_inc(ea_ready, 1)
                for t in range(T):
                    eng.wait_ge(*((zb_ps, 3 * l + t + 1) if t < 3 else (w_used, w0 + 4)))
                    A(zuv[:, t, :], ps[:, 4 + t, :], ACT.Gelu_apprx_tanh).then_inc(zuv_ready, 1)
                eng.wait_ge(lq_ready, l + 1)
                q = zxy[:, 0:2, :]
                A(q, q, ACT.Sqrt, scale=-0.25).then_inc(lsq_ready, 1)
                eng.wait_ge(bn_done, l + 1)
                A(sd[:, 0, :], mv[:, :, 1], ACT.Sqrt, bias=eps[:, 1:2]).then_inc(sd_ready, 1)
                junk = lt[:, 1, 0, :]
                for t in range(T):
                    eng.wait_ge(zq_cp, T * l + t + 1)
                    A(junk[:, 0:QL], zq[:, t, 0:QL], ACT.Square, accum_out=st8[:, 0, t:t + 1])
                    link(A(junk[:, QL:QL + KVL], zq[:, t, QL:QL + KVL], ACT.Square, accum_out=st8[:, 0, 4 + t:5 + t]))
                    root(st8[:, 1, t:t + 1], st8[:, 0, t:t + 1], 1.0 / QL, 0)
                    root(st8[:, 1, 4 + t:5 + t], st8[:, 0, 4 + t:5 + t], 1.0 / KVL, 0).then_inc(qs_ready, 1)
                eng.wait_ge(ylru, l + 1)
                eng.wait_ge(qkT_ps, l + 1)
                for b in range(2):
                    A(kb[64:128, b, :], ps[0:64, 3, :], ACT.Copy)
                A(qT[:, 2, :], ps[:, 0, :], ACT.Copy, scale=kvg[:, l:l + 1]).then_inc(att_in, 1)
                eng.wait_ge(w_used, w0 + 6)
                for j in range(2):
                    eng.wait_ge(ysT_ps, 2 * l + j + 1)
                    tile_hi(4 + j, 1 + j)
                for j in range(2):
                    A(yT[:, 0, 6 + j, :], zxy[:, 2 + j, :], ACT.Copy).then_inc(yT_hi, 1)
                eng.wait_ge(v_ps, l + 1)
                A(vb[:, 0:2], ps[:, 4:6, :], ACT.Copy).then_inc(v_ready, 1)

                def keys(h):
                    n = HEADS * l + h
                    eng.wait_ge(k_ps, n + 1)
                    if h >= 2:
                        eng.wait_ge(s_ps, T * (n - 1))
                    A(kb[0:NOPE, h % 2, :], ps[0:NOPE, 1, :], ACT.Copy).then_inc(k_ev, 1)

                def weights(h, i):
                    n = HEADS * l + h
                    eng.wait_ge(nm_ready, n + 1)
                    if h:
                        eng.wait_ge(pt_ps, T * (n - 1) + i + 1)
                    A(pr[:, i, 0:P * (i + 1)], score(i), ACT.Exp, scale=SCALE, bias=am[:, 1, h % 4, i:i + 1],
                      accum_out=st8[:, 2, 4 * (h % 2) + i:4 * (h % 2) + i + 1]).then_inc(exp_ready, 1)

                def turned(h, i):
                    n = HEADS * l + h
                    if h:
                        eng.wait_ge(o_ps, n)
                    eng.wait_ge(pt_ps, T * n + i + 1)
                    w = P * (i + 1)
                    A(pT[:, 0:i + 1, P * i:w], ps[:, TURN_BANK[i % 2], 0:w].rearrange("p (j q) -> p j q", j=i + 1),
                      ACT.Copy).then_inc(pt_ev, 1)

                keys(0)
                keys(1)
                for i in range(T):
                    weights(0, i)
                eng.wait_ge(yT_ready, 8 * l + 4)
                for h in range(HEADS):
                    if h and h % 2 == 0:
                        eng.wait_ge(o_ps, HEADS * l + h)
                        tile_hi(h // 2 - 1, 2)
                    for i in range(T):
                        turned(h, i)
                    if h + 1 < HEADS:
                        for i in range(T):
                            weights(h + 1, i)
                    if h + 2 < HEADS:
                        keys(h + 2)
                    if h >= HEADS - 3:
                        hi(W_O[l] + h - (HEADS - 3))
                eng.wait_ge(o_ps, HEADS * (l + 1))
                tile_hi(3, 2)
                hi(W_O[l] + 3)
                if l == 0:
                    for i in range(2):
                        hi(W_FF + i)

                def tile(t):
                    eng.wait_ge(*((wo_ps, 6 * l + 4 + t) if t < 3 else (w_used, W_O[l] + 4)))
                    post_stat(2 * l, t, ps[:, 2 * t:2 * t + 2, :], xn[:, t, :].rearrange("p (n c) -> p n c", n=2))

                update(2 * l, tile)

            def dense():
                s, f = W_FF, 0

                def evict(w_end):
                    eng.wait_ge(*w_end)
                    if f >= 2:
                        eng.wait_ge(act_mul, f - 1)
                    A(sgf[:, f % 2, :], ps[:, 2 * (f % 2), :], ACT.Silu).then_inc(silu_ready, 1)
                    eng.wait_ge(act_mul, f + 1)
                    A(act[:, 0, f % 6, :], actf[:, f % 2, :], ACT.Copy).then_inc(act_hi, 1)

                for g, blocks in enumerate(GROUPS):
                    for c in range(blocks[0] // 2, blocks[-1] // 2 + 1):
                        hi(s + 2)
                        evict((gu_ps, c + 1))
                        f += 1
                        hi(s + 3)
                        evict((w_used, s + 2))
                        f += 1
                        s += 2
                    for i in range(4 if g < 3 else 1):
                        hi(s + 2)
                        s += 1

                def tile(t):
                    eng.wait_ge(dn_ev, 24 + t + 1)
                    post_stat(1, t, yf[:, t, :], xnf[:, t, :])

                update(1, tile)
                hi(s + 2)

            def experts():
                eng.wait_ge(gexp_in, 1)
                A(ge[:, 0, :], ge[:, 0, :], ACT.Exp).then_inc(gexp, 1)
                eng.wait_ge(tab_ready, 1)
                n = eng.value_load(eti[0:1, 0:1], min_val=8, max_val=MAXT - 1)

                def part(i, j):
                    eng.wait_ge(mraw_full[j % MRAWS], i * (16 * EU // MRAWS) + 16 * (j // MRAWS + 1))
                    eng.wait_ge(w_used, i * EU + (SB + j - SPLS + 1))
                    w = unit_size(j % EU)
                    A(spl[:, (SB + j) % SPLS, 0, 0:w], mraw[:, j % MRAWS, 0:w], ACT.Copy).then_inc(hi_ready, 1)

                def rows(count):
                    eng.wait_ge(xg_full, count)
                    A(xgT[:, 0], xfull[:], ACT.Copy).then_inc(xg_hi, 1)

                part(0, 0)
                part(0, 1)
                rows(1)
                with eng.Fori(0, n) as i:
                    def silu(c):
                        eng.wait_ge(w_used, i * EU + (SB + 4 * c + 2))
                        w = EW[c][1]
                        eng.wait_ge(e_mul, i * 3 + c) if c else None
                        A(sge[:, 0:w], ps[:, 2 * (c % 2), 0:w], ACT.Silu).then_inc(e_silu, 1)

                    def turned(c):
                        eng.wait_ge(aT_ps, i * 3 + (c + 1))
                        w = EW[c][1]
                        A(aT[:, 0, 4 * c:4 * c + w // P, :].rearrange("p f q -> p (f q)"), ps[:, 6 + c % 2, 0:w],
                          ACT.Copy).then_inc(aT_hi, 1)

                    for j in range(2, 6):
                        part(i, j)
                        if j == 4:
                            silu(0)
                    for j in range(6, 10):
                        part(i, j)
                        if j == 8:
                            silu(1)
                    turned_at = {11: 0}
                    for j in range(10, 14):
                        part(i, j)
                        if j in turned_at:
                            turned(0)
                        if j == 12:
                            silu(2)
                    turned(1)
                    rows(i + 2)
                    turned(2)
                    for j in range(14, 20):
                        part(i, j)
                    eng.wait_ge(w_used, i * EU + (SB + EU))
                    eng.wait_ge(ye_free, i + 1)
                    A(ye[:].rearrange("p (h c) -> p h c", h=2), ps[:, 4:6, :], ACT.Copy).then_inc(ye_ev, 1)
                for t in range(T):
                    eng.wait_ge(ym_ready, t + 1)
                    post_stat(3, t, ym[:, t, :], yg[:, t, 0, :])

            eng.wait_ge(c_dma, 16)
            A(cond[:, 1, :], cond[:, 0, :], ACT.Silu).then_inc(cond_ready, 1)
            eng.wait_ge(const_ready, 1)
            eng.wait_ge(col_ps, 1)
            A(colp[:], ps[:, 0, 0:2 * P].rearrange("p (a b) -> p a b", a=2)[:, :, 0:96], ACT.Copy).then_inc(col_ready, 1)
            eng.wait_ge(col_ready, 1)
            link(A(sp[:, 0], lcol[:, 3], ACT.Abs))
            A(sp[:, 0], sp[:, 0], ACT.Exp, scale=-1.0).then_inc(sp_a, 1)
            eng.wait_ge(sp_b, 1)
            A(sp[:, 2], sp[:, 1], ACT.Ln).then_inc(sp_c, 1)
            for t in range(T):
                pre_stat(0, t)
            for i in range(2):
                hi(i)
            for l in range(L):
                prenorm(2 * l)
                mixer(l)
                if l == 0:
                    prenorm(1)
                    dense()
                else:
                    experts()

        @block.vector
        def _(eng):
            V = nc.vector
            chain = [0]

            def link(ins):
                chain[0] += 1
                ins.then_inc(dve_chain, 1)
                eng.wait_ge(dve_chain, chain[0])

            def after(ins, s, v):
                ins.then_inc(s, 1)
                eng.wait_ge(s, v)

            def lo(s):
                r = WEIGHTS[s]
                n = size_of(UNITS[r])
                eng.wait_ge(hi_ready, s + 1)
                V.tensor_tensor(spl[:, s % SPLS, 1, 0:n], raw[:, r % RAWS, 0:n],
                                spl[:, s % SPLS, 0, 0:n].bitcast(F32), ALU.subtract).then_inc(lo_ready, 1)

            def mod_half(m, kh):
                v = acc[:, m % 2, :]
                if m >= 2 and kh == 0:
                    eng.wait_ge(mod_ps, m - 1)
                r = MODS[2 * m + kh]
                eng.wait_ge(raw_full[r % RAWS], 16 * (r // RAWS + 1))
                for kk in range(4):
                    w = raw[:, r % RAWS, 512 * kk:512 * kk + 512]
                    c = cond[:, 1, 4 * kh + kk:4 * kh + kk + 1]
                    if kh + kk == 0:
                        ins = V.tensor_scalar(v, w, c, None, ALU.mult)
                    else:
                        ins = V.scalar_tensor_tensor(out=v, in0=w, scalar=c, in1=v, op0=ALU.mult, op1=ALU.add)
                    if kk < 3:
                        link(ins)
                    else:
                        after(ins, mod_read, 2 * m + kh + 1)

            def mod_sum(m):
                for kh in range(2):
                    mod_half(m, kh)

            def mod_evict(m, bank):
                l, c = divmod(m, MODC)
                kind, half = divmod(c, 2)
                eng.wait_ge(mod_ps, m + 1)
                if kind in (2, 5):
                    slot = 0 if kind == 2 else 1 + l
                    eng.wait_ge(post_dma, 64 if l and kind == 2 else 48)
                    g = gp[:, slot, 512 * half:512 * half + 512]
                    V.tensor_tensor(g, ps[:, bank, :], g, ALU.mult).then_inc(mod_out, 1)
                else:
                    k = slice(4 * half, 4 * half + 4)
                    dst = (modn if l else modc)[:, {0: 0, 1: 1, 3: 2, 4: 3}[kind], k]
                    ins = V.tensor_tensor(dst, ps[:, bank, 0:4], bmod[:, l, 4 * c:4 * c + 4], ALU.add)
                    if kind in (1, 4):
                        link(ins)
                        ins = V.scalar_tensor_tensor(out=dst, in0=dst, scalar=1.0, in1=gpre[:, kind // 4, l, k],
                                                     op0=ALU.add, op1=ALU.mult)
                    after(ins, mod_out, m + 1)

            def pre_tile(s, t):
                eng.wait_ge(rms_ready, T * s + t + 1)
                link(V.reciprocal(rinv[:, t:t + 1], rms[:, t:t + 1]))
                V.tensor_scalar(xn_of(s)[:, t, :], x[:, t, :], rinv[:, t:t + 1], None, ALU.mult).then_inc(
                    xn_ready, 1)

            def post_tile(s, t, y, slot, tmp):
                eng.wait_ge(pss, T * s + t + 1)
                link(V.reciprocal(rinv[:, t:t + 1], rms[:, t:t + 1]))
                link(V.scalar_tensor_tensor(out=tmp[:, t % 2, :].rearrange("p (n c) -> p n c", n=2), in0=y,
                                            scalar=rinv[:, t:t + 1],
                                            in1=gp[:, slot, :].rearrange("p (n c) -> p n c", n=2),
                                            op0=ALU.mult, op1=ALU.mult))
                V.tensor_tensor(x[:, t, :], x[:, t, :], tmp[:, t % 2, :], ALU.add).then_inc(x_upd, 1)

            def prenorm(s):
                c = modn if s >= 2 else modc
                b = 2 * (s % 2)
                for q in range(KD):
                    eng.wait_ge(*((xT_ps, KD * s + q + 1) if s == 3 else (hT_hi, KD * s + q + 1)))
                    o = hTf[:, q, :] if s == 3 else full[:, q % 2, :]
                    ins = V.tensor_scalar(o, ps[:, q, :], c[:, b + 1, q:q + 1], c[:, b, q:q + 1], ALU.mult, ALU.add)
                    if s == 3:
                        ins.then_inc(hT_ready, 1)
                        continue
                    link(ins)
                    V.tensor_tensor(hT[:, 1, q, :], o, hT[:, 0, q, :].bitcast(F32), ALU.subtract).then_inc(hT_ready, 1)

            def tile_lo(l, i, k, src):
                eng.wait_ge(yT_hi, 8 * l + i + 1)
                V.tensor_tensor(yT[:, 1, k, :], src, yT[:, 0, k, :].bitcast(F32), ALU.subtract).then_inc(yT_ready, 1)

            def mixer(l):
                w0 = W_IN[l]
                if l == 0:
                    mod_sum(4)
                    mod_sum(5)
                lo(w0 + 2)
                if l == 0:
                    mod_evict(4, 7)
                    mod_sum(6)
                lo(w0 + 3)
                for j in range(2):
                    eng.wait_ge(zc_ps, 3 * l + j + 1)
                    V.tensor_copy(zxy[:, j, :], ps[:, j, :]).then_inc(zx_cp, 1)
                eng.wait_ge(zx_cp, 2 * (l + 1))
                for j in range(2):
                    ins = V.tensor_scalar(lt[:, 0, j, :], zxy[:, j, :], cw[:, l, 3, j:j + 1], lcol[:, 0, l, j:j + 1],
                                          ALU.mult, ALU.add)
                link(ins)
                for tap in range(3):
                    sh = 3 - tap
                    for j in range(2):
                        ins = V.scalar_tensor_tensor(out=lt[:, 0, j, sh:], in0=zxy[:, j, 0:S - sh],
                                                     scalar=cw[:, l, tap, j:j + 1], in1=lt[:, 0, j, sh:],
                                                     op0=ALU.mult, op1=ALU.add)
                    if tap == 2:
                        after(ins, xc_ready, l + 1)
                    else:
                        link(ins)
                if l == 0:
                    mod_evict(5, 7)
                eng.wait_ge(sw_ps, l + 1)
                V.tensor_copy(sguw[:], ps[:, 6, :].rearrange("p (g t) -> p g t", g=4)).then_inc(sw_cp, 1)
                lo(w0 + 4)
                eng.wait_ge(gate_t, l + 1)
                for j in range(2):
                    ins = V.tensor_scalar(lt[:, 1, j, :], lt[:, 1, j, :], 1.0, nsp[:, l, j:j + 1], ALU.add, ALU.mult)
                after(ins, la_ready, l + 1)
                link(V.scalar_tensor_tensor(out=lt[:, 2], in0=lt[:, 2], scalar=1.0, in1=lt[:, 0],
                                            op0=ALU.add, op1=ALU.mult))
                lo(w0 + 5)
                eng.wait_ge(ea_ready, l + 1)
                q = zxy[:, 0:2, :]
                link(V.tensor_tensor(q, lt[:, 3], lt[:, 3], ALU.mult))
                after(V.scalar_tensor_tensor(out=q, in0=q, scalar=1.0, in1=lt[:, 1], op0=ALU.add, op1=ALU.mult),
                      lq_ready, l + 1)
                for t in range(T):
                    eng.wait_ge(zuv_ready, T * l + t + 1)
                    link(V.bn_stats(bn[:, t, :], zuv[:, t, SGU:2 * SGU]))
                    ins = V.bn_aggr(mv[:, t, :], bn[:, t, :])
                after(ins, bn_done, l + 1)
                eng.wait_ge(lsq_ready, l + 1)
                link(V.tensor_tensor(lt[:, 2], lt[:, 2], q, ALU.mult))
                for j in range(2):
                    ins = V.tensor_tensor_scan(lt[:, 0, j, :], lt[:, 3, j, :], lt[:, 2, j, :], 0.0, ALU.mult, ALU.add)
                eng.wait_ge(sd_ready, l + 1)
                link(V.reciprocal(sd[:, 1, :], sd[:, 0, :]))
                v = zuv[:, :, SGU:2 * SGU]
                for t in range(T):
                    ins = V.tensor_scalar(v[:, t, :], v[:, t, :], mv[:, t, 0:1], sd[:, 1, t:t + 1],
                                          ALU.subtract, ALU.mult)
                link(ins)
                for i, op in enumerate((ALU.mult, ALU.add)):
                    ins = V.tensor_tensor(v, v, lnrow[:, i:i + 1, :].to_broadcast([P, T, SGU]), op)
                    if i == 0:
                        link(ins)
                    else:
                        after(ins, vn_ready, l + 1)
                V.tensor_tensor(zxy[:, 2:4, :], lt[:, 0], zxy[:, 2:4, :], ALU.mult).then_inc(ylru, 1)
                if l == 0:
                    mod_evict(6, 7)
                eng.wait_ge(mix_ps, l + 1)
                for g in range(4):
                    u = zuv[:, :, 64 * g:64 * g + 64]
                    o = ps[:, 5 + g // 2, 256 * (g % 2):256 * (g % 2) + 256].rearrange("p (t c) -> p t c", t=T)
                    ins = V.scalar_tensor_tensor(out=u, in0=o, scalar=sgub[:, l, g:g + 1], in1=u,
                                                 op0=ALU.add, op1=ALU.mult)
                ins.then_inc(ysg_ready, 1)

                def norm(t):
                    eng.wait_ge(qs_ready, T * l + t + 1)
                    link(V.reciprocal(st8[:, 0, t:t + 5:4], st8[:, 1, t:t + 5:4]))
                    V.tensor_scalar(zq[:, t, 0:QL], zq[:, t, 0:QL], st8[:, 0, t:t + 1], None, ALU.mult)
                    V.tensor_scalar(zq[:, t, QL:QL + KVL], zq[:, t, QL:QL + KVL], st8[:, 0, 4 + t:5 + t], None,
                                    ALU.mult).then_inc(zqn_ready, 1)

                for t in range(T):
                    eng.wait_ge(*((za_ps, 3 * l + t + 1) if t < 3 else (w_used, w0 + 6)))
                    V.tensor_copy(zq[:, t, :], ps[:, t, 0:QKR]).then_inc(zq_cp, 1)
                    if t:
                        norm(t - 1)
                eng.wait_ge(zq_cp, T * (l + 1))
                x1, x2 = zq[:, :, QL + KVL:QL + KVL + HALF], zq[:, :, QL + KVL + HALF:QKR]
                cos, sin = trig[:, 0], trig[:, 1]
                ra, rb = krd[:, :, 0, 0:HALF], krd[:, :, 0, HALF:ROPE]
                rc, rd = krd[:, :, 1, 0:HALF], krd[:, :, 1, HALF:ROPE]
                V.tensor_tensor(ra, x1, cos, ALU.mult)
                V.tensor_tensor(rc, x2, sin, ALU.mult)
                V.tensor_tensor(rb, x2, cos, ALU.mult)
                link(V.tensor_tensor(rd, x1, sin, ALU.mult))
                V.tensor_tensor(ra, ra, rc, ALU.subtract)
                link(V.tensor_tensor(rb, rb, rd, ALU.add))
                V.tensor_copy(krd[:, :, 1, :], krd[:, :, 0, :]).then_inc(kr_ready, 1)
                norm(3)
                eng.wait_ge(qkT_ps, l + 1)
                for j in range(2):
                    ins = V.tensor_scalar(qT[:, j, :], ps[:, 5 + j, :], qg[:, l, j:j + 1], None, ALU.mult)
                ins.then_inc(q_in, 1)
                for j in range(2):
                    tile_lo(l, j, 4 + j, ps[:, 1 + j, :])
                for j in range(2):
                    tile_lo(l, 2 + j, 6 + j, zxy[:, 2 + j, :])
                eng.wait_ge(v_ps, l + 1)
                V.tensor_copy(vb[:, 2:4], ps[:, 6:8, :]).then_inc(v2_ready, 1)

                def queries(h):
                    n = HEADS * l + h
                    eng.wait_ge(q_ps, n + 1)
                    if h >= 2:
                        eng.wait_ge(s_ps, T * (n - 1))
                    V.tensor_tensor(qb[:, h % 2, :], ps[:, 0, :], cs[:], ALU.mult).then_inc(q_ev, 1)

                def maxima(h):
                    n = HEADS * l + h
                    for i, count in zip(SCORE_ORDER, (1, 3, 3, 4)):
                        eng.wait_ge(s_ps, T * n + count)
                        ins = V.memset(score(i)[0:64, P * i + 64:P * i + P], NEG)
                    link(ins)
                    for i in range(T):
                        ins = V.reduce_max(am[:, 0, h % 4, i:i + 1], score(i), AX.X)
                    link(ins)
                    V.tensor_scalar(am[:, 1, h % 4, :], am[:, 0, h % 4, :], -SCALE, None, ALU.mult).then_inc(
                        nm_ready, 1)

                def normalise(h):
                    n = HEADS * l + h
                    eng.wait_ge(exp_ready, T * (n + 1))
                    link(V.reciprocal(am[:, 0, h % 4, :], st8[:, 2, 4 * (h % 2):4 * (h % 2) + 4]))
                    for i in range(T):
                        p = pr[:, i, 0:P * (i + 1)]
                        V.tensor_scalar(p, p, am[:, 0, h % 4, i:i + 1], None, ALU.mult).then_inc(pn_ready, 1)

                queries(0)
                queries(1)
                maxima(0)
                normalise(0)
                for h in range(HEADS):
                    if h + 1 < HEADS:
                        maxima(h + 1)
                    if l == 0 and h in (3, 5, 7):
                        mod_evict(6 + h // 2, 0)
                    if h and h % 2 == 0:
                        tile_lo(l, 3 + h // 2, h // 2 - 1, ps[:, 2, :])
                    if h + 2 < HEADS:
                        queries(h + 2)
                    if l == 0 and h < 6:
                        mod_half(7 + h // 2, h % 2)
                    if h + 1 < HEADS:
                        normalise(h + 1)
                    if h >= HEADS - 3:
                        lo(W_O[l] + h - (HEADS - 3))
                tile_lo(l, 7, 3, ps[:, 2, :])
                lo(W_O[l] + 3)
                if l == 0:
                    for i in range(2):
                        lo(W_FF + i)

            def dense():
                s, f, m, downs = W_FF, 0, 10, 0

                def evict(w_end):
                    eng.wait_ge(*w_end)
                    eng.wait_ge(silu_ready, f + 1)
                    after(V.tensor_tensor(actf[:, f % 2, :], sgf[:, f % 2, :], ps[:, 2 * (f % 2) + 1, :], ALU.mult),
                          act_mul, f + 1)
                    eng.wait_ge(act_hi, f + 1)
                    V.tensor_tensor(act[:, 1, f % 6, :], actf[:, f % 2, :], act[:, 0, f % 6, :].bitcast(F32),
                                    ALU.subtract).then_inc(act_ready, 1)

                def down_evict(g, n, w_last):
                    for t in range(T):
                        eng.wait_ge(*((dn_ps, 6 * g + 3 * n + t + 1) if t < 3 else (w_used, w_last)))
                        o = yf[:, t, 512 * n:512 * n + 512]
                        if g:
                            V.tensor_tensor(o, ps[:, 4 + t, :], o, ALU.add).then_inc(dn_ev, 1)
                        else:
                            V.tensor_copy(o, ps[:, 4 + t, :]).then_inc(dn_ev, 1)

                for g, blocks in enumerate(GROUPS):
                    for c in range(blocks[0] // 2, blocks[-1] // 2 + 1):
                        lo(s + 2)
                        evict((gu_ps, c + 1))
                        f += 1
                        if 2 * c > blocks[0]:
                            mod_evict(m - 1, 4)
                        mod_sum(m)
                        m += 1
                        lo(s + 3)
                        evict((w_used, s + 2))
                        f += 1
                        s += 2
                    if g == 3:
                        break
                    for i in range(4):
                        lo(s + 2)
                        s += 1
                        if i == 0:
                            mod_evict(m - 1, 0)
                            mod_sum(m)
                            m += 1
                        if i == 1:
                            down_evict(g, 0, s)
                        if i == 2:
                            mod_evict(m - 1, 0)
                    down_evict(g, 1, s)
                lo(s + 2)
                for t in range(T + 2):
                    if t < T:
                        eng.wait_ge(*((dn_ps, 18 + t + 1) if t < 3 else (w_used, s + 2)))
                        o = yf[:, t, :].rearrange("p (n c) -> p n c", n=2)
                        V.tensor_tensor(o, ps[:, 2 * t:2 * t + 2, :], o, ALU.add).then_inc(dn_ev, 1)
                    if t == T - 1:
                        mod_evict(m - 1, 0)
                    if 1 <= t <= T:
                        eng.wait_ge(dn_ev, 24 + t)
                        post_tile(1, t - 1, yf[:, t - 1, :].rearrange("p (n c) -> p n c", n=2), 1, tmpf)
                    if t >= 2:
                        pre_tile(2, t - 2)
                lo(s + 3)

            def route():
                eng.wait_ge(lg_ps, 1)
                link(V.tensor_copy(lg[:], ps[:, 0, 0:T * E].rearrange("p (t e) -> p t e", t=T)))
                for t in range(T):
                    link(V.max(mx8[:, t, :], lg[:, t, :]))
                    link(V.max_index(ix8[:, t, :], mx8[:, t, :], lg[:, t, :]))
                link(V.tensor_copy(ixf[:], ix8[:]))
                ex = iot[:, 0:E].unsqueeze(1).to_broadcast([P, T, E])
                for k in range(2):
                    link(V.tensor_tensor(oh[:, k], ex, ixf[:, :, k:k + 1].to_broadcast([P, T, E]), ALU.is_equal))
                after(V.tensor_tensor(msk[:], oh[:, 0], oh[:, 1], ALU.add), msk_ready, 1)
                V.tensor_tensor(ge[:, 0, :], mx8[:, :, 1], mx8[:, :, 0], ALU.subtract).then_inc(gexp_in, 1)
                eng.wait_ge(gexp, 1)
                link(V.tensor_scalar(ge[:, 1, :], ge[:, 0, :], 1.0, None, ALU.add))
                link(V.reciprocal(gt[:, 0, :], ge[:, 1, :]))
                link(V.tensor_tensor(gt[:, 1, :], gt[:, 0, :], ge[:, 0, :], ALU.mult))
                eng.wait_ge(pos_ps, 1)
                link(V.tensor_copy(tl[:, 1, :], ps[:, 2, 0:E]))
                link(V.tensor_scalar(tl[:, 0, :], tl[:, 1, :], 0.0, None, ALU.is_gt))
                for r in range(1, T):
                    link(V.scalar_tensor_tensor(out=tl[:, 0, :], in0=tl[:, 1, :], scalar=float(P * r), in1=tl[:, 0, :],
                                                op0=ALU.is_gt, op1=ALU.add))
                link(V.tensor_tensor_scan(tl[:, 1, :], ones[:, 0:E], tl[:, 0, :], 0.0, ALU.mult, ALU.add))
                link(V.tensor_tensor(tl[:, 2, :], tl[:, 1, :], tl[:, 0, :], ALU.subtract))
                link(V.scalar_tensor_tensor(out=gpos[:], in0=tl[:, 2:3, :].to_broadcast([P, T, E]), scalar=float(P),
                                            in1=ps[:, 1, 0:T * E].rearrange("p (t e) -> p t e", t=T),
                                            op0=ALU.mult, op1=ALU.add))
                for k in range(2):
                    link(V.tensor_tensor(prod[:, k], oh[:, k], gpos[:], ALU.mult))
                    link(V.reduce_sum(slf[:, k, :], prod[:, k], AX.X))
                link(V.tensor_copy(sli[:], slf[:]))
                link(V.tensor_tensor(cmp_[:], tl[:, 1:2, :].to_broadcast([P, MAXT, E]),
                                     iot[:].unsqueeze(2).to_broadcast([P, MAXT, E]), ALU.is_le))
                link(V.reduce_sum(etf[:, 1:], cmp_[:], AX.X))
                link(V.tensor_scalar(etf[:, 1:], etf[:, 1:], float(E - 1), None, ALU.min))
                link(V.tensor_copy(etf[:, 0:1], tl[:, 1, E - 1:E]))
                V.tensor_copy(eti[:], etf[:]).then_inc(tab_ready, 1)

            def experts():
                eng.wait_ge(tab_ready, 1)
                n = eng.value_load(eti[0:1, 0:1], min_val=8, max_val=MAXT - 1)

                def part(i, j):
                    eng.wait_ge(hi_ready, i * EU + (SB + j + 1))
                    w = unit_size(j % EU)
                    o = spl[:, (SB + j) % SPLS]
                    V.tensor_tensor(o[:, 1, 0:w], mraw[:, j % MRAWS, 0:w], o[:, 0, 0:w].bitcast(F32),
                                    ALU.subtract).then_inc(lo_ready, 1)

                def rows(count):
                    eng.wait_ge(xg_ps, count)
                    for k in range(KD):
                        ins = V.tensor_scalar(xfull[:, k, :], ps[:, 2 + k // 4, P * (k % 4):P * (k % 4) + P],
                                              modn[:, 3, k:k + 1], modn[:, 2, k:k + 1], ALU.mult, ALU.add)
                    ins.then_inc(xg_full, 1)
                    eng.wait_ge(xg_hi, count)
                    V.tensor_tensor(xgT[:, 1], xfull[:], xgT[:, 0].bitcast(F32), ALU.subtract).then_inc(xg_ready, 1)

                part(0, 0)
                part(0, 1)
                rows(1)
                with eng.Fori(0, n) as i:
                    def multiply(c):
                        eng.wait_ge(e_silu, i * 3 + (c + 1))
                        eng.wait_ge(w_used, i * EU + (SB + 4 * c + 4))
                        c0, w = EW[c]
                        V.tensor_tensor(acte[:, c0:c0 + w], sge[:, 0:w], ps[:, 2 * (c % 2) + 1, 0:w],
                                        ALU.mult).then_inc(e_mul, 1)

                    def turned(c):
                        eng.wait_ge(aT_hi, i * 3 + (c + 1))
                        w = EW[c][1]
                        f = slice(4 * c, 4 * c + w // P)
                        V.tensor_tensor(aT[:, 1, f, :], ps[:, 6 + c % 2, 0:w].rearrange("p (f q) -> p f q", q=P),
                                        aT[:, 0, f, :].bitcast(F32), ALU.subtract).then_inc(aT_ready, 1)

                    for j in range(2, 6):
                        part(i, j)
                    multiply(0)
                    for j in range(6, 10):
                        part(i, j)
                    multiply(1)
                    part(i, 10)
                    part(i, 11)
                    turned(0)
                    part(i, 12)
                    part(i, 13)
                    multiply(2)
                    turned(1)
                    rows(i + 2)
                    turned(2)
                    for j in range(14, 20):
                        part(i, j)
                for t in range(T):
                    eng.wait_ge(yg_dma, 32 * (t + 1))
                    link(V.tensor_scalar(ym[:, t, :], yg[:, t, 0, :], gt[:, 0, t:t + 1], None, ALU.mult))
                    V.scalar_tensor_tensor(out=ym[:, t, :], in0=yg[:, t, 1, :], scalar=gt[:, 1, t:t + 1],
                                           in1=ym[:, t, :], op0=ALU.mult, op1=ALU.add).then_inc(ym_ready, 1)
                for t in range(T):
                    post_tile(3, t, ym[:, t, :].rearrange("p (n c) -> p n c", n=2), 2, tmpf)

            eng.wait_ge(sp_a, 1)
            after(V.tensor_scalar(sp[:, 1], sp[:, 0], 1.0, None, ALU.add), sp_b, 1)
            eng.wait_ge(sp_c, 1)
            link(V.tensor_scalar(sp[:, 1], sp[:, 1], 1.0, None, ALU.subtract))
            link(V.tensor_scalar(sp[:, 3], sp[:, 1], 0.0, None, ALU.is_equal))
            link(V.tensor_tensor(sp[:, 1], sp[:, 1], sp[:, 3], ALU.add))
            link(V.reciprocal(sp[:, 1], sp[:, 1]))
            link(V.tensor_tensor(sp[:, 2], sp[:, 2], sp[:, 1], ALU.mult))
            link(V.tensor_tensor(sp[:, 2], sp[:, 2], sp[:, 3], ALU.add))
            link(V.tensor_tensor(sp[:, 2], sp[:, 2], sp[:, 0], ALU.mult))
            link(V.tensor_scalar(sp[:, 3], lcol[:, 3], -1.0, 0.0, ALU.mult, ALU.max))
            link(V.tensor_tensor(sp[:, 2], sp[:, 2], sp[:, 3], ALU.add))
            link(V.tensor_scalar(nsp[:], sp[:, 2], -4.0, None, ALU.mult))
            link(V.tensor_scalar(hb[:], lcol[:, 1:3], 0.5, None, ALU.mult))
            eng.wait_ge(cond_ready, 1)
            for m in range(4):
                mod_sum(m)
                if m:
                    mod_evict(m - 1, 3)
            mod_evict(3, 3)
            for t in range(T):
                pre_tile(0, t)
            for i in range(2):
                lo(i)
            for l in range(L):
                prenorm(2 * l)
                mixer(l)
                for t in range(T):
                    post_tile(2 * l, t, ps[:, 2 * t:2 * t + 2, :], 0, tmpm)
                    if t:
                        pre_tile(2 * l + 1, t - 1)
                pre_tile(2 * l + 1, T - 1)
                prenorm(2 * l + 1)
                if l == 0:
                    dense()
                else:
                    route()
                    experts()


def tables():
    pos = np.arange(S, dtype=np.float32)
    inv = np.float32(10000.0) ** (-np.arange(0, ROPE, 2, dtype=np.float32) / np.float32(ROPE))
    ang = (pos[:, None] * inv[None, :]).astype(np.float32)
    cos, sin = np.cos(ang), np.sin(ang)
    cs = np.concatenate([np.ones((NOPE, S), np.float32), cos.T, cos.T, -sin.T, sin.T]).astype(np.float32)
    trig = np.stack([cos, sin]).reshape(2, T, P, HALF).transpose(2, 0, 1, 3)
    return {"cs_table": np.ascontiguousarray(cs), "trig_table": np.ascontiguousarray(trig.astype(np.float32))}


def kernel(**inputs):
    from concourse import bacc
    from concourse.bass_utils import run_bass_kernel_spmd

    nc = bacc.Bacc("TRN2", target_bir_lowering=False, num_devices=1)
    arrays = {name: np.ascontiguousarray(v) for name, v in inputs.items()} | tables()
    args = {name: nc.dram_tensor(f"in_{name}", v.shape, mybir.dt.from_np(v.dtype), kind="ExternalInput").ap()
            for name, v in arrays.items()}
    out = nc.dram_tensor("out", (1, S, D), F32, kind="ExternalOutput").ap()
    build(nc, args, out)
    r = run_bass_kernel_spmd(nc, [{f"in_{name}": v for name, v in arrays.items()}], core_ids=[0])
    return r.results[0]["out"]
```

```python
from contextlib import ExitStack

import numpy as np

import concourse.bass as bass
from concourse import mybir

F32 = mybir.dt.float32
F32R = mybir.dt.float32r
I32 = mybir.dt.int32
U32 = mybir.dt.uint32
ALU = mybir.AluOpType
ACT = mybir.ActivationFunctionType
AX = mybir.AxisListType

P = 128
L = 2
S = 512
T = S // P
D = 1024
KD = D // P
HEADS, NOPE, ROPE, VD = 8, 64, 32, 64
QL, KVL = 256, 128
HALF = ROPE // 2
QKR = QL + KVL + ROPE
SGU, LRU = 256, 256
NEG = -1e30
SCALE = (NOPE + ROPE) ** -0.5
FF, FFE, E = 2816, 1408, 8
NB = FFE // P
UNIT = 2048
RAWS, SPLS, MRAWS = 4, 3, 6
MAXT = 16
MAXI, MAX2 = 12, 7
POOL_MODS = (5, 9)
MOD_AFTER = {0: 5, 2: 6, 4: 7, 6: 8}
MODC = 6 * D // 512
GROUPS = [list(range(0, 6)), list(range(6, 12)), list(range(12, 18)), list(range(18, 22))]
EW = [(0, 512), (512, 512), (1024, 384)]
SCORE_AT = ((5, 384), (6, 0), (5, 0), (4, 0))
SCORE_ORDER = (1, 0, 2, 3)
TURN_BANK = (3, 7)
EU = 4 * len(EW) + (NB + 1) // 2


def plan():
    units = []

    def mod(m):
        for kh in range(2):
            units.append(("mod", m // MODC, m % MODC, kh))

    for m in range(4):
        mod(m)
    for l in range(L):
        for part in range(3):
            for kh in range(2):
                units.append(("win", l, part, kh))
                if l == 0 and part == 0 and kh == 1:
                    mod(4)
        halves = [("mod", 0, c, kh) for c in range(5, 10) for kh in range(2)] if l == 0 else []
        wo = [("wo", l, n, kh) for n in range(2) for kh in (1, 0)]
        units += halves[:2] + wo[:3] + halves[2:] + wo[3:]
        if l == 0:
            m = 10
            for g, blocks in enumerate(GROUPS):
                for c in range(blocks[0] // 2, blocks[-1] // 2 + 1):
                    units.append(("gate", l, c, 0))
                    units.append(("up", l, c, 0))
                    mod(m)
                    m += 1
                step = 3 if len(blocks) == 6 else 4
                for n in range(2):
                    for f in range(blocks[0], blocks[-1] + 1, step):
                        units.append(("down", n, f, step))
                if g < 3:
                    mod(m)
                    m += 1
    assert m == L * MODC
    return units


UNITS = plan()
WEIGHTS = [r for r, u in enumerate(UNITS) if u[0] != "mod"]
MODS = [r for r, u in enumerate(UNITS) if u[0] == "mod"]
SB = len(WEIGHTS)
W_IN = [WEIGHTS.index(UNITS.index(("win", l, 0, 0))) for l in range(L)]
W_O = [WEIGHTS.index(UNITS.index(("wo", l, 0, 1))) for l in range(L)]
W_FF = WEIGHTS.index(UNITS.index(("gate", 0, 0, 0)))


def build(nc, a, out):
    with ExitStack() as ctx:
        place = [16512]

        def at(name, offset, shape, dt=F32):
            return nc.alloc_sbuf_tensor_at(name, shape, dt, offset=offset)

        def region(size):
            o = place[0]
            place[0] += size
            return o

        X_, RAW_, HT_, SPL_ = region(16384), region(32768), region(32768), region(49152)
        W_ = region(57856)
        x = at("x", X_, [P, T, D])
        raw = at("raw", RAW_, [P, RAWS, UNIT])
        spl = at("spl", SPL_, [P, SPLS, 2, UNIT], F32R)
        hT = at("hT", HT_, [P, 2, KD, S], F32R)
        yT = at("yT", HT_, [P, 2, KD, S], F32R)
        zq = at("zq", W_, [P, T, QKR])
        qT = at("qT", W_, [P, 3, S])
        wuq = at("wuq", W_ + 6656, [P, 2, HEADS, P])
        wukv = at("wukv", W_ + 6656 + 8192, [P, HEADS, NOPE + VD])
        xn = at("xn", W_ + 18944, [P, T, D])
        xnf = at("xnf", HT_, [P, T, D])
        zuv = at("zuv", W_ + 18944, [P, T, 2 * SGU])
        zxy = at("zxy", W_ + 27136, [P, 4, S])
        pr = at("pr", W_ + 18944, [P, T, S])
        pT = at("pT", W_ + 27136, [P, T, S])
        T1 = W_ + 35328
        lt = at("lt", T1, [P, 4, 2, S])
        vb = at("vb", T1, [P, T, S])
        qb = at("qb", T1 + 8192, [P, 2, S])
        kb = at("kb", T1 + 12288, [P, 2, S])
        full = at("full", T1 + 8192, [P, 2, S])
        lnrow = at("lnrow", T1 + 16384, [P, 2, SGU])
        sguw = at("sguw", T1 + 18432, [P, 4, P])
        bd = at("bd", T1 + 20480, [P, 2, 2, P])
        tmpm = at("tmpm", T1, [P, 2, D])
        act = at("act", W_, [P, 2, 6, S], F32R)
        yf = at("yf", W_ + 24576, [P, T, D])
        sgf = at("sgf", W_ + 40960, [P, 2, S])
        actf = at("actf", W_ + 45056, [P, 2, S])
        tmpf = at("tmpf", W_ + 49152, [P, 2, D])
        mraw = at("mraw", RAW_, [P, MRAWS, UNIT])
        hTf = at("hTf", HT_, [P, KD, S])
        xgT = [at(f"xgT{b}", HT_ + 16384 + 8192 * b, [P, 2, KD, P], F32R) for b in range(2)]
        yg = at("yg", HT_, [P, T, 2, D])
        lgt = at("lgt", W_ + 42496, [P, S])
        xg = [at(f"xg{b}", W_ + 18944 * b, [P, D]) for b in range(2)]
        acte = [at(f"acte{b}", W_ + 4096 + 2048 * b, [P, 512]) for b in range(2)]
        sge = [at(f"sge{b}", W_ + 8192 + 2048 * b, [P, 512]) for b in range(2)]
        ye = [at(f"ye{b}", W_ + 23040 + 4096 * b, [P, D]) for b in range(2)]
        aT = [at(f"aT{b}", W_ + 31232 + 11264 * b, [P, 2, NB, P], F32R) for b in range(2)]
        xfull = at("xfull", W_ + 53760, [P, KD, P])
        ym = at("ym", W_ + 18944, [P, T, D])
        small = [W_ + 12288]

        def little(name, shape, dt=F32):
            n = int(np.prod(shape[1:])) * 4
            o = small[0]
            small[0] += (n + 31) // 32 * 32
            return at(name, o, shape, dt)

        lg = little("lg", [P, T, E])
        mx8 = little("mx8", [P, T, 8])
        ix8 = little("ix8", [P, T, 8], U32)
        ixf = little("ixf", [P, T, 8])
        oh = little("oh", [P, 2, T, E])
        msk = little("msk", [P, T + 1, E])
        gpos = little("gpos", [P, T, E])
        prod = little("prod", [P, 2, T, E])
        slf = little("slf", [P, 2, T])
        sli = little("sli", [P, 2, T], I32)
        gt = little("gt", [P, 2, T])
        ge = little("ge", [P, 2, T])
        cnt = little("cnt", [P, E])
        above = little("above", [P, T, E])
        pairs = little("pairs", [P, 2, E])
        ends = little("ends", [P, 2, E])
        starts = little("starts", [P, 2, E])
        limit = little("limit", [P, E])
        first = little("first", [P, E])
        jump = little("jump", [P, E])
        beyond = little("beyond", [P, T, E])
        cmp_ = little("cmp", [P, 2, MAXT, E])
        owner = little("owner", [P, 2, MAXT])
        etf = little("etf", [P, 2 + MAXT])
        eti = little("eti", [P, 2 + MAXT], I32)
        assert small[0] <= W_ + 18944

        def keep(name, shape, dt=F32):
            return at(name, region((int(np.prod(shape[1:])) * 4 + 31) // 32 * 32), shape, dt)

        gp = keep("gp", [P, 3, D])
        acc = keep("acc", [P, 2, 512])
        ident = keep("ident", [P, P])
        ones = keep("ones", [P, P])
        upper = keep("upper", [P, P])
        cs = keep("cs", [P, S])
        trig = keep("trig", [P, 2, T, HALF])
        krd = keep("krd", [P, T, 2, ROPE])
        colp = keep("colp", [P, 2, 96])
        prow = at("prow", W_ + 49152, [P, 2, P])
        bmod = colp[:, 0, :].rearrange("p (l k) -> p l k", l=L)
        gpre = colp[:, 1, 0:32].rearrange("p (w l k) -> p w l k", w=2, l=L)
        qg = colp[:, 1, 32:36].rearrange("p (l k) -> p l k", l=L)
        kvg = colp[:, 1, 36:38]
        lcol = colp[:, 1, 38:54].rearrange("p (w l k) -> p w l k", w=4, l=L)
        cw = colp[:, 1, 54:70].rearrange("p (l w k) -> p l w k", l=L, w=4)
        sgub = colp[:, 1, 70:78].rearrange("p (l g) -> p l g", l=L)
        modc = keep("modc", [P, 4, KD])
        modn = keep("modn", [P, 4, KD])
        sp = keep("sp", [P, 4, L, 2])
        nsp = keep("nsp", [P, L, 2])
        hb = keep("hb", [P, 2, L, 2])
        cond = keep("cond", [P, 2, KD])
        eps = keep("eps", [P, 2])
        ss = keep("ss", [P, T])
        rms = keep("rms", [P, T])
        rinv = keep("rinv", [P, T])
        st8 = keep("st8", [P, 3, 8])
        bn = keep("bn", [P, T, 6])
        mv = keep("mv", [P, T, 2])
        sd = keep("sd", [P, 2, T])
        am = keep("am", [P, 2, 4, T])
        router = keep("router", [P, KD, E])
        iot = keep("iot", [P, MAXT])
        assert place[0] <= 229344, place[0]

        ps = ctx.enter_context(nc.psum_tensor("ps", [P, 8, 512], F32))
        tiles_dram = nc.dram_tensor("scratch", ((MAXI + MAX2 + 1) * P, D), F32).ap()
        scratch = tiles_dram[0:MAXT * P, :]

        def sem(name):
            return ctx.enter_context(nc.semaphore(name))

        raw_full = [sem(f"raw_full{i}") for i in range(RAWS)]
        mraw_full = [sem(f"mraw_full{i}") for i in range(MRAWS)]
        pool_read, pool_chain, xn_scale = sem("pool_read"), sem("pool_chain"), sem("xn_scale")
        mod_read, hi_ready, lo_ready, w_used, mod_ps, mod_out = map(sem, (
            "mod_read", "hi_ready", "lo_ready", "w_used", "mod_ps", "mod_out"))
        x_dma, c_dma, par_dma, lpar_dma, post_dma, zero_dma, out_dma = map(sem, (
            "x_dma", "c_dma", "par_dma", "lpar_dma", "post_dma", "zero_dma", "out_dma"))
        const_ready, prow_zero, cond_ready, sp_a, sp_b, sp_c, zeros_ready, zeros2_ready = map(sem, (
            "const_ready", "prow_zero", "cond_ready", "sp_a", "sp_b", "sp_c", "zeros_ready", "zeros2_ready"))
        act_chain, dve_chain = sem("act_chain"), sem("dve_chain")
        rms_ready, xn_ready, xT_ps, hT_hi, hT_ready, x_upd, pss = map(sem, (
            "rms_ready", "xn_ready", "xT_ps", "hT_hi", "hT_ready", "x_upd", "pss"))
        za_ps, zb_ps, zc_ps, zq_cp, zuv_ready, zx_cp, zy_ready = map(sem, (
            "za_ps", "zb_ps", "zc_ps", "zq_cp", "zuv_ready", "zx_cp", "zy_ready"))
        sw_ps, sw_cp, sw_ready, bn_done, sd_ready, vn_ready, mix_ps, ysg_ready, ysT_ps = map(sem, (
            "sw_ps", "sw_cp", "sw_ready", "bn_done", "sd_ready", "vn_ready", "mix_ps", "ysg_ready", "ysT_ps"))
        yT_hi, yT_ready = sem("yT_hi"), sem("yT_ready")
        xc_ready, gate_ps, gate_t, la_ready, ea_ready, lq_ready, lsq_ready, ylru = map(sem, (
            "xc_ready", "gate_ps", "gate_t", "la_ready", "ea_ready", "lq_ready", "lsq_ready", "ylru"))
        bd_ready, col_ps, col_ready, kr_ready, q_in, v2_ready = map(sem, (
            "bd_ready", "col_ps", "col_ready", "kr_ready", "q_in", "v2_ready"))
        qs_ready, zqn_ready, qkT_ps, att_in, v_ps, v_ready = map(sem, (
            "qs_ready", "zqn_ready", "qkT_ps", "att_in", "v_ps", "v_ready"))
        q_ps, k_ps, q_ev, k_ev, s_ps, nm_ready, exp_ready, pn_ready, pt_ps, pt_ev, o_ps = map(sem, (
            "q_ps", "k_ps", "q_ev", "k_ev", "s_ps", "nm_ready", "exp_ready", "pn_ready", "pt_ps", "pt_ev", "o_ps"))
        wo_ps, ye_free = sem("wo_ps"), sem("ye_free")
        gu_ps, silu_ready, act_mul, act_hi, act_ready, dn_ps, dn_ev = map(sem, (
            "gu_ps", "silu_ready", "act_mul", "act_hi", "act_ready", "dn_ps", "dn_ev"))
        lg_ps, msk_ready, pos_ps, gexp_in, gexp, tab_ready, scat_dma = map(sem, (
            "lg_ps", "msk_ready", "pos_ps", "gexp_in", "gexp", "tab_ready", "scat_dma"))
        lgt_ps, lgt_ready, slots_ready = sem("lgt_ps"), sem("lgt_ready"), sem("slots_ready")
        share_ready, ym_ready, scaled, x_final, x_last = map(sem, (
            "share_ready", "ym_ready", "scaled", "x_final", "x_last"))

        def of_tiles(name):
            return [sem(name + "_a"), sem(name + "_b")]

        xg_dma, xg_ps, xg_full, xg_hi, xg_ready = map(of_tiles, ("xg_dma", "xg_ps", "xg_full", "xg_hi", "xg_ready"))
        e_silu, e_mul, aT_ps, aT_hi, aT_ready, ye_ev, ye_dma = map(of_tiles, (
            "e_silu", "e_mul", "aT_ps", "aT_hi", "aT_ready", "ye_ev", "ye_dma"))
        yg_dma = [sem(f"yg_dma{t}") for t in range(T)]

        wmod = a["w_mod"].rearrange("l (p k) n -> l p k n", k=KD)

        def src_of(u):
            kind, l, c, kh = u
            if kind == "mod":
                return wmod[l, :, 4 * kh:4 * kh + 4, 512 * c:512 * c + 512], 4, 512
            if kind == "win":
                c0, w = ((QKR + 512, 512), (QKR, 512), (0, QKR))[c]
                return a["w_in"][l, 512 * kh:512 * kh + 512, c0:c0 + w].rearrange("(k p) n -> p k n", p=P), 4, w
            if kind == "wo":
                return a["w_o"][l, 512 * kh:512 * kh + 512, 512 * c:512 * c + 512].rearrange(
                    "(k p) n -> p k n", p=P), 4, 512
            if kind in ("gate", "up"):
                return a[f"ffn_w_{kind}"][0, :, 256 * c:256 * c + 256].rearrange("(k p) n -> p k n", p=P), 8, 256
            n, f, step = l, c, kh
            return a["ffn_w_down"][0, P * f:P * (f + step), 512 * n:512 * n + 512].rearrange(
                "(k p) n -> p k n", p=P), step, 512

        def score(i):
            bank, c0 = SCORE_AT[i]
            return ps[:, bank, c0:c0 + P * (i + 1)]

        def xn_of(s):
            return xnf if s == 2 else xn

        def unit_size(j):
            return 4 * EW[j // 4][1] if j < 4 * len(EW) else min(2, NB - 2 * (j - 4 * len(EW))) * D

        def mod_done(m, kh):
            before = sum(c < m for c in POOL_MODS)
            return (pool_read, 2 * before + kh + 1) if m in POOL_MODS else (mod_read, 2 * (m - before) + kh + 1)

        def size_of(u):
            _, k, w = src_of(u)
            return k * w

        block = ctx.enter_context(nc.Block())

        @block.sync
        def _(eng):
            def parameters():
                eng.wait_ge(prow_zero, 1)
                rows = [a["b_mod"].rearrange("l (k p) -> (l k) p", p=P)]
                rows += [a[n].rearrange("l (k p) -> (l k) p", p=P) for n in (
                    "pre_mix_g", "pre_ffn_g", "q_norm_g", "kv_norm_g", "conv_b", "lru_ba", "lru_bx", "lru_lambda")]
                rows += [a["conv_w"].rearrange("l w (j p) -> (l w j) p", p=P), a["sgu_b"].rearrange("l g p -> (l g) p")]
                at_row = 0
                for n, src in enumerate(rows):
                    k = src.shape[0]
                    dst = prow[0:k, 0, :] if n == 0 else prow[at_row:at_row + k, 1, :]
                    at_row += k if n else 0
                    eng.dma_start(dst, src).then_inc(par_dma, 16)
                assert at_row == 78
                for dst, src in (
                        (cs[:], a["cs_table"]), (trig[:], a["trig_table"]),
                        (router[:], a["moe_router"][0].rearrange("(k p) e -> p k e", p=P))):
                    eng.dma_start(dst, src).then_inc(par_dma, 16)

            mods = weights = 0
            seen = []
            for r, u in enumerate(UNITS):
                if r >= RAWS:
                    eng.wait_ge(*seen[r - RAWS])
                src, k, w = src_of(u)
                eng.dma_start(raw[:, r % RAWS, 0:k * w].rearrange("p (k n) -> p k n", k=k), src).then_inc(
                    raw_full[r % RAWS], 16)
                if u[0] == "mod":
                    seen.append(mod_done(*divmod(mods, 2)))
                    mods += 1
                else:
                    weights += 1
                    seen.append((lo_ready, weights))
                if r == 1:
                    eng.dma_start(x[:], a["x"][0].rearrange("(t p) d -> p t d", p=P)).then_inc(x_dma, 16)
                if r == RAWS - 1:
                    parameters()
            eng.wait_ge(lo_ready, SB)
            eng.wait_ge(lg_ps, 1)
            eng.wait_ge(tab_ready, 1)
            eng.wait_ge(scat_dma, 16 * 2 * T)
            n = eng.value_load(eti[0:1, 0:1], min_val=2, max_val=MAXI)

            def unit(i, e, j):
                eng.wait_ge(lo_ready, i * EU + (SB + j - MRAWS + 1))
                dst = mraw[:, j % MRAWS, :]
                if j < 4 * len(EW):
                    c0, w = EW[j // 4]
                    name = "moe_w_gate" if j % 4 < 2 else "moe_w_up"
                    kh = j % 2
                    src = a[name][0][bass.ds(e, 1), 512 * kh:512 * kh + 512, c0:c0 + w].rearrange(
                        "a (k p) n -> p (a k) n", p=P)
                    dst = dst[:, 0:4 * w].rearrange("p (k n) -> p k n", k=4)
                else:
                    f = 2 * (j - 4 * len(EW))
                    k = min(2, NB - f)
                    src = a["moe_w_down"][0][bass.ds(e, 1), P * f:P * (f + k), :].rearrange(
                        "a (k p) n -> p (a k) n", p=P)
                    dst = dst[:, 0:k * D].rearrange("p (k n) -> p k n", k=k)
                eng.dma_start(dst, src).then_inc(mraw_full[j % MRAWS], 16)

            with eng.Fori(0, n) as i:
                e = eng.value_load(eti[0:1, bass.ds(i + 2, 1)], min_val=0, max_val=E - 1)
                for j in range(EU):
                    unit(i, e, j)
            e = eng.value_load(eti[0:1, bass.ds(n + 2, 1)], min_val=0, max_val=E - 1)
            for j in range(2):
                unit(n, e, j)
            for t in range(T):
                eng.wait_ge(*((x_final, t + 1) if t < T - 1 else (x_last, 1)))
                eng.dma_start(out[0, P * t:P * t + P, :], x[:, t, :]).then_inc(out_dma, 16)
            eng.wait_ge(out_dma, 16 * T)
            eng.wait_ge(mraw_full[1], 16)

        @block.gpsimd
        def _(eng):
            g = nc.gpsimd
            done = [0]

            def mod_sum(m):
                eng.wait_ge(cond_ready, 1)
                if m >= 2:
                    eng.wait_ge(mod_ps, m - 1)
                v = acc[:, m % 2, :]
                for kh in range(2):
                    r = MODS[2 * m + kh]
                    eng.wait_ge(raw_full[r % RAWS], 16 * (r // RAWS + 1))
                    w = [raw[:, r % RAWS, 512 * kk:512 * kk + 512] for kk in range(4)]
                    for kk in range(4):
                        ins = g.tensor_scalar(w[kk], w[kk], cond[:, 1, 4 * kh + kk:4 * kh + kk + 1], None, ALU.mult)
                    for kk in range(1 - kh, 4):
                        done[0] += 1
                        ins.then_inc(pool_chain, 1)
                        eng.wait_ge(pool_chain, done[0])
                        ins = g.tensor_tensor(v, v if kh or kk > 1 else w[0], w[kk], ALU.add)
                    ins.then_inc(pool_read, 1)
                    eng.wait_ge(*mod_done(m, kh))

            g.memset(prow[:], 0.0).then_inc(prow_zero, 1)
            g.memset(ident[:], 0.0).then_inc(zeros_ready, 1)
            g.memset(upper[:], 1.0).then_inc(zeros_ready, 1)
            g.memset(ones[:], 1.0)
            g.memset(eps[:, 0:1], 1e-6)
            g.memset(eps[:, 1:2], 1e-5)
            g.iota(iot[:], [[1, MAXT]], base=0, channel_multiplier=0, allow_small_or_imprecise_dtypes=True)
            eng.wait_ge(zeros_ready, 2)
            g.affine_select(out=ident[:], in_=ident[:], compare_op=ALU.not_equal, fill=1.0, base=0,
                            pattern=[[-1, P]], channel_multiplier=1)
            g.affine_select(out=upper[:], in_=upper[:], compare_op=ALU.is_gt, fill=0.0, base=0,
                            pattern=[[1, P]], channel_multiplier=-1).then_inc(const_ready, 1)
            eng.wait_ge(mod_read, 6)
            for slot, name, l in ((0, "post_mix_g", 0), (1, "post_ffn_g", 0), (2, "post_ffn_g", 1)):
                g.dma_start(gp[:, slot, :], a[name][l:l + 1, :].to_broadcast([P, D])).then_inc(post_dma, 16)

            def layer_params(l):
                if l:
                    eng.wait_ge(x_upd, 2 * T * l)
                loads = [
                    (lnrow[:, 0, :], a["sgu_ln_g"][l:l + 1, :].to_broadcast([P, SGU])),
                    (lnrow[:, 1, :], a["sgu_ln_b"][l:l + 1, :].to_broadcast([P, SGU])),
                    (sguw[:], a["sgu_w"][l].rearrange("g t s -> t g s")),
                    (wukv[:], a["w_ukv"][l].rearrange("p (h n) -> p h n", h=HEADS)),
                ]
                for k in range(2):
                    w = a["w_uq"][l, P * k:P * k + P, :].rearrange("p (h n) -> p h n", h=HEADS)
                    loads += [
                        (wuq[:, k, :, 0:NOPE + ROPE], w),
                        (wuq[:, k, :, NOPE + ROPE:NOPE + ROPE + HALF], w[:, :, NOPE + HALF:NOPE + ROPE]),
                        (wuq[:, k, :, NOPE + ROPE + HALF:P], w[:, :, NOPE:NOPE + HALF]),
                    ]
                for dst, src in loads:
                    g.dma_start(dst, src).then_inc(lpar_dma, 16)
                g.memset(bd[:], 0.0).then_inc(zeros2_ready, 1)
                eng.wait_ge(zeros2_ready, l + 1)
                for which, name in enumerate(("lru_wa", "lru_wx")):
                    for h in range(4):
                        o = 64 * (h % 2)
                        g.dma_start(bd[o:o + 64, which, h // 2, o:o + 64], a[name][l, h]).then_inc(bd_ready, 16)

            def sgu_mask(l):
                eng.wait_ge(sw_cp, l + 1)
                g.affine_select(out=sguw[:], in_=sguw[:], compare_op=ALU.is_ge, fill=0.0, base=0,
                                pattern=[[0, 4], [1, P]], channel_multiplier=-1).then_inc(sw_ready, 1)

            layer_params(0)
            sgu_mask(0)
            for m in POOL_MODS:
                mod_sum(m)
            eng.wait_ge(x_upd, T)
            g.dma_start(gp[:, 0, :], a["post_mix_g"][1:2, :].to_broadcast([P, D])).then_inc(post_dma, 16)
            layer_params(1)
            sgu_mask(1)
            g.memset(gp[:, 1, :], 0.0).then_inc(zeros2_ready, 1)
            eng.wait_ge(zeros2_ready, L + 1)
            for i in range(MAXT):
                g.dma_start(scratch[P * i:P * i + P, :], gp[:, 1, :]).then_inc(zero_dma, 16)
            eng.wait_ge(slots_ready, 1)
            eng.wait_ge(xn_ready, 4 * T)
            eng.wait_ge(zero_dma, 16 * MAXT)
            for t in range(T):
                for k in range(2):
                    g.indirect_dma_start(out=scratch, out_offset=bass.IndirectOffsetOnAxis(
                        ap=sli[:, k, t:t + 1], axis=0), in_=xn[:, t, :], in_offset=None).then_inc(scat_dma, 16)
            eng.wait_ge(scat_dma, 16 * 2 * T)
            eng.wait_ge(tab_ready, 1)
            n = eng.value_load(eti[0:1, 0:1], min_val=2, max_val=MAXI)
            n2 = eng.value_load(eti[0:1, 1:2], min_val=1, max_val=MAX2)
            eng.sem_inc(ye_free, 1)
            for b in range(2):
                g.dma_start(xg[b][:], scratch[P * b:P * b + P, :]).then_inc(xg_dma[b], 16)

            def item(i, tiles, first_row):
                for b in range(tiles):
                    eng.wait_ge(xg_ps[b], i + 1)
                    g.dma_start(xg[b][:], tiles_dram[bass.ds(first_row + P * (tiles + b), P), :]).then_inc(xg_dma[b], 16)
                for b in range(tiles):
                    eng.wait_ge(ye_ev[b], i + 1)
                    g.dma_start(tiles_dram[bass.ds(first_row + P * b, P), :], ye[b][:]).then_inc(ye_dma[b], 16)
                eng.wait_ge(xg_ready[0], i + 2)
                if tiles == 2:
                    eng.wait_ge(xg_ready[1], i + 2)
                eng.wait_ge(lo_ready, i * EU + (SB + EU + 2))
                for b in range(tiles):
                    eng.wait_ge(ye_dma[b], i * 16 + 16)
                eng.sem_inc(ye_free, 1)

            with eng.Fori(0, n2) as i:
                item(i, 2, i * (2 * P))
            with eng.Fori(n2, n) as i:
                item(i, 1, (i + n2) * P)
            for t in range(T):
                for k in range(2):
                    g.indirect_dma_start(out=yg[:, t, k, :], out_offset=None, in_=scratch,
                                         in_offset=bass.IndirectOffsetOnAxis(ap=sli[:, k, t:t + 1], axis=0)
                                         ).then_inc(yg_dma[t], 16)
            for t in range(T - 1):
                eng.wait_ge(scaled, t + 1)
                g.tensor_tensor(x[:, t, :], x[:, t, :], ym[:, t, :], ALU.add).then_inc(x_final, 1)

        @block.tensor
        def _(eng):
            mm = nc.tensor.matmul

            def mm3(o, lhs, rhs, start, stop):
                (lh, ll), (rh, rl) = lhs, rhs
                mm(o, lh, rh, start=start, stop=False)
                mm(o, lh, rl, start=False, stop=False)
                return mm(o, ll, rh, start=False, stop=stop)

            def unit_of(s, k, w):
                v = spl[:, s % SPLS, :, 0:k * w].rearrange("p h (k n) -> p h k n", k=k)
                return lambda kk, c0, n: (v[:, 0, kk, c0:c0 + n], v[:, 1, kk, c0:c0 + n])

            def hi_lo(t, k, c0, n):
                return t[:, 0, k, c0:c0 + n], t[:, 1, k, c0:c0 + n]

            def tr(o, i):
                return nc.tensor.transpose(o, i, ident[:])

            def mod(m, bank):
                c = m % MODC
                eng.wait_ge(*mod_done(m, 1))
                if m:
                    eng.wait_ge(mod_out, m)
                v = acc[:, m % 2, :]
                if c // 2 in (2, 5):
                    mm(ps[:, bank, :], ones[:], v, start=True, stop=True, skip_group_check=True)
                    for q in range(4):
                        b = bmod[:, m // MODC, 4 * c + q:4 * c + q + 1].to_broadcast([P, P])
                        last = mm(ps[:, bank, P * q:P * q + P], b, ident[:], start=False, stop=True,
                                  skip_group_check=True)
                else:
                    for q in range(4):
                        last = mm(ps[:, bank, q:q + 1], v[:, P * q:P * q + P], ones[:, 0:1], start=True, stop=True)
                last.then_inc(mod_ps, 1)

            def prenorm(s):
                if s:
                    eng.wait_ge(x_upd, T * s)
                for t in range(T):
                    eng.wait_ge(xn_ready, T * s + t + 1)
                    for k in range(KD):
                        last = tr(ps[:, k, P * t:P * t + P], xn_of(s)[:, t, P * k:P * k + P])
                        if t == T - 1:
                            last.then_inc(xT_ps, 1)

            def in_proj(l, part, kh):
                w, bank0, done = ((512, 0, zc_ps), (512, 4, zb_ps), (QKR, 0, za_ps))[part]
                s = W_IN[l] + 2 * part + kh
                u = unit_of(s, 4, w)
                eng.wait_ge(lo_ready, s + 1)
                if part == 0 and kh == 0:
                    for t0 in (0, 2):
                        for kk in range(4):
                            eng.wait_ge(hT_ready, KD * 2 * l + max(kk + 1, t0 + 2))
                            for t in (t0, t0 + 1):
                                last = mm3(ps[:, t, :], u(kk, P * t, P), hi_lo(hT, kk, 0, S), kk == 0, False)
                    last.then_inc(w_used, 1)
                    return
                if part == 2 and kh == 0:
                    eng.wait_ge(gate_t, l + 1)
                for t in range(T):
                    if part == 1 and kh == 0 and t == 2:
                        eng.wait_ge(sw_cp, l + 1)
                    if part == 1 and kh == 0 and t == 3 and l == 0:
                        eng.wait_ge(mod_out, 5)
                    for kk in range(4):
                        k = 4 * kh + kk
                        if part == 0 and kh == 1 and t == 0:
                            eng.wait_ge(hT_ready, KD * 2 * l + k + 1)
                        o = ps[:, bank0 + t, 0:w]
                        if part:
                            last = mm3(o, hi_lo(hT, k, P * t, P), u(kk, 0, w), k == 0, k == 7)
                        else:
                            last = mm3(o, u(kk, P * t, P), hi_lo(hT, k, 0, S), k == 0, k == 7)
                    if kh and t < 3:
                        last.then_inc(done, 1)
                last.then_inc(w_used, 1)

            def projections(l):
                for kh in range(2):
                    in_proj(l, 0, kh)
                if l == 0:
                    mod(4, 7)
                eng.wait_ge(lpar_dma, 16 * 10 * (l + 1))
                for g in range(4):
                    last = tr(ps[:, 6, P * g:P * g + P], sguw[:, g, :])
                last.then_inc(sw_ps, 1)
                in_proj(l, 1, 0)
                eng.wait_ge(bd_ready, 16 * 8 * (l + 1))
                eng.wait_ge(zy_ready, 2 * (l + 1))
                eng.wait_ge(xc_ready, l + 1)
                for which in range(2):
                    for j in range(2):
                        last = mm(ps[:, 2 * which + j, :], bd[:, which, j, :], lt[:, 0, j, :], start=True, stop=True)
                last.then_inc(gate_ps, 1)
                in_proj(l, 1, 1)
                in_proj(l, 2, 0)
                eng.wait_ge(zuv_ready, T * (l + 1))
                eng.wait_ge(vn_ready, l + 1)
                eng.wait_ge(sw_ready, l + 1)
                for g in range(4):
                    o = ps[:, 5 + g // 2, 256 * (g % 2):256 * (g % 2) + 256].rearrange("p (t c) -> p t c", t=T)
                    last = mm(o, sguw[:, g, :], zuv[:, :, SGU + 64 * g:SGU + 64 * g + 64], start=True, stop=True)
                last.then_inc(mix_ps, 1)
                in_proj(l, 2, 1)
                eng.wait_ge(ysg_ready, l + 1)
                eng.wait_ge(zq_cp, T * l + 3)
                for j in range(2):
                    for t in range(T):
                        last = tr(ps[:, 1 + j, P * t:P * t + P], zuv[:, t, P * j:P * j + P])
                    last.then_inc(ysT_ps, 1)

            def latents(l):
                eng.wait_ge(zq_cp, T * (l + 1))
                for t in range(T):
                    eng.wait_ge(zqn_ready, T * l + t + 1)
                    for j in range(3):
                        tr(ps[:, (5, 6, 0)[j], P * t:P * t + P], zq[:, t, P * j:P * j + P])
                eng.wait_ge(kr_ready, l + 1)
                for t in range(T):
                    last = tr(ps[0:64, 3, P * t:P * t + P], krd[:, t].rearrange("p a b -> p (a b)"))
                last.then_inc(qkT_ps, 1)
                eng.wait_ge(att_in, l + 1)
                for t in (0, 3, 1, 2):
                    if t == 1:
                        eng.wait_ge(q_in, l + 1)
                    last = mm(ps[:, 4 + t, :].rearrange("p (h c) -> p h c", h=HEADS), qT[:, 2, P * t:P * t + P],
                              wukv[:, :, NOPE:NOPE + VD], start=True, stop=True)
                last.then_inc(v_ps, 1)

            def queries(l, h):
                n = HEADS * l + h
                if n:
                    eng.wait_ge(q_ev, n)
                if l == 0 and h - 3 in MOD_AFTER:
                    eng.wait_ge(mod_out, MOD_AFTER[h - 3] + 1)
                for k in range(2):
                    last = mm(ps[:, 0, :], wuq[:, k, h, :], qT[:, k, :], start=(k == 0), stop=(k == 1))
                last.then_inc(q_ps, 1)

            def keys(l, h):
                n = HEADS * l + h
                if n:
                    eng.wait_ge(k_ev, n)
                if h == 0:
                    eng.wait_ge(yT_ready, 8 * l + 1)
                mm(ps[0:NOPE, 1, :], wukv[:, h, 0:NOPE], qT[:, 2, :], start=True, stop=True).then_inc(k_ps, 1)

            def scores(l, h):
                n = HEADS * l + h
                eng.wait_ge(q_ev, n + 1)
                eng.wait_ge(k_ev, n + 1)
                if h == 0:
                    eng.wait_ge(v_ready, l + 1)
                    eng.wait_ge(v2_ready, l + 1)
                else:
                    eng.wait_ge(exp_ready, T * n)
                for i in SCORE_ORDER:
                    mm(score(i), qb[:, h % 2, P * i:P * (i + 1)], kb[:, h % 2, 0:P * (i + 1)], start=True,
                       stop=True).then_inc(s_ps, 1)

            def turn(l, h, i):
                n = HEADS * l + h
                eng.wait_ge(pn_ready, T * n + i + 1)
                if T * n + i >= 2:
                    eng.wait_ge(pt_ev, T * n + i - 1)
                for j in range(i + 1):
                    last = tr(ps[:, TURN_BANK[i % 2], P * j:P * j + P], pr[:, i, P * j:P * j + P])
                last.then_inc(pt_ps, 1)

            def values(l, h):
                n = HEADS * l + h
                eng.wait_ge(pt_ev, T * (n + 1))
                if h % 2 == 0:
                    eng.wait_ge(yT_ready, 8 * l + 4 + h // 2)
                o = 64 * (h % 2)
                for j in range(T):
                    last = mm(ps[o:o + 64, 2, P * j:S], vb[:, j, VD * h:VD * h + VD], pT[:, j, P * j:S],
                              start=(j == 0), stop=True, skip_group_check=True)
                last.then_inc(o_ps, 1)

            def attention(l):
                for h in range(2):
                    queries(l, h)
                    keys(l, h)
                scores(l, 0)
                for h in range(HEADS):
                    if h + 1 < HEADS:
                        scores(l, h + 1)
                    else:
                        eng.wait_ge(yT_ready, 8 * l + 4)
                        eng.wait_ge(q_ev, HEADS * (l + 1))
                        if l == 0:
                            eng.wait_ge(mod_out, 9)
                        eng.wait_ge(lo_ready, W_O[l] + 1)
                        out_tile(l, 0, 0, 0)
                        eng.wait_ge(exp_ready, T * HEADS * (l + 1))
                        out_tile(l, 0, 0, 2)
                    turn(l, h, 0)
                    turn(l, h, 1)
                    if h + 2 < HEADS:
                        keys(l, h + 2)
                    turn(l, h, 2)
                    turn(l, h, 3)
                    if h + 2 < HEADS:
                        queries(l, h + 2)
                    values(l, h)
                    if l == 0 and h in MOD_AFTER:
                        eng.wait_ge(q_ev, min(h + 3, HEADS))
                        mod(MOD_AFTER[h], 0)

            def out_tile(l, n, i, t):
                u = unit_of(W_O[l] + 2 * n + i, 4, 512)
                for kk in range(4):
                    last = mm3(ps[:, 2 * t + n, :], hi_lo(yT, 4 * (1 - i) + kk, P * t, P), u(kk, 0, 512),
                               i == 0 and kk == 0, i == 1 and kk == 3)
                return last

            def out_proj(l):
                out_tile(l, 0, 0, 3)
                eng.wait_ge(yT_ready, 8 * (l + 1))
                out_tile(l, 0, 0, 1).then_inc(w_used, 1)
                for n, i in ((0, 1), (1, 0), (1, 1)):
                    if n == 1 and i == 0:
                        if l == 0:
                            mod(9, 1)
                        eng.wait_ge(pt_ev, T * HEADS * (l + 1))
                        if l == 0:
                            eng.wait_ge(mod_out, 10)
                    eng.wait_ge(lo_ready, W_O[l] + 2 * n + i + 1)
                    for t in range(T):
                        last = out_tile(l, n, i, t)
                        if t < 3 and i == 1:
                            last.then_inc(wo_ps, 1)
                    last.then_inc(w_used, 1)

            def dense():
                s, m, downs = W_FF, 10, 0
                for g, blocks in enumerate(GROUPS):
                    for c in range(blocks[0] // 2, blocks[-1] // 2 + 1):
                        units = [unit_of(s + i, KD, 256) for i in range(2)]
                        for b in range(2):
                            f = 2 * c + b
                            if f >= 2:
                                eng.wait_ge(act_mul, f - 1)
                            if b == 0 and 2 * c == blocks[0] and g:
                                eng.wait_ge(mod_out, m)
                            steps = [(i, k) for i in range(2) for k in range(KD)]
                            if f == 0:
                                steps = [(i, k) for k in range(KD) for i in range(2)]
                            for i, k in steps:
                                if b == 0 and k == 0:
                                    eng.wait_ge(lo_ready, s + i + 1)
                                if f == 0 and i == 0:
                                    eng.wait_ge(hT_ready, KD + max(k + 1, 2))
                                last = mm3(ps[:, 2 * b + i, :], units[i](k, P * b, P), hi_lo(hT, k, 0, S),
                                           k == 0, k == KD - 1)
                                if k == KD - 1 and b == 1:
                                    last.then_inc(w_used, 1)
                                elif k == KD - 1 and i == 1:
                                    last.then_inc(gu_ps, 1)
                            if b == 0 and 2 * c > blocks[0]:
                                if g:
                                    eng.wait_ge(dn_ev, 8 * g)
                                mod(m, 4)
                                m += 1
                        s += 2
                    eng.wait_ge(mod_out, m)
                    step = 3 if len(blocks) == 6 else 4
                    if g == 3:
                        break
                    for n in range(2):
                        for f0 in range(blocks[0], blocks[-1] + 1, step):
                            u = unit_of(s, step, 512)
                            eng.wait_ge(lo_ready, s + 1)
                            for t in range(T):
                                if downs and f0 == blocks[0]:
                                    eng.wait_ge(dn_ev, 4 * (downs - 1) + t + 1)
                                for i in range(step):
                                    f = f0 + i
                                    if t == 0 and n == 0:
                                        eng.wait_ge(act_ready, f + 1)
                                    last = mm3(ps[:, 4 + t, :], hi_lo(act, f - blocks[0], P * t, P), u(i, 0, 512),
                                               f == blocks[0], f == blocks[-1])
                                if t < 3 and f0 + step > blocks[-1]:
                                    last.then_inc(dn_ps, 1)
                            last.then_inc(w_used, 1)
                            s += 1
                            if f0 == blocks[0]:
                                if n == 0:
                                    eng.wait_ge(act_mul, blocks[-1])
                                mod(m, 0)
                                m += 1
                        downs += 1
                eng.wait_ge(act_mul, FF // P)
                eng.wait_ge(dn_ev, 4 * downs)
                for t in range(T):
                    for n in range(2):
                        u = unit_of(s + n, step, 512)
                        if t == 0:
                            eng.wait_ge(lo_ready, s + n + 1)
                        for i in range(step):
                            if t == 0 and n == 0:
                                eng.wait_ge(act_ready, blocks[i] + 1)
                            last = mm3(ps[:, 2 * t + n, :], hi_lo(act, i, P * t, P), u(i, 0, 512),
                                       i == 0, i == step - 1)
                        if t == 3:
                            last.then_inc(w_used, 1)
                        elif n == 1:
                            last.then_inc(dn_ps, 1)
                eng.wait_ge(dn_ev, 4 * downs + 1)
                mod(m, 0)

            def route():
                for k in range(KD):
                    eng.wait_ge(hT_ready, KD * 3 + k + 1)
                    last = mm(ps[0:E, 0, :], router[:, k, :], hTf[:, k, :], start=(k == 0), stop=(k == KD - 1))
                last.then_inc(lgt_ps, 1)
                eng.wait_ge(lgt_ready, 1)
                for t in range(T):
                    last = nc.tensor.transpose(ps[:, 1, E * t:E * t + E], lgt[0:E, P * t:P * t + P], ident[0:E, 0:E])
                last.then_inc(lg_ps, 1)
                eng.wait_ge(msk_ready, 1)
                mm(ps[:, 2, 0:(T + 1) * E], upper[:], msk[:].rearrange("p t e -> p (t e)"), start=True, stop=True,
                   skip_group_check=True)
                for t in range(T):
                    last = mm(ps[:, 2, E * (t + 1):E * (T + 1)].rearrange("p (t e) -> p t e", e=E), ones[:],
                              msk[:, t:t + 1, :].to_broadcast([P, T - t, E]), start=False, stop=True,
                              skip_group_check=True)
                last.then_inc(pos_ps, 1)

            def turn_rows(b, count):
                eng.wait_ge(xg_dma[b], count * 16)
                for k in range(KD):
                    last = tr(ps[:, 2 * b + k // 4, P * (k % 4):P * (k % 4) + P], xg[b][:, P * k:P * k + P])
                last.then_inc(xg_ps[b], 1)

            def item(i, tiles):
                def unit(j, k, w):
                    eng.wait_ge(lo_ready, i * EU + (SB + j + 1))
                    return unit_of(SB + j, k, w)

                def turn_act(c):
                    bank = (4, 5, 0)[c]
                    for b in range(tiles):
                        eng.wait_ge(e_mul[b], i * 3 + (c + 1))
                        for q in range(EW[c][1] // P):
                            last = tr(ps[:, bank + 2 * b, P * q:P * q + P], acte[b][:, P * q:P * q + P])
                        last.then_inc(aT_ps[b], 1)

                for c, (c0, w) in enumerate(EW):
                    for part in range(2):
                        for kh in range(2):
                            u = unit(4 * c + 2 * part + kh, 4, w)
                            for b in range(tiles):
                                if c + part + kh == 0:
                                    eng.wait_ge(xg_ready[b], i + 1)
                                if c and kh == 0:
                                    eng.wait_ge((e_mul if part else e_silu)[b], i * 3 + c)
                                for kk in range(4):
                                    k = 4 * kh + kk
                                    last = mm3(ps[:, 2 * b + part, 0:w], hi_lo(xgT[b], k, 0, P), u(kk, 0, w),
                                               k == 0, k == KD - 1)
                            last.then_inc(w_used, 1)
                        if c and part == 0:
                            if c == 1:
                                eng.wait_ge(ye_free, i + 1)
                            turn_act(c - 1)
                for j in range(4 * len(EW), EU):
                    f0 = 2 * (j - 4 * len(EW))
                    step = min(2, NB - f0)
                    u = unit(j, step, D)
                    for b in range(tiles):
                        eng.wait_ge(aT_ready[b], i * 3 + (3 if f0 >= 8 else 2))
                        for q in range(step):
                            for h in range(2):
                                last = mm3(ps[:, 4 + 2 * b + h, :], hi_lo(aT[b], f0 + q, 0, P), u(q, 512 * h, 512),
                                           f0 + q == 0, f0 + q == NB - 1)
                    last.then_inc(w_used, 1)
                    if f0 == 0:
                        turn_act(2)
                    if f0 == 2:
                        for b in range(tiles):
                            eng.wait_ge(aT_ready[b], i * 3 + 3)
                            turn_rows(b, i + 2)

            def experts():
                eng.wait_ge(tab_ready, 1)
                n = eng.value_load(eti[0:1, 0:1], min_val=2, max_val=MAXI)
                n2 = eng.value_load(eti[0:1, 1:2], min_val=1, max_val=MAX2)
                turn_rows(0, 1)
                turn_rows(1, 1)
                with eng.Fori(0, n2) as i:
                    item(i, 2)
                with eng.Fori(n2, n) as i:
                    item(i, 1)

            eng.wait_ge(const_ready, 1)
            eng.wait_ge(par_dma, 16 * 14)
            for i in range(2):
                last = tr(ps[0:P, 0, P * i:P * i + P], prow[:, i, :])
            last.then_inc(col_ps, 1)
            for m in range(3):
                mod(m, 7)
            eng.wait_ge(col_ready, 1)
            eng.wait_ge(xn_ready, T)
            for k in range(KD):
                if k == 7:
                    mod(3, 7)
                    eng.wait_ge(mod_out, 4)
                for t in range(T):
                    last = tr(ps[:, k, P * t:P * t + P], xn[:, t, P * k:P * k + P])
                last.then_inc(xT_ps, 1)
            for l in range(L):
                if l:
                    eng.wait_ge(mod_out, L * MODC)
                    prenorm(2 * l)
                projections(l)
                latents(l)
                attention(l)
                out_proj(l)
                prenorm(2 * l + 1)
                if l == 0:
                    dense()
                else:
                    route()
                    experts()

        @block.scalar
        def _(eng):
            A = nc.scalar.activation
            chain = [0]

            def link(ins):
                chain[0] += 1
                ins.then_inc(act_chain, 1)
                eng.wait_ge(act_chain, chain[0])

            def hi(s):
                r = WEIGHTS[s]
                n = size_of(UNITS[r])
                eng.wait_ge(raw_full[r % RAWS], 16 * (r // RAWS + 1))
                if s >= SPLS:
                    eng.wait_ge(w_used, s - SPLS + 1)
                A(spl[:, s % SPLS, 0, 0:n], raw[:, r % RAWS, 0:n], ACT.Copy).then_inc(hi_ready, 1)

            def root(out_, in_, scale, e):
                return A(out_, in_, ACT.Sqrt, scale=scale, bias=eps[:, e:e + 1])

            def post_stat(s, t, y, junk):
                link(A(junk, y, ACT.Square, accum_out=ss[:, t:t + 1]))
                root(rms[:, t:t + 1], ss[:, t:t + 1], 1.0 / D, 0).then_inc(pss, 1)

            def pre_stat(s, t):
                if s:
                    eng.wait_ge(x_upd, T * (s - 1) + t + 1)
                elif t == 0:
                    eng.wait_ge(x_dma, 16)
                link(A(xn_of(s)[:, t, :], x[:, t, :], ACT.Square, accum_out=ss[:, t:t + 1]))
                root(rms[:, t:t + 1], ss[:, t:t + 1], 1.0 / D, 0).then_inc(rms_ready, 1)

            def update(s, tile):
                for t in range(T):
                    tile(t)
                    if t:
                        pre_stat(s + 1, t - 1)
                pre_stat(s + 1, T - 1)

            def prenorm(s):
                c = modn if s >= 2 else modc
                b = 2 * (s % 2)
                for q in range(KD):
                    eng.wait_ge(xT_ps, KD * (s + 1) if s == 2 else KD * s + q + 1)
                    if q == 0:
                        eng.wait_ge(mod_out, MODC * (s // 2) + (4 if s % 2 == 0 else 10))
                    if q % 2:
                        if q > 1:
                            eng.wait_ge(hT_ready, KD * s + q - 1)
                        A(full[:, 1, :], ps[:, q, :], ACT.Identity, scale=c[:, b + 1, q:q + 1],
                          bias=c[:, b, q:q + 1])
                    A(hT[:, 0, q, :], ps[:, q, :], ACT.Identity, scale=c[:, b + 1, q:q + 1],
                      bias=c[:, b, q:q + 1]).then_inc(hT_hi, 1)

            def tile_hi(k, bank):
                A(yT[:, 0, k, :], ps[:, bank, :], ACT.Copy).then_inc(yT_hi, 1)

            def mixer(l):
                w0 = W_IN[l]
                for s in range(w0 + 2, w0 + 5):
                    hi(s)
                for j in (2, 3):
                    eng.wait_ge(*((zc_ps, 3 * l + j + 1) if j < 3 else (w_used, w0 + 2)))
                    A(zxy[:, j, :], ps[:, j, :], ACT.Gelu_apprx_tanh).then_inc(zy_ready, 1)
                hi(w0 + 5)
                eng.wait_ge(gate_ps, l + 1)
                for which in range(2):
                    for j in range(2):
                        last = A(lt[:, 1 + which, j, :], ps[:, 2 * which + j, :], ACT.Tanh, scale=0.5,
                                 bias=hb[:, which, l, j:j + 1])
                last.then_inc(gate_t, 1)
                eng.wait_ge(la_ready, l + 1)
                lf = lt[:].rearrange("p a j s -> p a (j s)")
                A(lf[:, 3], lf[:, 1], ACT.Exp)
                A(lf[:, 1], lf[:, 1], ACT.Tanh).then_inc(ea_ready, 1)
                for t in range(T):
                    eng.wait_ge(*((zb_ps, 3 * l + t + 1) if t < 3 else (w_used, w0 + 4)))
                    A(zuv[:, t, :], ps[:, 4 + t, :], ACT.Gelu_apprx_tanh).then_inc(zuv_ready, 1)
                eng.wait_ge(lq_ready, l + 1)
                q = zxy[:, 0:2, :]
                A(q, q, ACT.Sqrt, scale=-0.25).then_inc(lsq_ready, 1)
                eng.wait_ge(bn_done, l + 1)
                A(sd[:, 0, :], mv[:, :, 1], ACT.Sqrt, bias=eps[:, 1:2]).then_inc(sd_ready, 1)
                junk = lt[:, 1, 0, :]
                for t in range(T):
                    eng.wait_ge(zq_cp, T * l + t + 1)
                    A(junk[:, 0:QL], zq[:, t, 0:QL], ACT.Square, accum_out=st8[:, 0, t:t + 1])
                    link(A(junk[:, QL:QL + KVL], zq[:, t, QL:QL + KVL], ACT.Square, accum_out=st8[:, 0, 4 + t:5 + t]))
                    root(st8[:, 1, t:t + 1], st8[:, 0, t:t + 1], 1.0 / QL, 0)
                    root(st8[:, 1, 4 + t:5 + t], st8[:, 0, 4 + t:5 + t], 1.0 / KVL, 0).then_inc(qs_ready, 1)
                eng.wait_ge(ylru, l + 1)
                eng.wait_ge(qkT_ps, l + 1)
                A(qT[:, 2, :], ps[:, 0, :], ACT.Copy, scale=kvg[:, l:l + 1]).then_inc(att_in, 1)
                for b in range(2):
                    A(kb[64:128, b, :], ps[0:64, 3, :], ACT.Copy)
                eng.wait_ge(w_used, w0 + 6)
                for j in range(2):
                    eng.wait_ge(ysT_ps, 2 * l + j + 1)
                    tile_hi(4 + j, 1 + j)
                for j in range(2):
                    A(yT[:, 0, 6 + j, :], zxy[:, 2 + j, :], ACT.Copy).then_inc(yT_hi, 1)
                eng.wait_ge(v_ps, l + 1)
                A(vb[:, 0:2], ps[:, 4:6, :], ACT.Copy).then_inc(v_ready, 1)

                def keys(h):
                    n = HEADS * l + h
                    eng.wait_ge(k_ps, n + 1)
                    if h >= 2:
                        eng.wait_ge(s_ps, T * (n - 1))
                    A(kb[0:NOPE, h % 2, :], ps[0:NOPE, 1, :], ACT.Copy).then_inc(k_ev, 1)

                def weights(h, i):
                    n = HEADS * l + h
                    eng.wait_ge(nm_ready, n + 1)
                    if h:
                        eng.wait_ge(pt_ps, T * (n - 1) + i + 1)
                    A(pr[:, i, 0:P * (i + 1)], score(i), ACT.Exp, scale=SCALE, bias=am[:, 1, h % 4, i:i + 1],
                      accum_out=st8[:, 2, 4 * (h % 2) + i:4 * (h % 2) + i + 1]).then_inc(exp_ready, 1)

                def turned(h, i):
                    n = HEADS * l + h
                    if h:
                        eng.wait_ge(o_ps, n)
                    eng.wait_ge(pt_ps, T * n + i + 1)
                    w = P * (i + 1)
                    A(pT[:, 0:i + 1, P * i:w], ps[:, TURN_BANK[i % 2], 0:w].rearrange("p (j q) -> p j q", j=i + 1),
                      ACT.Copy).then_inc(pt_ev, 1)

                hi(W_O[l])
                keys(0)
                keys(1)
                hi(W_O[l] + 1)
                for i in range(T):
                    weights(0, i)
                eng.wait_ge(yT_ready, 8 * l + 4)
                for h in range(HEADS):
                    if h and h % 2 == 0:
                        eng.wait_ge(o_ps, HEADS * l + h)
                        tile_hi(h // 2 - 1, 2)
                    for i in range(T):
                        turned(h, i)
                    if h + 1 < HEADS:
                        for i in range(T):
                            weights(h + 1, i)
                    if h + 2 < HEADS:
                        keys(h + 2)
                    if h == 0:
                        hi(W_O[l] + 2)
                eng.wait_ge(o_ps, HEADS * (l + 1))
                tile_hi(3, 2)
                hi(W_O[l] + 3)
                if l == 0:
                    for i in range(2):
                        hi(W_FF + i)

                def tile(t):
                    eng.wait_ge(*((wo_ps, 6 * l + 4 + t) if t < 3 else (w_used, W_O[l] + 4)))
                    post_stat(2 * l, t, ps[:, 2 * t:2 * t + 2, :], xn[:, t, :].rearrange("p (n c) -> p n c", n=2))

                update(2 * l, tile)

            def dense():
                s, f = W_FF, 0

                def evict(w_end):
                    eng.wait_ge(*w_end)
                    if f >= 2:
                        eng.wait_ge(act_mul, f - 1)
                    A(sgf[:, f % 2, :], ps[:, 2 * (f % 2), :], ACT.Silu).then_inc(silu_ready, 1)
                    eng.wait_ge(act_mul, f + 1)
                    A(act[:, 0, f % 6, :], actf[:, f % 2, :], ACT.Copy).then_inc(act_hi, 1)

                for g, blocks in enumerate(GROUPS):
                    for c in range(blocks[0] // 2, blocks[-1] // 2 + 1):
                        hi(s + 2)
                        evict((gu_ps, c + 1))
                        f += 1
                        hi(s + 3)
                        evict((w_used, s + 2))
                        f += 1
                        s += 2
                    for i in range(4 if g < 3 else 1):
                        hi(s + 2)
                        s += 1

                def tile(t):
                    eng.wait_ge(dn_ev, 24 + t + 1)
                    post_stat(1, t, yf[:, t, :], xnf[:, t, :])

                update(1, tile)
                hi(s + 2)

            def experts():
                eng.wait_ge(gexp_in, 1)
                A(ge[:, 0, :], ge[:, 0, :], ACT.Exp).then_inc(gexp, 1)
                eng.wait_ge(tab_ready, 1)
                n = eng.value_load(eti[0:1, 0:1], min_val=2, max_val=MAXI)
                n2 = eng.value_load(eti[0:1, 1:2], min_val=1, max_val=MAX2)

                def part(i, j):
                    eng.wait_ge(mraw_full[j % MRAWS], i * (16 * EU // MRAWS) + 16 * (j // MRAWS + 1))
                    eng.wait_ge(w_used, i * EU + (SB + j - SPLS + 1))
                    w = unit_size(j % EU)
                    A(spl[:, (SB + j) % SPLS, 0, 0:w], mraw[:, j % MRAWS, 0:w], ACT.Copy).then_inc(hi_ready, 1)

                def rows(b, count):
                    eng.wait_ge(xg_full[b], count)
                    A(xgT[b][:, 0], xfull[:], ACT.Copy).then_inc(xg_hi[b], 1)

                def item(i, tiles):
                    def silu(c):
                        eng.wait_ge(w_used, i * EU + (SB + 4 * c + 2))
                        w = EW[c][1]
                        for b in range(tiles):
                            if c:
                                eng.wait_ge(e_mul[b], i * 3 + c)
                            A(sge[b][:, 0:w], ps[:, 2 * b, 0:w], ACT.Silu).then_inc(e_silu[b], 1)

                    def turned(c):
                        w = EW[c][1]
                        for b in range(tiles):
                            eng.wait_ge(aT_ps[b], i * 3 + (c + 1))
                            A(aT[b][:, 0, 4 * c:4 * c + w // P, :].rearrange("p f q -> p (f q)"),
                              ps[:, (4, 5, 0)[c] + 2 * b, 0:w], ACT.Copy).then_inc(aT_hi[b], 1)

                    for j in range(2, EU + 2):
                        part(i, j)
                        if j in (4, 8, 12):
                            silu(j // 4 - 1)
                        if j in (8, 12):
                            turned(j // 4 - 2)
                        if j == 15:
                            turned(2)
                        if j == 16:
                            for b in range(tiles):
                                rows(b, i + 2)
                    eng.wait_ge(w_used, i * EU + (SB + EU))
                    eng.wait_ge(ye_free, i + 1)
                    for b in range(tiles):
                        A(ye[b][:].rearrange("p (h c) -> p h c", h=2), ps[:, 4 + 2 * b:6 + 2 * b, :],
                          ACT.Copy).then_inc(ye_ev[b], 1)

                part(0, 0)
                part(0, 1)
                rows(0, 1)
                rows(1, 1)
                with eng.Fori(0, n2) as i:
                    item(i, 2)
                with eng.Fori(n2, n) as i:
                    item(i, 1)
                for t in range(T + 1):
                    if t < T:
                        eng.wait_ge(yg_dma[t], 32)
                        A(ym[:, t, :], yg[:, t, 0, :], ACT.Copy, scale=gt[:, 0, t:t + 1]).then_inc(share_ready, 1)
                    if t:
                        eng.wait_ge(ym_ready, t)
                        post_stat(3, t - 1, ym[:, t - 1, :], yg[:, t - 1, 0, :])

            eng.dma_start(cond[:, 0, :], a["c"][0].rearrange("(p k) -> p k", k=KD)).then_inc(c_dma, 16)
            eng.wait_ge(c_dma, 16)
            A(cond[:, 1, :], cond[:, 0, :], ACT.Silu).then_inc(cond_ready, 1)
            eng.wait_ge(const_ready, 1)
            for t in range(T):
                pre_stat(0, t)
            eng.wait_ge(col_ps, 1)
            A(colp[:], ps[:, 0, 0:2 * P].rearrange("p (a b) -> p a b", a=2)[:, :, 0:96], ACT.Copy).then_inc(col_ready, 1)
            eng.wait_ge(xn_scale, 1)
            for t in range(T):
                A(xn[:, t, :], x[:, t, :], ACT.Copy, scale=rinv[:, t:t + 1]).then_inc(xn_ready, 1)
            eng.wait_ge(col_ready, 1)
            link(A(sp[:, 0], lcol[:, 3], ACT.Abs))
            A(sp[:, 0], sp[:, 0], ACT.Exp, scale=-1.0).then_inc(sp_a, 1)
            eng.wait_ge(sp_b, 1)
            A(sp[:, 2], sp[:, 1], ACT.Ln).then_inc(sp_c, 1)
            for i in range(2):
                hi(i)
            for l in range(L):
                prenorm(2 * l)
                mixer(l)
                if l == 0:
                    prenorm(1)
                    dense()
                else:
                    experts()

        @block.vector
        def _(eng):
            V = nc.vector
            chain = [0]

            def link(ins):
                chain[0] += 1
                ins.then_inc(dve_chain, 1)
                eng.wait_ge(dve_chain, chain[0])

            def after(ins, s, v):
                ins.then_inc(s, 1)
                eng.wait_ge(s, v)

            def lo(s):
                r = WEIGHTS[s]
                n = size_of(UNITS[r])
                eng.wait_ge(hi_ready, s + 1)
                V.tensor_tensor(spl[:, s % SPLS, 1, 0:n], raw[:, r % RAWS, 0:n],
                                spl[:, s % SPLS, 0, 0:n].bitcast(F32), ALU.subtract).then_inc(lo_ready, 1)

            def mod_half(m, kh):
                v = acc[:, m % 2, :]
                if m >= 2 and kh == 0:
                    eng.wait_ge(mod_ps, m - 1)
                r = MODS[2 * m + kh]
                eng.wait_ge(raw_full[r % RAWS], 16 * (r // RAWS + 1))
                for kk in range(4):
                    w = raw[:, r % RAWS, 512 * kk:512 * kk + 512]
                    c = cond[:, 1, 4 * kh + kk:4 * kh + kk + 1]
                    if kh + kk == 0:
                        ins = V.tensor_scalar(v, w, c, None, ALU.mult)
                    else:
                        ins = V.scalar_tensor_tensor(out=v, in0=w, scalar=c, in1=v, op0=ALU.mult, op1=ALU.add)
                    if kk < 3:
                        link(ins)
                    else:
                        after(ins, *mod_done(m, kh))

            def mod_sum(m):
                for kh in range(2):
                    mod_half(m, kh)

            def mod_evict(m, bank):
                l, c = divmod(m, MODC)
                kind, half = divmod(c, 2)
                eng.wait_ge(mod_ps, m + 1)
                if kind in (2, 5):
                    slot = 0 if kind == 2 else 1 + l
                    eng.wait_ge(post_dma, 64 if l and kind == 2 else 48)
                    g = gp[:, slot, 512 * half:512 * half + 512]
                    V.tensor_tensor(g, ps[:, bank, :], g, ALU.mult).then_inc(mod_out, 1)
                else:
                    k = slice(4 * half, 4 * half + 4)
                    dst = (modn if l else modc)[:, {0: 0, 1: 1, 3: 2, 4: 3}[kind], k]
                    ins = V.tensor_tensor(dst, ps[:, bank, 0:4], bmod[:, l, 4 * c:4 * c + 4], ALU.add)
                    if kind in (1, 4):
                        link(ins)
                        ins = V.scalar_tensor_tensor(out=dst, in0=dst, scalar=1.0, in1=gpre[:, kind // 4, l, k],
                                                     op0=ALU.add, op1=ALU.mult)
                    after(ins, mod_out, m + 1)

            def pre_tile(s, t):
                eng.wait_ge(rms_ready, T * s + t + 1)
                link(V.reciprocal(rinv[:, t:t + 1], rms[:, t:t + 1]))
                V.tensor_scalar(xn_of(s)[:, t, :], x[:, t, :], rinv[:, t:t + 1], None, ALU.mult).then_inc(
                    xn_ready, 1)

            def post_tile(s, t, y, slot, tmp):
                eng.wait_ge(pss, T * s + t + 1)
                link(V.reciprocal(rinv[:, t:t + 1], rms[:, t:t + 1]))
                link(V.scalar_tensor_tensor(out=tmp[:, t % 2, :].rearrange("p (n c) -> p n c", n=2), in0=y,
                                            scalar=rinv[:, t:t + 1],
                                            in1=gp[:, slot, :].rearrange("p (n c) -> p n c", n=2),
                                            op0=ALU.mult, op1=ALU.mult))
                V.tensor_tensor(x[:, t, :], x[:, t, :], tmp[:, t % 2, :], ALU.add).then_inc(x_upd, 1)

            def prenorm(s):
                c = modn if s >= 2 else modc
                b = 2 * (s % 2)
                for q in range(KD):
                    eng.wait_ge(*((xT_ps, KD * s + q + 1) if s == 3 else (hT_hi, KD * s + q + 1)))
                    o = hTf[:, q, :] if s == 3 else full[:, q % 2, :]
                    if s < 3 and q and q % 2 == 0:
                        eng.wait_ge(hT_ready, KD * s + q - 1)
                    if s == 3 or q % 2 == 0:
                        ins = V.tensor_scalar(o, ps[:, q, :], c[:, b + 1, q:q + 1], c[:, b, q:q + 1],
                                              ALU.mult, ALU.add)
                    if s == 3:
                        ins.then_inc(hT_ready, 1)
                        continue
                    if q % 2 == 0:
                        link(ins)
                    V.tensor_tensor(hT[:, 1, q, :], o, hT[:, 0, q, :].bitcast(F32), ALU.subtract).then_inc(hT_ready, 1)

            def tile_lo(l, i, k, src):
                eng.wait_ge(yT_hi, 8 * l + i + 1)
                V.tensor_tensor(yT[:, 1, k, :], src, yT[:, 0, k, :].bitcast(F32), ALU.subtract).then_inc(yT_ready, 1)

            def mixer(l):
                w0 = W_IN[l]
                if l == 0:
                    mod_sum(4)
                lo(w0 + 2)
                lo(w0 + 3)
                for j in range(2):
                    eng.wait_ge(zc_ps, 3 * l + j + 1)
                    V.tensor_copy(zxy[:, j, :], ps[:, j, :]).then_inc(zx_cp, 1)
                eng.wait_ge(zx_cp, 2 * (l + 1))
                for j in range(2):
                    ins = V.tensor_scalar(lt[:, 0, j, :], zxy[:, j, :], cw[:, l, 3, j:j + 1], lcol[:, 0, l, j:j + 1],
                                          ALU.mult, ALU.add)
                link(ins)
                for tap in range(3):
                    sh = 3 - tap
                    for j in range(2):
                        ins = V.scalar_tensor_tensor(out=lt[:, 0, j, sh:], in0=zxy[:, j, 0:S - sh],
                                                     scalar=cw[:, l, tap, j:j + 1], in1=lt[:, 0, j, sh:],
                                                     op0=ALU.mult, op1=ALU.add)
                    if tap == 2:
                        after(ins, xc_ready, l + 1)
                    else:
                        link(ins)
                if l == 0:
                    mod_evict(4, 7)
                eng.wait_ge(sw_ps, l + 1)
                V.tensor_copy(sguw[:], ps[:, 6, :].rearrange("p (g t) -> p g t", g=4)).then_inc(sw_cp, 1)
                lo(w0 + 4)
                eng.wait_ge(gate_t, l + 1)
                for j in range(2):
                    ins = V.tensor_scalar(lt[:, 1, j, :], lt[:, 1, j, :], 1.0, nsp[:, l, j:j + 1], ALU.add, ALU.mult)
                after(ins, la_ready, l + 1)
                link(V.scalar_tensor_tensor(out=lt[:, 2], in0=lt[:, 2], scalar=1.0, in1=lt[:, 0],
                                            op0=ALU.add, op1=ALU.mult))
                lo(w0 + 5)
                eng.wait_ge(ea_ready, l + 1)
                q = zxy[:, 0:2, :]
                link(V.tensor_tensor(q, lt[:, 3], lt[:, 3], ALU.mult))
                after(V.scalar_tensor_tensor(out=q, in0=q, scalar=1.0, in1=lt[:, 1], op0=ALU.add, op1=ALU.mult),
                      lq_ready, l + 1)
                for t in range(T):
                    eng.wait_ge(zuv_ready, T * l + t + 1)
                    link(V.bn_stats(bn[:, t, :], zuv[:, t, SGU:2 * SGU]))
                    ins = V.bn_aggr(mv[:, t, :], bn[:, t, :])
                after(ins, bn_done, l + 1)
                eng.wait_ge(lsq_ready, l + 1)
                link(V.tensor_tensor(lt[:, 2], lt[:, 2], q, ALU.mult))
                for j in range(2):
                    ins = V.tensor_tensor_scan(lt[:, 0, j, :], lt[:, 3, j, :], lt[:, 2, j, :], 0.0, ALU.mult, ALU.add)
                eng.wait_ge(sd_ready, l + 1)
                link(V.reciprocal(sd[:, 1, :], sd[:, 0, :]))
                v = zuv[:, :, SGU:2 * SGU]
                for t in range(T):
                    ins = V.tensor_scalar(v[:, t, :], v[:, t, :], mv[:, t, 0:1], sd[:, 1, t:t + 1],
                                          ALU.subtract, ALU.mult)
                link(ins)
                for i, op in enumerate((ALU.mult, ALU.add)):
                    ins = V.tensor_tensor(v, v, lnrow[:, i:i + 1, :].to_broadcast([P, T, SGU]), op)
                    if i == 0:
                        link(ins)
                    else:
                        after(ins, vn_ready, l + 1)
                V.tensor_tensor(zxy[:, 2:4, :], lt[:, 0], zxy[:, 2:4, :], ALU.mult).then_inc(ylru, 1)
                eng.wait_ge(mix_ps, l + 1)
                for g in range(4):
                    u = zuv[:, :, 64 * g:64 * g + 64]
                    o = ps[:, 5 + g // 2, 256 * (g % 2):256 * (g % 2) + 256].rearrange("p (t c) -> p t c", t=T)
                    ins = V.scalar_tensor_tensor(out=u, in0=o, scalar=sgub[:, l, g:g + 1], in1=u,
                                                 op0=ALU.add, op1=ALU.mult)
                ins.then_inc(ysg_ready, 1)


                def norm(t):
                    eng.wait_ge(qs_ready, T * l + t + 1)
                    link(V.reciprocal(st8[:, 0, t:t + 5:4], st8[:, 1, t:t + 5:4]))
                    V.tensor_scalar(zq[:, t, 0:QL], zq[:, t, 0:QL], st8[:, 0, t:t + 1], None, ALU.mult)
                    V.tensor_scalar(zq[:, t, QL:QL + KVL], zq[:, t, QL:QL + KVL], st8[:, 0, 4 + t:5 + t], None,
                                    ALU.mult).then_inc(zqn_ready, 1)

                for t in range(T):
                    eng.wait_ge(*((za_ps, 3 * l + t + 1) if t < 3 else (w_used, w0 + 6)))
                    V.tensor_copy(zq[:, t, :], ps[:, t, 0:QKR]).then_inc(zq_cp, 1)
                    if t:
                        norm(t - 1)
                eng.wait_ge(zq_cp, T * (l + 1))
                x1, x2 = zq[:, :, QL + KVL:QL + KVL + HALF], zq[:, :, QL + KVL + HALF:QKR]
                cos, sin = trig[:, 0], trig[:, 1]
                ra, rb = krd[:, :, 0, 0:HALF], krd[:, :, 0, HALF:ROPE]
                rc, rd = krd[:, :, 1, 0:HALF], krd[:, :, 1, HALF:ROPE]
                V.tensor_tensor(ra, x1, cos, ALU.mult)
                V.tensor_tensor(rc, x2, sin, ALU.mult)
                V.tensor_tensor(rb, x2, cos, ALU.mult)
                link(V.tensor_tensor(rd, x1, sin, ALU.mult))
                V.tensor_tensor(ra, ra, rc, ALU.subtract)
                link(V.tensor_tensor(rb, rb, rd, ALU.add))
                V.tensor_copy(krd[:, :, 1, :], krd[:, :, 0, :]).then_inc(kr_ready, 1)
                norm(3)
                eng.wait_ge(qkT_ps, l + 1)
                for j in range(2):
                    ins = V.tensor_scalar(qT[:, j, :], ps[:, 5 + j, :], qg[:, l, j:j + 1], None, ALU.mult)
                ins.then_inc(q_in, 1)
                for j in range(2):
                    tile_lo(l, j, 4 + j, ps[:, 1 + j, :])
                for j in range(2):
                    tile_lo(l, 2 + j, 6 + j, zxy[:, 2 + j, :])
                eng.wait_ge(v_ps, l + 1)
                V.tensor_copy(vb[:, 2:4], ps[:, 6:8, :]).then_inc(v2_ready, 1)

                def queries(h):
                    n = HEADS * l + h
                    eng.wait_ge(q_ps, n + 1)
                    if h >= 2:
                        eng.wait_ge(s_ps, T * (n - 1))
                    V.tensor_tensor(qb[:, h % 2, :], ps[:, 0, :], cs[:], ALU.mult).then_inc(q_ev, 1)

                def maxima(h):
                    n = HEADS * l + h
                    for i, count in zip(SCORE_ORDER, (1, 3, 3, 4)):
                        eng.wait_ge(s_ps, T * n + count)
                        ins = V.memset(score(i)[0:64, P * i + 64:P * i + P], NEG)
                    link(ins)
                    for i in range(T):
                        ins = V.reduce_max(am[:, 0, h % 4, i:i + 1], score(i), AX.X)
                    link(ins)
                    V.tensor_scalar(am[:, 1, h % 4, :], am[:, 0, h % 4, :], -SCALE, None, ALU.mult).then_inc(
                        nm_ready, 1)

                def normalise(h):
                    n = HEADS * l + h
                    eng.wait_ge(exp_ready, T * (n + 1))
                    link(V.reciprocal(am[:, 0, h % 4, :], st8[:, 2, 4 * (h % 2):4 * (h % 2) + 4]))
                    for i in range(T):
                        p = pr[:, i, 0:P * (i + 1)]
                        V.tensor_scalar(p, p, am[:, 0, h % 4, i:i + 1], None, ALU.mult).then_inc(pn_ready, 1)

                queries(0)
                lo(W_O[l])
                queries(1)
                maxima(0)
                lo(W_O[l] + 1)
                normalise(0)
                for h in range(HEADS):
                    if l == 0 and h - 1 in MOD_AFTER:
                        mod_evict(MOD_AFTER[h - 1], 0)
                    if h + 1 < HEADS:
                        maxima(h + 1)
                    if h and h % 2 == 0:
                        tile_lo(l, 3 + h // 2, h // 2 - 1, ps[:, 2, :])
                    if h + 2 < HEADS:
                        queries(h + 2)
                    if l == 0 and h < 6:
                        mod_half(6 + h // 2, h % 2)
                    if h + 1 < HEADS:
                        normalise(h + 1)
                    if h == 1:
                        lo(W_O[l] + 2)
                tile_lo(l, 7, 3, ps[:, 2, :])
                lo(W_O[l] + 3)
                if l == 0:
                    mod_evict(9, 1)
                if l == 0:
                    for i in range(2):
                        lo(W_FF + i)

            def dense():
                s, f, m, downs = W_FF, 0, 10, 0

                def evict(w_end):
                    eng.wait_ge(*w_end)
                    eng.wait_ge(silu_ready, f + 1)
                    after(V.tensor_tensor(actf[:, f % 2, :], sgf[:, f % 2, :], ps[:, 2 * (f % 2) + 1, :], ALU.mult),
                          act_mul, f + 1)
                    eng.wait_ge(act_hi, f + 1)
                    V.tensor_tensor(act[:, 1, f % 6, :], actf[:, f % 2, :], act[:, 0, f % 6, :].bitcast(F32),
                                    ALU.subtract).then_inc(act_ready, 1)

                def down_evict(g, n, w_last):
                    for t in range(T):
                        eng.wait_ge(*((dn_ps, 6 * g + 3 * n + t + 1) if t < 3 else (w_used, w_last)))
                        o = yf[:, t, 512 * n:512 * n + 512]
                        if g:
                            V.tensor_tensor(o, ps[:, 4 + t, :], o, ALU.add).then_inc(dn_ev, 1)
                        else:
                            V.tensor_copy(o, ps[:, 4 + t, :]).then_inc(dn_ev, 1)

                for g, blocks in enumerate(GROUPS):
                    for c in range(blocks[0] // 2, blocks[-1] // 2 + 1):
                        lo(s + 2)
                        evict((gu_ps, c + 1))
                        f += 1
                        if 2 * c > blocks[0]:
                            mod_evict(m - 1, 4)
                        mod_sum(m)
                        m += 1
                        lo(s + 3)
                        evict((w_used, s + 2))
                        f += 1
                        s += 2
                    if g == 3:
                        break
                    for i in range(4):
                        lo(s + 2)
                        s += 1
                        if i == 0:
                            mod_evict(m - 1, 0)
                            mod_sum(m)
                            m += 1
                        if i == 1:
                            down_evict(g, 0, s)
                        if i == 2:
                            mod_evict(m - 1, 0)
                    down_evict(g, 1, s)
                lo(s + 2)
                for t in range(T + 2):
                    if t < T:
                        eng.wait_ge(*((dn_ps, 18 + t + 1) if t < 3 else (w_used, s + 2)))
                        o = yf[:, t, :].rearrange("p (n c) -> p n c", n=2)
                        V.tensor_tensor(o, ps[:, 2 * t:2 * t + 2, :], o, ALU.add).then_inc(dn_ev, 1)
                    if t == T - 1:
                        mod_evict(m - 1, 0)
                    if 1 <= t <= T:
                        eng.wait_ge(dn_ev, 24 + t)
                        post_tile(1, t - 1, yf[:, t - 1, :].rearrange("p (n c) -> p n c", n=2), 1, tmpf)
                    if t >= 2:
                        pre_tile(2, t - 2)
                lo(s + 3)

            def route():
                V.memset(msk[:, T, :], 0.0)
                eng.wait_ge(lgt_ps, 1)
                V.tensor_copy(lgt[0:E, :], ps[0:E, 0, :]).then_inc(lgt_ready, 1)
                eng.wait_ge(lg_ps, 1)
                link(V.tensor_copy(lg[:], ps[:, 1, 0:T * E].rearrange("p (t e) -> p t e", t=T)))
                for t in range(T):
                    ins = V.max(mx8[:, t, :], lg[:, t, :])
                link(ins)
                for t in range(T):
                    ins = V.max_index(ix8[:, t, :], mx8[:, t, :], lg[:, t, :])
                link(ins)
                link(V.tensor_copy(ixf[:], ix8[:]))
                ex = iot[:, 0:E].unsqueeze(1).to_broadcast([P, T, E])
                for k in range(2):
                    ins = V.tensor_tensor(oh[:, k], ex, ixf[:, :, k:k + 1].to_broadcast([P, T, E]), ALU.is_equal)
                link(ins)
                V.tensor_tensor(msk[:, 0:T], oh[:, 0], oh[:, 1], ALU.add).then_inc(msk_ready, 1)
                V.tensor_tensor(ge[:, 0, :], mx8[:, :, 1], mx8[:, :, 0], ALU.subtract).then_inc(gexp_in, 1)
                eng.wait_ge(gexp, 1)
                link(V.tensor_scalar(ge[:, 1, :], ge[:, 0, :], 1.0, None, ALU.add))
                link(V.reciprocal(gt[:, 0, :], ge[:, 1, :]))
                link(V.tensor_tensor(gt[:, 1, :], gt[:, 0, :], ge[:, 0, :], ALU.mult))
                eng.wait_ge(pos_ps, 1)
                rank = ps[:, 2, 0:T * E].rearrange("p (t e) -> p t e", t=T)
                link(V.tensor_copy(cnt[:], ps[:, 2, T * E:(T + 1) * E]))
                for r in range(T):
                    ins = V.tensor_scalar(above[:, r, :], cnt[:], float(P * r), None, ALU.is_gt)
                link(ins)
                V.tensor_tensor(pairs[:, 1], above[:, 0], above[:, 2], ALU.add)
                link(V.tensor_tensor(pairs[:, 0], above[:, 1], above[:, 3], ALU.add))
                link(V.tensor_tensor(pairs[:, 1], pairs[:, 1], pairs[:, 0], ALU.subtract))
                for r in range(2):
                    ins = V.tensor_tensor_scan(ends[:, r], ones[:, 0:E], pairs[:, r], 0.0, ALU.mult, ALU.add)
                link(ins)
                V.tensor_tensor(starts[:], ends[:], pairs[:], ALU.subtract)
                V.tensor_scalar(limit[:], pairs[:, 0], 2.0 * P, None, ALU.mult)
                link(V.tensor_scalar(etf[:, 1:2], ends[:, 0, E - 1:E], 1.0, None, ALU.max))
                V.scalar_tensor_tensor(out=etf[:, 0:1], in0=ends[:, 1, E - 1:E], scalar=1.0, in1=etf[:, 1:2],
                                       op0=ALU.max, op1=ALU.add)
                V.tensor_scalar(first[:], starts[:, 0], 2.0 * P, None, ALU.mult)
                link(V.tensor_scalar(jump[:], ends[:, 0], etf[:, 1:2], -2.0 * P, ALU.subtract, ALU.mult))
                V.scalar_tensor_tensor(out=jump[:], in0=starts[:, 1], scalar=float(P), in1=jump[:],
                                       op0=ALU.mult, op1=ALU.add)
                link(V.tensor_tensor(beyond[:], rank, limit[:].unsqueeze(1).to_broadcast([P, T, E]), ALU.is_ge))
                V.tensor_tensor(gpos[:], rank, first[:].unsqueeze(1).to_broadcast([P, T, E]), ALU.add)
                link(V.tensor_tensor(beyond[:], beyond[:], jump[:].unsqueeze(1).to_broadcast([P, T, E]), ALU.mult))
                link(V.tensor_tensor(gpos[:], gpos[:], beyond[:], ALU.add))
                for k in range(2):
                    ins = V.tensor_tensor(prod[:, k], oh[:, k], gpos[:], ALU.mult)
                link(ins)
                for k in range(2):
                    ins = V.reduce_sum(slf[:, k, :], prod[:, k], AX.X)
                link(ins)
                V.tensor_copy(sli[:], slf[:]).then_inc(slots_ready, 1)
                link(V.tensor_scalar(ends[:, 1], ends[:, 1], etf[:, 1:2], None, ALU.add))
                for r in range(2):
                    ins = V.tensor_tensor(cmp_[:, r], ends[:, r:r + 1, :].to_broadcast([P, MAXT, E]),
                                          iot[:].unsqueeze(2).to_broadcast([P, MAXT, E]), ALU.is_le)
                link(ins)
                for r in range(2):
                    ins = V.reduce_sum(owner[:, r], cmp_[:, r], AX.X)
                link(ins)
                V.tensor_scalar(etf[:, 2:], iot[:], etf[:, 1:2], None, ALU.is_lt)
                link(V.tensor_tensor(owner[:, 0], owner[:, 0], owner[:, 1], ALU.subtract))
                link(V.tensor_tensor(etf[:, 2:], etf[:, 2:], owner[:, 0], ALU.mult))
                link(V.tensor_tensor(etf[:, 2:], etf[:, 2:], owner[:, 1], ALU.add))
                link(V.tensor_scalar(etf[:, 2:], etf[:, 2:], float(E - 1), None, ALU.min))
                V.tensor_copy(eti[:], etf[:]).then_inc(tab_ready, 1)

            def experts():
                eng.wait_ge(tab_ready, 1)
                n = eng.value_load(eti[0:1, 0:1], min_val=2, max_val=MAXI)
                n2 = eng.value_load(eti[0:1, 1:2], min_val=1, max_val=MAX2)

                def part(i, j):
                    eng.wait_ge(hi_ready, i * EU + (SB + j + 1))
                    w = unit_size(j % EU)
                    o = spl[:, (SB + j) % SPLS]
                    V.tensor_tensor(o[:, 1, 0:w], mraw[:, j % MRAWS, 0:w], o[:, 0, 0:w].bitcast(F32),
                                    ALU.subtract).then_inc(lo_ready, 1)

                def rows(b, count):
                    eng.wait_ge(xg_ps[b], count)
                    if b:
                        eng.wait_ge(xg_ready[0], count)
                    for k in range(KD):
                        ins = V.tensor_scalar(xfull[:, k, :], ps[:, 2 * b + k // 4, P * (k % 4):P * (k % 4) + P],
                                              modn[:, 3, k:k + 1], modn[:, 2, k:k + 1], ALU.mult, ALU.add)
                    ins.then_inc(xg_full[b], 1)
                    eng.wait_ge(xg_hi[b], count)
                    V.tensor_tensor(xgT[b][:, 1], xfull[:], xgT[b][:, 0].bitcast(F32), ALU.subtract).then_inc(
                        xg_ready[b], 1)

                def item(i, tiles):
                    def multiply(c):
                        eng.wait_ge(w_used, i * EU + (SB + 4 * c + 4))
                        w = EW[c][1]
                        for b in range(tiles):
                            eng.wait_ge(e_silu[b], i * 3 + (c + 1))
                            if c:
                                eng.wait_ge(aT_ps[b], i * 3 + c)
                            V.tensor_tensor(acte[b][:, 0:w], sge[b][:, 0:w], ps[:, 2 * b + 1, 0:w],
                                            ALU.mult).then_inc(e_mul[b], 1)

                    def turned(c):
                        w = EW[c][1]
                        f = slice(4 * c, 4 * c + w // P)
                        for b in range(tiles):
                            eng.wait_ge(aT_hi[b], i * 3 + (c + 1))
                            V.tensor_tensor(aT[b][:, 1, f, :],
                                            ps[:, (4, 5, 0)[c] + 2 * b, 0:w].rearrange("p (f q) -> p f q", q=P),
                                            aT[b][:, 0, f, :].bitcast(F32), ALU.subtract).then_inc(aT_ready[b], 1)

                    for j in range(2, EU + 2):
                        if j in (6, 10, 14):
                            multiply((j - 6) // 4)
                        part(i, j)
                        if j in (8, 12):
                            turned(j // 4 - 2)
                        if j == 15:
                            turned(2)
                        if j == 16:
                            for b in range(tiles):
                                rows(b, i + 2)

                part(0, 0)
                rows(0, 1)
                part(0, 1)
                rows(1, 1)
                with eng.Fori(0, n2) as i:
                    item(i, 2)
                with eng.Fori(n2, n) as i:
                    item(i, 1)
                for t in range(T + 1):
                    if t < T:
                        eng.wait_ge(yg_dma[t], 32)
                        eng.wait_ge(share_ready, t + 1)
                        V.scalar_tensor_tensor(out=ym[:, t, :], in0=yg[:, t, 1, :], scalar=gt[:, 1, t:t + 1],
                                               in1=ym[:, t, :], op0=ALU.mult, op1=ALU.add).then_inc(ym_ready, 1)
                    if t:
                        u = t - 1
                        eng.wait_ge(pss, T * 3 + u + 1)
                        link(V.reciprocal(rinv[:, u:u + 1], rms[:, u:u + 1]))
                        V.scalar_tensor_tensor(out=ym[:, u, :], in0=ym[:, u, :], scalar=rinv[:, u:u + 1],
                                               in1=gp[:, 2, :], op0=ALU.mult, op1=ALU.mult).then_inc(scaled, 1)
                eng.wait_ge(scaled, T)
                V.tensor_tensor(x[:, T - 1, :], x[:, T - 1, :], ym[:, T - 1, :], ALU.add).then_inc(x_last, 1)

            def softplus():
                eng.wait_ge(sp_c, 1)
                link(V.tensor_scalar(sp[:, 1], sp[:, 1], 1.0, None, ALU.subtract))
                link(V.tensor_scalar(sp[:, 3], sp[:, 1], 0.0, None, ALU.is_equal))
                link(V.tensor_tensor(sp[:, 1], sp[:, 1], sp[:, 3], ALU.add))
                link(V.reciprocal(sp[:, 1], sp[:, 1]))
                link(V.tensor_tensor(sp[:, 2], sp[:, 2], sp[:, 1], ALU.mult))
                link(V.tensor_tensor(sp[:, 2], sp[:, 2], sp[:, 3], ALU.add))
                link(V.tensor_tensor(sp[:, 2], sp[:, 2], sp[:, 0], ALU.mult))
                link(V.tensor_scalar(sp[:, 3], lcol[:, 3], -1.0, 0.0, ALU.mult, ALU.max))
                link(V.tensor_tensor(sp[:, 2], sp[:, 2], sp[:, 3], ALU.add))
                link(V.tensor_scalar(nsp[:], sp[:, 2], -4.0, None, ALU.mult))
                link(V.tensor_scalar(hb[:], lcol[:, 1:3], 0.5, None, ALU.mult))

            eng.wait_ge(cond_ready, 1)
            mod_sum(0)
            eng.wait_ge(rms_ready, T)
            V.reciprocal(rinv[:], rms[:]).then_inc(xn_scale, 1)
            mod_sum(1)
            eng.wait_ge(col_ready, 1)
            mod_evict(0, 7)
            mod_sum(2)
            mod_evict(1, 7)
            eng.wait_ge(sp_a, 1)
            after(V.tensor_scalar(sp[:, 1], sp[:, 0], 1.0, None, ALU.add), sp_b, 1)
            mod_sum(3)
            mod_evict(2, 7)
            lo(0)
            mod_evict(3, 7)
            for l in range(L):
                prenorm(2 * l)
                if l == 0:
                    lo(1)
                    softplus()
                mixer(l)
                for t in range(T):
                    post_tile(2 * l, t, ps[:, 2 * t:2 * t + 2, :], 0, tmpm)
                    if t:
                        pre_tile(2 * l + 1, t - 1)
                pre_tile(2 * l + 1, T - 1)
                prenorm(2 * l + 1)
                if l == 0:
                    dense()
                else:
                    route()
                    experts()


def tables():
    pos = np.arange(S, dtype=np.float32)
    inv = np.float32(10000.0) ** (-np.arange(0, ROPE, 2, dtype=np.float32) / np.float32(ROPE))
    ang = (pos[:, None] * inv[None, :]).astype(np.float32)
    cos, sin = np.cos(ang), np.sin(ang)
    cs = np.concatenate([np.ones((NOPE, S), np.float32), cos.T, cos.T, -sin.T, sin.T]).astype(np.float32)
    trig = np.stack([cos, sin]).reshape(2, T, P, HALF).transpose(2, 0, 1, 3)
    return {"cs_table": np.ascontiguousarray(cs), "trig_table": np.ascontiguousarray(trig.astype(np.float32))}


def kernel(**inputs):
    from concourse import bacc
    from concourse.bass_utils import run_bass_kernel_spmd

    nc = bacc.Bacc("TRN2", target_bir_lowering=False, num_devices=1)
    arrays = {name: np.ascontiguousarray(v) for name, v in inputs.items()} | tables()
    args = {name: nc.dram_tensor(f"in_{name}", v.shape, mybir.dt.from_np(v.dtype), kind="ExternalInput").ap()
            for name, v in arrays.items()}
    out = nc.dram_tensor("out", (1, S, D), F32, kind="ExternalOutput").ap()
    build(nc, args, out)
    r = run_bass_kernel_spmd(nc, [{f"in_{name}": v for name, v in arrays.items()}], core_ids=[0])
    return r.results[0]["out"]
```
